# Optimizing a Trainium2 kernel written in Bass

```python
import jax
import jax.numpy as jnp
from jax import lax
import numpy as np
import math

D_MODEL = 1024
BATCH = 1
SEQ = 256
DEPTH = 2

N_META = 16
EPS = 1e-6
GATE_CLAMP = 1.0 - 1e-6
CONV_DIM = D_MODEL // 2
CONV_K = 31
MLA_HEADS = D_MODEL // 128
Q_RANK = D_MODEL // 4
KV_RANK = D_MODEL // 8
NOPE_DIM = 64
ROPE_DIM = 32
V_DIM = 64
QK_DIM = NOPE_DIM + ROPE_DIM
ROPE_BASE = 10000.0
Q_BLOCK = 128
HGRN_HEADS = D_MODEL // 256
HGRN_DK = 128
HGRN_DV = (D_MODEL // 2) // HGRN_HEADS
HGRN_CHUNK = 64
D_FF = 4 * D_MODEL
N_BRANCH = 3

SPLIT_SIZES = (
    2 * CONV_DIM,
    Q_RANK,
    KV_RANK,
    ROPE_DIM,
    HGRN_HEADS * HGRN_DK,
    HGRN_HEADS * HGRN_DK,
    HGRN_HEADS * HGRN_DV,
    HGRN_HEADS * HGRN_DV,
    N_BRANCH * D_MODEL,
)
SPLIT_POINTS = tuple(int(s) for s in np.cumsum(SPLIT_SIZES)[:-1])
N_IN = int(sum(SPLIT_SIZES))


def rms_norm(x, g):
    xf = x.astype(jnp.float32)
    y = xf * lax.rsqrt(jnp.mean(xf * xf, axis=-1, keepdims=True) + EPS)
    return (y * g.astype(jnp.float32)).astype(x.dtype)

def layer_norm(x, g, b):
    xf = x.astype(jnp.float32)
    mu = jnp.mean(xf, axis=-1, keepdims=True)
    xc = xf - mu
    y = xc * lax.rsqrt(jnp.mean(xc * xc, axis=-1, keepdims=True) + EPS)
    return (y * g.astype(jnp.float32) + b.astype(jnp.float32)).astype(x.dtype)

def apply_rope(x, cos, sin):
    half = ROPE_DIM // 2
    xf = x.astype(jnp.float32)
    x1, x2 = xf[..., :half], xf[..., half:]
    out = jnp.concatenate([x1 * cos - x2 * sin, x1 * sin + x2 * cos], axis=-1)
    return out.astype(x.dtype)

def conv_module(u, conv_w, conv_b, ln_g, ln_b, w_proj):
    a, gt = jnp.split(u, 2, axis=-1)
    h = a * jax.nn.sigmoid(gt)
    h = lax.conv_general_dilated(
        h, conv_w[:, None, :].astype(h.dtype), window_strides=(1,), padding=[(CONV_K - 1, 0)],
        dimension_numbers=('NWC', 'WIO', 'NWC'), feature_group_count=CONV_DIM) + conv_b
    h = jax.nn.silu(layer_norm(h, ln_g, ln_b))
    return h @ w_proj

def causal_block_attention(q, k, v):
    B, L, H, Dq = q.shape
    n_blk = -(-L // Q_BLOCK)
    Lp = n_blk * Q_BLOCK
    qp = jnp.pad(q, ((0, 0), (0, Lp - L), (0, 0), (0, 0)))
    qb = qp.reshape(B, n_blk, Q_BLOCK, H, Dq).transpose(1, 0, 2, 3, 4)
    starts = jnp.arange(n_blk, dtype=jnp.int32) * Q_BLOCK
    k_pos = jnp.arange(L, dtype=jnp.int32)
    scale = Dq ** -0.5

    def one_block(args):
        q_blk, start = args
        s = jnp.einsum('bqhd,bkhd->bhqk', q_blk, k).astype(jnp.float32) * scale
        q_pos = start + jnp.arange(Q_BLOCK, dtype=jnp.int32)
        mask = k_pos[None, :] <= q_pos[:, None]
        s = jnp.where(mask, s, -1e30)
        p = jax.nn.softmax(s, axis=-1).astype(v.dtype)
        return jnp.einsum('bhqk,bkhd->bqhd', p, v)

    ob = lax.map(one_block, (qb, starts))
    return ob.transpose(1, 0, 2, 3, 4).reshape(B, Lp, H, V_DIM)[:, :L]

def mla(c_q, c_kv, k_rope, cos, sin, q_a_g, w_uq, kv_a_g, w_ukv, q_norm_g, k_norm_g, w_proj):
    B, L = c_q.shape[:2]
    q = (rms_norm(c_q, q_a_g) @ w_uq).reshape(B, L, MLA_HEADS, QK_DIM)
    kv = (rms_norm(c_kv, kv_a_g) @ w_ukv).reshape(B, L, MLA_HEADS, NOPE_DIM + V_DIM)
    k_nope, v = kv[..., :NOPE_DIM], kv[..., NOPE_DIM:]
    k_r = jnp.broadcast_to(k_rope[:, :, None, :], (B, L, MLA_HEADS, ROPE_DIM))
    k = jnp.concatenate([k_nope, k_r], axis=-1)
    q = rms_norm(q, q_norm_g)
    k = rms_norm(k, k_norm_g)
    q = jnp.concatenate([q[..., :NOPE_DIM], apply_rope(q[..., NOPE_DIM:], cos, sin)], axis=-1)
    k = jnp.concatenate([k[..., :NOPE_DIM], apply_rope(k[..., NOPE_DIM:], cos, sin)], axis=-1)
    o = causal_block_attention(q, k, v)
    return o.reshape(B, L, MLA_HEADS * V_DIM) @ w_proj

def hgrn2(q, f_raw, i, g, lb, norm_g, w_proj):
    B, L = q.shape[:2]
    f32 = jnp.float32
    lbf = lb.astype(f32)
    fr = f_raw.astype(f32)
    k = (1.0 - lbf) * jax.nn.sigmoid(-fr)
    log_f = jnp.log1p(-jnp.minimum(k, GATE_CLAMP))
    v = jax.nn.silu(i.astype(f32))
    qf = q.astype(f32)
    pad_front = (-N_META) % HGRN_CHUNK
    pad_back = (-(pad_front + L)) % HGRN_CHUNK
    pads = ((0, 0), (pad_front, pad_back), (0, 0))
    qf, k, v, log_f = [jnp.pad(a, pads) for a in (qf, k, v, log_f)]
    Lp = L + pad_front + pad_back
    nc = Lp // HGRN_CHUNK

    def to_chunks(a, d):
        return a.reshape(B, nc, HGRN_CHUNK, HGRN_HEADS, d).transpose(1, 0, 3, 2, 4)

    qc, kc, lfc = to_chunks(qf, HGRN_DK), to_chunks(k, HGRN_DK), to_chunks(log_f, HGRN_DK)
    vc = to_chunks(v, HGRN_DV)
    causal = jnp.tril(jnp.ones((HGRN_CHUNK, HGRN_CHUNK), dtype=bool))[:, :, None]

    def chunk_step(S, inp):
        q_c, k_c, v_c, lf_c = inp
        b = jnp.cumsum(lf_c, axis=2)
        o_inter = jnp.einsum('bhtk,bhkv->bhtv', q_c * jnp.exp(b), S)
        diff = b[:, :, :, None, :] - b[:, :, None, :, :]
        decay = jnp.where(causal, jnp.exp(jnp.where(causal, diff, 0.0)), 0.0)
        A = jnp.einsum('bhtk,bhtsk,bhsk->bhts', q_c, decay, k_c)
        o_intra = jnp.einsum('bhts,bhsv->bhtv', A, v_c)
        b_last = b[:, :, -1:, :]
        S_new = jnp.exp(b_last[:, :, 0, :])[..., None] * S + jnp.einsum(
            'bhsk,bhsv->bhkv', k_c * jnp.exp(b_last - b), v_c)
        return S_new, o_inter + o_intra

    S0 = jnp.zeros((B, HGRN_HEADS, HGRN_DK, HGRN_DV), f32)
    _, oc = lax.scan(chunk_step, S0, (qc, kc, vc, lfc))
    o = oc.transpose(1, 0, 3, 2, 4).reshape(B, Lp, HGRN_HEADS, HGRN_DV)[:, pad_front:pad_front + L]
    o = o * lax.rsqrt(jnp.mean(o * o, axis=-1, keepdims=True) + EPS)
    o = o.reshape(B, L, HGRN_HEADS * HGRN_DV) * norm_g.astype(f32)
    o = (o * jax.nn.silu(g.astype(f32))).astype(q.dtype)
    return o @ w_proj

def first_inputs(seed: int = 0) -> dict:
    key = jax.random.key(seed)
    ks = iter(jax.random.split(key, 32))

    def nrm(shape, scale):
        return jax.random.normal(next(ks), shape, jnp.float32) * scale

    def gain(shape):
        return 1.0 + 0.1 * nrm(shape, 1.0)

    D = D_MODEL
    return {
        'x': nrm((BATCH, SEQ, D), 1.0),
        'meta': nrm((N_META, D), 1.0),
        'norm1_g': gain((DEPTH, D)),
        'w_in': nrm((DEPTH, D, N_IN), D ** -0.5),
        'conv_w': nrm((DEPTH, CONV_K, CONV_DIM), CONV_K ** -0.5),
        'conv_b': nrm((DEPTH, CONV_DIM), 0.02),
        'conv_ln_g': gain((DEPTH, CONV_DIM)),
        'conv_ln_b': nrm((DEPTH, CONV_DIM), 0.02),
        'w_conv_out': nrm((DEPTH, CONV_DIM, D), CONV_DIM ** -0.5),
        'q_a_norm_g': gain((DEPTH, Q_RANK)),
        'w_uq': nrm((DEPTH, Q_RANK, MLA_HEADS * QK_DIM), Q_RANK ** -0.5),
        'kv_a_norm_g': gain((DEPTH, KV_RANK)),
        'w_ukv': nrm((DEPTH, KV_RANK, MLA_HEADS * (NOPE_DIM + V_DIM)), KV_RANK ** -0.5),
        'q_norm_g': gain((DEPTH, QK_DIM)),
        'k_norm_g': gain((DEPTH, QK_DIM)),
        'w_attn_out': nrm((DEPTH, MLA_HEADS * V_DIM, D), (MLA_HEADS * V_DIM) ** -0.5),
        'hgrn_lb_logits': nrm((DEPTH, HGRN_HEADS * HGRN_DK), 1.0),
        'hgrn_norm_g': gain((DEPTH, HGRN_HEADS * HGRN_DV)),
        'w_hgrn_out': nrm((DEPTH, HGRN_HEADS * HGRN_DV, D), (HGRN_HEADS * HGRN_DV) ** -0.5),
        'w_out': nrm((DEPTH, D, D), D ** -0.5),
        'norm2_g': gain((DEPTH, D)),
        'w_ff1': nrm((DEPTH, D, D_FF), D ** -0.5),
        'w_ff2': nrm((DEPTH, D_FF, D), D_FF ** -0.5),
    }

def first_block(x, meta, norm1_g, w_in, conv_w, conv_b, conv_ln_g, conv_ln_b, w_conv_out,
              q_a_norm_g, w_uq, kv_a_norm_g, w_ukv, q_norm_g, k_norm_g, w_attn_out,
              hgrn_lb_logits, hgrn_norm_g, w_hgrn_out, w_out, norm2_g, w_ff1, w_ff2):
    B = x.shape[0]
    D = D_MODEL
    x = jnp.concatenate([jnp.broadcast_to(meta[None].astype(x.dtype), (B, N_META, D)), x], axis=1)
    L = x.shape[1]
    half = ROPE_DIM // 2
    pos = jnp.arange(L, dtype=jnp.float32)
    inv_freq = ROPE_BASE ** (-jnp.arange(half, dtype=jnp.float32) / half)
    ang = pos[:, None] * inv_freq[None, :]
    cos = jnp.cos(ang)[None, :, None, :]
    sin = jnp.sin(ang)[None, :, None, :]
    p_lb = jax.nn.softmax(hgrn_lb_logits.astype(jnp.float32), axis=0)
    lower_bounds = jnp.cumsum(p_lb, axis=0) - p_lb[0:1]

    for l in range(DEPTH):
        h = rms_norm(x, norm1_g[l])
        u = h @ w_in[l]
        (u_conv, c_q, c_kv, k_rope, hq, hf, hi, hg, u_gate) = jnp.split(u, SPLIT_POINTS, axis=-1)
        y_a = conv_module(u_conv, conv_w[l], conv_b[l], conv_ln_g[l], conv_ln_b[l], w_conv_out[l])
        y_b = mla(c_q, c_kv, k_rope, cos, sin, q_a_norm_g[l], w_uq[l], kv_a_norm_g[l], w_ukv[l],
                  q_norm_g[l], k_norm_g[l], w_attn_out[l])
        y_c = hgrn2(hq, hf, hi, hg, lower_bounds[l], hgrn_norm_g[l], w_hgrn_out[l])
        gates = jax.nn.sigmoid(u_gate).reshape(B, L, N_BRANCH, D)
        mix = gates[:, :, 0] * y_a + gates[:, :, 1] * y_b + gates[:, :, 2] * y_c
        x = x + mix @ w_out[l]
        h2 = rms_norm(x, norm2_g[l])
        x = x + jnp.square(jax.nn.relu(h2 @ w_ff1[l])) @ w_ff2[l]

    return x[:, N_META:]


DEEPNORM_ALPHA = (2.0 * DEPTH) ** 0.25
DEEPNORM_BETA = (8.0 * DEPTH) ** -0.25
LN_EPS = 1e-5

N_ATTN_HEADS = 8
REL_BUCKETS = 32
REL_MAX_DIST = 2048

A_HEADS = 8
A_HEAD_DIM = D_MODEL // 16
A_WIDTH = A_HEADS * A_HEAD_DIM
A_PATTERNS = ((128, 1), (512, 4), (2048, 16))
A_BLOCK = 128

B_HEADS = 4
B_HEAD_DIM = D_MODEL // 8
B_WIDTH = B_HEADS * B_HEAD_DIM
B_CHUNK = 128
B_CONV = 4

AB_AQ = 0
AB_AK = AB_AQ + A_WIDTH
AB_AV = AB_AK + A_WIDTH
AB_BQ = AB_AV + A_WIDTH
AB_BK = AB_BQ + B_WIDTH
AB_BV = AB_BK + B_WIDTH
AB_BO = AB_BV + B_WIDTH
AB_BI = AB_BO + B_WIDTH
AB_BF = AB_BI + B_HEADS
AB_PROJ = AB_BF + B_HEADS
AB_MIX = A_WIDTH + B_WIDTH

C_HEADS = 8
C_GROUPS = 2
C_HPG = C_HEADS // C_GROUPS
C_HEAD_DIM = D_MODEL // 8
C_WIDTH = C_HEADS * C_HEAD_DIM
CMP_BLOCK = 32
CMP_STRIDE = 16
CMP_HIDDEN = 256
SLC_BLOCK = 64
SLC_TOP_N = 16
WIN = 512
C_QBLOCK = 64
C_OFF_KV = C_WIDTH
C_OFF_GATE = C_OFF_KV + 3 * 2 * C_GROUPS * C_HEAD_DIM
C_PROJ = C_OFF_GATE + 3 * C_HEADS

N_GROUPS = 4
EXPERTS_PER_GROUP = 4
N_EXPERTS = N_GROUPS * EXPERTS_PER_GROUP
EXPERT_HIDDEN = D_MODEL // 2
MOE_TOP_K = 2
MOE_CHUNK = 128


def layer_norm_2(x, g, b):
    xf = x.astype(jnp.float32)
    mu = xf.mean(-1, keepdims=True)
    var = jnp.square(xf - mu).mean(-1, keepdims=True)
    y = (xf - mu) * lax.rsqrt(var + LN_EPS) * g.astype(jnp.float32) + b.astype(jnp.float32)
    return y.astype(x.dtype)

def _t5_bucket(dist):
    n = jnp.maximum(dist, 0)
    exact = REL_BUCKETS // 2
    nf = jnp.maximum(n, 1).astype(jnp.float32)
    large = exact + (jnp.log(nf / exact) / math.log(REL_MAX_DIST / exact)
                     * (REL_BUCKETS - exact)).astype(jnp.int32)
    return jnp.where(n < exact, n, jnp.minimum(large, REL_BUCKETS - 1))

def _t5_bias(table, dist):
    return table.astype(jnp.float32)[_t5_bucket(dist)]

def masked_softmax(logits, valid):
    masked = jnp.where(valid, logits.astype(jnp.float32), -jnp.inf)
    m = jnp.max(masked, axis=-1, keepdims=True)
    m = jnp.where(jnp.isfinite(m), m, 0.0)
    p = jnp.exp(masked - m)
    s = p.sum(-1, keepdims=True)
    return p / jnp.maximum(s, 1e-30)

def causal_conv(x, w):
    K, C = w.shape
    return lax.conv_general_dilated(x, w[:, None, :].astype(x.dtype), window_strides=(1,),
                                    padding=[(K - 1, 0)],
                                    dimension_numbers=('NWC', 'WIO', 'NWC'),
                                    feature_group_count=C)

def _dilated_branch(q, k, v, rel_bias, window, dilation):
    Bn, S, H, E = q.shape
    nk = window // dilation
    L = -(-S // dilation)
    nb = -(-L // A_BLOCK)
    Lp = nb * A_BLOCK
    pad = Lp * dilation - S

    def to_res(t):
        t = jnp.pad(t, ((0, 0), (0, pad), (0, 0), (0, 0)))
        t = t.reshape(Bn, Lp, dilation, H, E).transpose(0, 2, 1, 3, 4)
        return t.reshape(Bn, dilation, nb, A_BLOCK, H, E)

    def with_prev(t):
        prev = jnp.pad(t, ((0, 0), (0, 0), (1, 0), (0, 0), (0, 0), (0, 0)))[:, :, :-1]
        return jnp.concatenate([prev, t], axis=3)

    qb = to_res(q)
    kk = with_prev(to_res(k))
    vv = with_prev(to_res(v))
    logits = jnp.einsum('brnqhe,brnkhe->brnhqk', qb, kk).astype(jnp.float32) * (E ** -0.5)
    qi = jnp.arange(A_BLOCK)[:, None]
    ki = jnp.arange(2 * A_BLOCK)[None, :]
    j = qi + A_BLOCK - ki
    valid = (j >= 0) & (j <= nk)
    bias = _t5_bias(rel_bias, jnp.maximum(j, 0) * dilation).transpose(2, 0, 1)
    first = (jnp.arange(nb)[:, None, None] > 0) | (ki[None] >= A_BLOCK)
    valid = valid[None] & first
    logits = jnp.where(valid[None, None, :, None], logits + bias, -jnp.inf)
    m = logits.max(-1, keepdims=True)
    p = jnp.exp(logits - m)
    s = p.sum(-1)
    o = jnp.einsum('brnhqk,brnkhe->brnhqe', p, vv.astype(jnp.float32)) / s[..., None]
    lse = m[..., 0] + jnp.log(s)
    o = o.transpose(0, 2, 4, 1, 3, 5).reshape(Bn, Lp * dilation, H, E)[:, :S]
    lse = lse.transpose(0, 2, 4, 1, 3).reshape(Bn, Lp * dilation, H)[:, :S]
    return o, lse

def dilated_attention(q, k, v, rel_bias):
    outs, lses = [], []
    for window, dilation in A_PATTERNS:
        o, lse = _dilated_branch(q, k, v, rel_bias, window, dilation)
        outs.append(o)
        lses.append(lse)
    wts = jax.nn.softmax(jnp.stack(lses, 0), axis=0)
    return jnp.einsum('pbsh,pbshe->bshe', wts, jnp.stack(outs, 0))

def mlstm(q, k, v, i_pre, f_pre):
    f32 = jnp.float32
    Bn, S, H, dk = q.shape
    dv = v.shape[-1]
    L = B_CHUNK
    nc = S // L

    def chunks(t):
        t = t.astype(f32).reshape((Bn, nc, L) + t.shape[2:])
        return t.transpose((1, 0, 3, 2) + tuple(range(4, t.ndim)))

    qc = chunks(q) * (dk ** -0.5)
    kc, vc = chunks(k), chunks(v)
    ic = chunks(i_pre)
    fc = chunks(jax.nn.log_sigmoid(f_pre.astype(f32)))
    tri = jnp.tril(jnp.ones((L, L), bool))

    def step(carry, inp):
        C, n, m = carry
        qt, kt, vt, it, ft = inp
        b = jnp.cumsum(ft, axis=-1)
        Dm = jnp.where(tri, b[..., :, None] - b[..., None, :] + it[..., None, :], -jnp.inf)
        inter = b + m[..., None]
        m_t = jnp.maximum(inter, Dm.max(-1))
        P = jnp.exp(Dm - m_t[..., None])
        Sqk = jnp.einsum('bhtd,bhsd->bhts', qt, kt) * P
        sc = jnp.exp(inter - m_t)
        num = sc[..., None] * jnp.einsum('bhtd,bhdv->bhtv', qt, C) + jnp.einsum('bhts,bhsv->bhtv', Sqk, vt)
        den = sc * jnp.einsum('bhtd,bhd->bht', qt, n) + Sqk.sum(-1)
        h = num / jnp.maximum(jnp.abs(den), jnp.exp(-m_t))[..., None]
        bL = b[..., -1]
        g = bL[..., None] - b + it
        m_new = jnp.maximum(bL + m, g.max(-1))
        wk = jnp.exp(g - m_new[..., None])
        decay = jnp.exp(bL + m - m_new)
        C_new = decay[..., None, None] * C + jnp.einsum('bhs,bhsd,bhsv->bhdv', wk, kt, vt)
        n_new = decay[..., None] * n + jnp.einsum('bhs,bhsd->bhd', wk, kt)
        return (C_new, n_new, m_new), h

    init = (jnp.zeros((Bn, H, dk, dv), f32), jnp.zeros((Bn, H, dk), f32), jnp.zeros((Bn, H), f32))
    _, hs = lax.scan(step, init, (qc, kc, vc, ic, fc))
    return hs.transpose(1, 0, 3, 2, 4).reshape(Bn, S, H, dv)

def head_norm(h, g):
    mu = h.mean(-1, keepdims=True)
    var = jnp.square(h - mu).mean(-1, keepdims=True)
    y = (h - mu) * lax.rsqrt(var + LN_EPS)
    return y.reshape(h.shape[0], h.shape[1], -1) * g.astype(jnp.float32)

def mixer_ab(x, w_in, gate_b, conv_w, head_g, w_out, rel_bias):
    Bn, S, _ = x.shape
    p = jnp.einsum('bsd,de->bse', x, w_in)
    aq = p[..., AB_AQ:AB_AK].reshape(Bn, S, A_HEADS, A_HEAD_DIM)
    ak = p[..., AB_AK:AB_AV].reshape(Bn, S, A_HEADS, A_HEAD_DIM)
    av = p[..., AB_AV:AB_BQ].reshape(Bn, S, A_HEADS, A_HEAD_DIM)
    qk = jax.nn.silu(causal_conv(p[..., AB_BQ:AB_BV], conv_w))
    bq = qk[..., :B_WIDTH].reshape(Bn, S, B_HEADS, B_HEAD_DIM)
    bk = qk[..., B_WIDTH:].reshape(Bn, S, B_HEADS, B_HEAD_DIM)
    bv = p[..., AB_BV:AB_BO].reshape(Bn, S, B_HEADS, B_HEAD_DIM)
    bo = p[..., AB_BO:AB_BI]
    bi = p[..., AB_BI:AB_BF] + gate_b[:B_HEADS]
    bf = p[..., AB_BF:AB_PROJ] + gate_b[B_HEADS:]
    ya = dilated_attention(aq, ak, av, rel_bias).reshape(Bn, S, A_WIDTH)
    yb = jax.nn.sigmoid(bo.astype(jnp.float32)) * head_norm(mlstm(bq, bk, bv, bi, bf), head_g)
    y = jnp.concatenate([ya.astype(x.dtype), yb.astype(x.dtype)], axis=-1)
    return jnp.einsum('bse,ed->bsd', y, w_out)

def mixer_c(x, w_in, gate_b, cmp_pos, cmp_w1, cmp_w2, w_out, rel_bias):
    f32 = jnp.float32
    Bn, S, _ = x.shape
    G, J, E = C_GROUPS, C_HPG, C_HEAD_DIM
    p = jnp.einsum('bsd,de->bse', x, w_in)
    q = p[..., :C_OFF_KV].reshape(Bn, S, G, J, E).transpose(0, 2, 3, 1, 4).astype(f32) * (E ** -0.5)
    kv = p[..., C_OFF_KV:C_OFF_GATE].reshape(Bn, S, 3, 2, G, E).astype(f32)
    gates = jax.nn.sigmoid((p[..., C_OFF_GATE:] + gate_b).astype(f32)).reshape(Bn, S, 3, G, J)

    n_cmp = (S - CMP_BLOCK) // CMP_STRIDE + 1
    cidx = jnp.arange(n_cmp)[:, None] * CMP_STRIDE + jnp.arange(CMP_BLOCK)[None, :]
    cmp_start, cmp_end = cidx[:, 0], cidx[:, -1]

    def compress(t, pos, w1, w2):
        blocks = t[:, cidx] + pos[None, None, :, None, :]
        flat = blocks.transpose(0, 3, 1, 2, 4).reshape(Bn, G, n_cmp, CMP_BLOCK * E)
        return (jax.nn.gelu(flat @ w1) @ w2).astype(f32)

    k_cmp = compress(kv[:, :, 0, 0], cmp_pos[0], cmp_w1[0], cmp_w2[0])
    v_cmp = compress(kv[:, :, 0, 1], cmp_pos[1], cmp_w1[1], cmp_w2[1])

    n_slc = S // SLC_BLOCK
    top_n = min(SLC_TOP_N, n_slc)
    slc_start = jnp.arange(n_slc) * SLC_BLOCK

    def blocks_of(t):
        return t.transpose(0, 2, 1, 3).reshape(Bn, G, n_slc, SLC_BLOCK * E)

    k_sb, v_sb = blocks_of(kv[:, :, 1, 0]), blocks_of(kv[:, :, 1, 1])
    overlap = ((cmp_start[:, None] < slc_start[None, :] + SLC_BLOCK)
               & (cmp_end[:, None] >= slc_start[None, :])).astype(f32)

    def pad_win(t):
        return jnp.pad(t.transpose(0, 2, 1, 3), ((0, 0), (0, 0), (WIN, 0), (0, 0)))

    k_w, v_w = pad_win(kv[:, :, 2, 0]), pad_win(kv[:, :, 2, 1])

    tb = rel_bias.astype(f32).reshape(REL_BUCKETS, G, J)
    tb_g = tb.transpose(1, 0, 2)
    gsel = jnp.arange(G)[None, :, None, None]

    def grouped_bias(dist2d):
        return tb[_t5_bucket(dist2d)].transpose(2, 3, 0, 1)

    def block(blk):
        s0 = blk * C_QBLOCK
        qpos = s0 + jnp.arange(C_QBLOCK)
        qb = lax.dynamic_slice_in_dim(q, s0, C_QBLOCK, axis=3)
        dist_c = qpos[:, None] - cmp_end[None, :]
        lc = jnp.einsum('bgjqe,bgne->bgjqn', qb, k_cmp) + grouped_bias(dist_c)
        p_c = masked_softmax(lc, dist_c >= 0)
        o_c = jnp.einsum('bgjqn,bgne->bgjqe', p_c, v_cmp)
        imp = jnp.einsum('bgjqn,nm->bgqm', p_c, overlap)
        mblk = jnp.arange(n_slc)[None, :]
        qblk = (qpos // SLC_BLOCK)[:, None]
        forced = (mblk == 0) | (mblk == qblk) | (mblk == qblk - 1)
        score = jnp.where(forced, jnp.inf,
                          jnp.where(slc_start[None, :] <= qpos[:, None], imp, -jnp.inf))
        _, sel = lax.top_k(score, top_n)
        flat_sel = sel.reshape(Bn, G, C_QBLOCK * top_n, 1)
        T = top_n * SLC_BLOCK
        ks = jnp.take_along_axis(k_sb, flat_sel, axis=2).reshape(Bn, G, C_QBLOCK, T, E)
        vs = jnp.take_along_axis(v_sb, flat_sel, axis=2).reshape(Bn, G, C_QBLOCK, T, E)
        kpos_s = (sel[..., None] * SLC_BLOCK + jnp.arange(SLC_BLOCK)).reshape(Bn, G, C_QBLOCK, T)
        dist_s = qpos[None, None, :, None] - kpos_s
        bias_s = jnp.moveaxis(tb_g[gsel, _t5_bucket(dist_s)], -1, 2)
        ls = jnp.einsum('bgjqe,bgqte->bgjqt', qb, ks) + bias_s
        p_s = masked_softmax(ls, (dist_s >= 0)[:, :, None])
        o_s = jnp.einsum('bgjqt,bgqte->bgjqe', p_s, vs)
        kw = lax.dynamic_slice_in_dim(k_w, s0, WIN + C_QBLOCK, axis=2)
        vw = lax.dynamic_slice_in_dim(v_w, s0, WIN + C_QBLOCK, axis=2)
        kpos_w = s0 - WIN + jnp.arange(WIN + C_QBLOCK)
        dist_w = qpos[:, None] - kpos_w[None, :]
        valid_w = (dist_w >= 0) & (dist_w < WIN) & (kpos_w[None, :] >= 0)
        lw = jnp.einsum('bgjqe,bgte->bgjqt', qb, kw) + grouped_bias(dist_w)
        p_w = masked_softmax(lw, valid_w)
        o_w = jnp.einsum('bgjqt,bgte->bgjqe', p_w, vw)
        g = lax.dynamic_slice_in_dim(gates, s0, C_QBLOCK, axis=1).transpose(2, 0, 3, 4, 1)
        return g[0][..., None] * o_c + g[1][..., None] * o_s + g[2][..., None] * o_w

    out = lax.map(block, jnp.arange(S // C_QBLOCK))
    out = out.transpose(1, 0, 4, 2, 3, 5).reshape(Bn, S, C_WIDTH)
    return jnp.einsum('bse,ed->bsd', out.astype(x.dtype), w_out)

def hier_moe(x, wr_g, br_g, wr_e, br_e, w_gate, w_up, w_down):
    f32 = jnp.float32
    Bn, S, D = x.shape
    xt = x.reshape(-1, D)
    g_logits = (xt @ wr_g + br_g).astype(f32)
    g_prob = jax.nn.softmax(g_logits, axis=-1)
    _, g_idx = lax.top_k(g_logits, 1)
    g_w = jnp.take_along_axis(g_prob, g_idx, axis=-1)[:, 0]
    e_all = (jnp.einsum('nd,gde->nge', xt, wr_e) + br_e).astype(f32)
    e_logits = jnp.take_along_axis(e_all, g_idx[:, :, None], axis=1)[:, 0]
    top_v, top_i = lax.top_k(e_logits, MOE_TOP_K)
    e_w = jax.nn.softmax(top_v, axis=-1) * g_w[:, None]
    expert_id = g_idx * EXPERTS_PER_GROUP + top_i
    gates = jnp.einsum('nk,nke->ne', e_w, jax.nn.one_hot(expert_id, N_EXPERTS, dtype=f32))
    wg = w_gate.transpose(1, 0, 2).reshape(D, N_EXPERTS * EXPERT_HIDDEN)
    wu = w_up.transpose(1, 0, 2).reshape(D, N_EXPERTS * EXPERT_HIDDEN)
    wd = w_down.reshape(N_EXPERTS * EXPERT_HIDDEN, D)

    def chunk_fn(args):
        xc, gc = args
        h = jax.nn.silu(xc @ wg) * (xc @ wu)
        h = (h.reshape(-1, N_EXPERTS, EXPERT_HIDDEN) * gc[..., None]).reshape(-1, N_EXPERTS * EXPERT_HIDDEN)
        return h @ wd

    out = lax.map(chunk_fn, (xt.reshape(-1, MOE_CHUNK, D), gates.reshape(-1, MOE_CHUNK, N_EXPERTS)))
    return out.reshape(Bn, S, D).astype(x.dtype)

def second_inputs(seed: int = 0) -> dict:
    key = jax.random.key(seed)
    ks = iter(jax.random.split(key, 32))

    def nrm(shape, scale):
        return jax.random.normal(next(ks), shape, jnp.float32) * scale

    n_even = (DEPTH + 1) // 2
    n_odd = DEPTH // 2
    D = D_MODEL
    ab_col = np.ones(AB_PROJ, np.float32)
    ab_col[AB_AV:AB_AV + A_WIDTH] = DEEPNORM_BETA
    ab_col[AB_BV:AB_BV + B_WIDTH] = DEEPNORM_BETA
    kv_col = np.ones((3, 2, C_GROUPS * C_HEAD_DIM), np.float32)
    kv_col[:, 1] = DEEPNORM_BETA
    c_col = np.concatenate([np.ones(C_WIDTH, np.float32), kv_col.ravel(), np.ones(3 * C_HEADS, np.float32)])
    return {
        "x": nrm((BATCH, SEQ, D), 1.0),
        "rel_bias": nrm((REL_BUCKETS, N_ATTN_HEADS), 0.2),
        "ln_g": 1.0 + nrm((DEPTH, 2, D), 0.02),
        "ln_b": nrm((DEPTH, 2, D), 0.02),
        "ab_w_in": nrm((n_even, D, AB_PROJ), D ** -0.5) * jnp.asarray(ab_col),
        "ab_gate_b": jnp.concatenate([nrm((n_even, B_HEADS), 0.1),
                                      3.0 + nrm((n_even, B_HEADS), 0.5)], axis=-1),
        "ab_conv": nrm((n_even, B_CONV, 2 * B_WIDTH), B_CONV ** -0.5),
        "ab_head_norm": 1.0 + nrm((n_even, B_WIDTH), 0.02),
        "ab_w_out": nrm((n_even, AB_MIX, D), AB_MIX ** -0.5 * DEEPNORM_BETA),
        "c_w_in": nrm((n_odd, D, C_PROJ), D ** -0.5) * jnp.asarray(c_col),
        "c_gate_b": nrm((n_odd, 3 * C_HEADS), 0.1),
        "c_cmp_pos": nrm((n_odd, 2, CMP_BLOCK, C_HEAD_DIM), 0.1),
        "c_cmp_w1": nrm((n_odd, 2, CMP_BLOCK * C_HEAD_DIM, CMP_HIDDEN), (CMP_BLOCK * C_HEAD_DIM) ** -0.5),
        "c_cmp_w2": nrm((n_odd, 2, CMP_HIDDEN, C_HEAD_DIM), CMP_HIDDEN ** -0.5),
        "c_w_out": nrm((n_odd, C_WIDTH, D), C_WIDTH ** -0.5 * DEEPNORM_BETA),
        "moe_wr_g": nrm((DEPTH, D, N_GROUPS), D ** -0.5),
        "moe_br_g": nrm((DEPTH, N_GROUPS), 0.01),
        "moe_wr_e": nrm((DEPTH, N_GROUPS, D, EXPERTS_PER_GROUP), D ** -0.5),
        "moe_br_e": nrm((DEPTH, N_GROUPS, EXPERTS_PER_GROUP), 0.01),
        "moe_w_gate": nrm((DEPTH, N_EXPERTS, D, EXPERT_HIDDEN), D ** -0.5),
        "moe_w_up": nrm((DEPTH, N_EXPERTS, D, EXPERT_HIDDEN), D ** -0.5),
        "moe_w_down": nrm((DEPTH, N_EXPERTS, EXPERT_HIDDEN, D), EXPERT_HIDDEN ** -0.5 * DEEPNORM_BETA),
    }

def second_block(x, rel_bias, ln_g, ln_b, ab_w_in, ab_gate_b, ab_conv, ab_head_norm, ab_w_out,
              c_w_in, c_gate_b, c_cmp_pos, c_cmp_w1, c_cmp_w2, c_w_out,
              moe_wr_g, moe_br_g, moe_wr_e, moe_br_e, moe_w_gate, moe_w_up, moe_w_down):
    h = x
    for layer in range(DEPTH):
        j = layer // 2
        if layer % 2 == 0:
            y = mixer_ab(h, ab_w_in[j], ab_gate_b[j], ab_conv[j], ab_head_norm[j], ab_w_out[j], rel_bias)
        else:
            y = mixer_c(h, c_w_in[j], c_gate_b[j], c_cmp_pos[j], c_cmp_w1[j], c_cmp_w2[j], c_w_out[j], rel_bias)
        h = layer_norm_2(DEEPNORM_ALPHA * h + y, ln_g[layer, 0], ln_b[layer, 0])
        y = hier_moe(h, moe_wr_g[layer], moe_br_g[layer], moe_wr_e[layer], moe_br_e[layer],
                     moe_w_gate[layer], moe_w_up[layer], moe_w_down[layer])
        h = layer_norm_2(DEEPNORM_ALPHA * h + y, ln_g[layer, 1], ln_b[layer, 1])
    return h


def setup_inputs(seed=0):
    out = dict(first_inputs(seed))
    for name, value in second_inputs(seed + 1).items():
        if name != "x":
            out[name + "_2"] = value
    return out


def reference(
    x, meta, norm1_g, w_in, conv_w, conv_b, conv_ln_g, conv_ln_b, w_conv_out, q_a_norm_g, w_uq,
    kv_a_norm_g, w_ukv, q_norm_g, k_norm_g, w_attn_out, hgrn_lb_logits, hgrn_norm_g, w_hgrn_out,
    w_out, norm2_g, w_ff1, w_ff2, rel_bias_2, ln_g_2, ln_b_2, ab_w_in_2, ab_gate_b_2, ab_conv_2,
    ab_head_norm_2, ab_w_out_2, c_w_in_2, c_gate_b_2, c_cmp_pos_2, c_cmp_w1_2, c_cmp_w2_2,
    c_w_out_2, moe_wr_g_2, moe_br_g_2, moe_wr_e_2, moe_br_e_2, moe_w_gate_2, moe_w_up_2,
    moe_w_down_2,
):
    x = first_block(
        x, meta, norm1_g, w_in, conv_w, conv_b, conv_ln_g, conv_ln_b, w_conv_out, q_a_norm_g,
        w_uq, kv_a_norm_g, w_ukv, q_norm_g, k_norm_g, w_attn_out, hgrn_lb_logits, hgrn_norm_g,
        w_hgrn_out, w_out, norm2_g, w_ff1, w_ff2,
    )
    return second_block(
        x, rel_bias_2, ln_g_2, ln_b_2, ab_w_in_2, ab_gate_b_2, ab_conv_2, ab_head_norm_2,
        ab_w_out_2, c_w_in_2, c_gate_b_2, c_cmp_pos_2, c_cmp_w1_2, c_cmp_w2_2, c_w_out_2,
        moe_wr_g_2, moe_br_g_2, moe_wr_e_2, moe_br_e_2, moe_w_gate_2, moe_w_up_2, moe_w_down_2,
    )


_drawn_inputs = setup_inputs


def setup_inputs(seed=0):
    import zlib

    import numpy as np

    out = dict(_drawn_inputs(seed))
    spreads = {}
    factors = {'conv_ln_b': 4.386,
     'q_a_norm_g': 3.512,
     'q_norm_g': 3.492,
     'k_norm_g': 3.84,
     'rel_bias_2': 4.632,
     'ab_conv_2': 2.825,
     'ab_head_norm_2': 34.105,
     'c_gate_b_2': 8.0,
     'c_cmp_pos_2': 4.663,
     'moe_br_g_2': 7.07,
     'moe_br_e_2': 26.068}
    for name, (base, spread) in spreads.items():
        noise = np.random.default_rng([zlib.crc32(name.encode()), seed]).standard_normal(out[name].shape)
        drawn = base * np.exp(spread * noise) if base else spread * noise
        out[name] = jnp.asarray(drawn.astype(out[name].dtype))
    for name, factor in factors.items():
        out[name] = (out[name] * factor).astype(out[name].dtype)
    return out
```

```python
from contextlib import ExitStack

import numpy as np

import concourse.bass as bass
from concourse import mybir

F32 = mybir.dt.float32
ALU = mybir.AluOpType
ACT = mybir.ActivationFunctionType
AX = mybir.AxisListType

D = 1024
KT = D // 128
DEPTH = 2
N_META = 16
SEQ = 256
T = SEQ + N_META
TOK1 = [(0, 128), (128, 128), (256, T - 256)]
TP = 288
EPS = 1e-6
CLAMP = 1.0 - 1e-6
CONV_K = 31
HEADS = 8
NOPE, ROPE, QK, VD = 64, 32, 96, 64
H4 = 4
SB, SS = 32, 4
NB = TP // SB
D_FF = 4 * D
FT = D_FF // 128
ALPHA = (2.0 * DEPTH) ** 0.25
LN_EPS = 1e-5
BUCKETS, MAX_DIST = 32, 2048
NCMP = (SEQ - 32) // 16 + 1
NEXP, EH = 16, D // 2
NEG = -1e30
A_SCALE, C_SCALE = 64 ** -0.5, 128 ** -0.5

CHUNK = 1024
RING = 12


def feature_chunks(w):
    k, m = w.shape
    return w.reshape(k // 128, 128, m // 128, 128).transpose(2, 1, 0, 3).reshape(m // 128, 128, k)


def grouped(w, n):
    t = feature_chunks(w)
    return t.reshape(t.shape[0] // n, n, 128, -1).transpose(0, 2, 1, 3).reshape(-1, 128, n * t.shape[2])


def token_chunks(w):
    return w.reshape(4, 2, 128, 512).transpose(0, 2, 1, 3).reshape(4, 128, 1024)


def padded(a):
    out = np.zeros((a.shape[0], 128, CHUNK), np.float32)
    out[:, :, : a.shape[2]] = a
    return out


def weight_stream(i):
    out = []
    for l in range(DEPTH):
        w = i["w_in"][l]
        at = np.cumsum([0, 1024, 256, 128, 32, 512, 512, 512, 512, 3072])
        conv, cq, ckv, rope, hq, hf, hi, hg, gate = (w[:, at[j] : at[j + 1]] for j in range(9))
        c = feature_chunks(conv)
        out += [c.reshape(2, 4, 128, 1024).transpose(1, 0, 2, 3).reshape(8, 128, 1024)]
        out += [feature_chunks(hf), feature_chunks(hq), feature_chunks(hg), token_chunks(hi)]
        out += [feature_chunks(cq), feature_chunks(ckv)]
        r = np.zeros((D, 128), np.float32)
        r[:, NOPE:QK] = rope
        out += [feature_chunks(r)]
        gates = [feature_chunks(gate[:, g * D : (g + 1) * D]) for g in range(3)]
        out += [gates[0], grouped(i["w_conv_out"][l], 2), gates[2]]
        uq = i["w_uq"][l].reshape(2, 128, HEADS, QK).transpose(2, 1, 0, 3)
        out += [padded(uq.reshape(2, 4, 128, 2 * QK).transpose(0, 2, 1, 3).reshape(2, 128, 8 * QK))]
        ukv = i["w_ukv"][l].reshape(128, HEADS, 2, 64).transpose(0, 2, 1, 3)
        out += [ukv.reshape(1, 128, 1024)]
        out += [grouped(i["w_hgrn_out"][l], 2), gates[1], grouped(i["w_attn_out"][l], 2)]
        out += [feature_chunks(i["w_out"][l]), feature_chunks(i["w_ff1"][l])]
        f2 = feature_chunks(i["w_ff2"][l])
        out += [f2.reshape(KT, 128, 4, 1024).transpose(0, 2, 1, 3).reshape(-1, 128, 1024)]
    w = i["ab_w_in_2"][0]
    part = lambda j: w[:, 512 * j : 512 * j + 512]
    out += [feature_chunks(part(0)), feature_chunks(part(1)), token_chunks(part(2))]
    out += [feature_chunks(part(3)), feature_chunks(part(4)), token_chunks(part(5)), feature_chunks(part(6))]
    out += [feature_chunks(i["ab_w_out_2"][0])]
    moe = lambda l: experts(i["moe_w_gate_2"][l], i["moe_w_up_2"][l], i["moe_w_down_2"][l])
    out += [moe(0)]
    w = i["c_w_in_2"][0]
    kv = w[:, D : D + 1536].reshape(D, 3, 2, 256)
    out += [feature_chunks(kv[:, 0].reshape(D, 512)), feature_chunks(w[:, :D])]
    out += [feature_chunks(kv[:, 1, 0]), feature_chunks(kv[:, 2, 0])]
    out += [token_chunks(kv[:, 1:, 1].reshape(D, 512))]
    for s in range(2):
        out += [i["c_cmp_w1_2"][0, s].reshape(8, 4, 128, 256).transpose(0, 2, 1, 3).reshape(8, 128, 1024)]
    w2 = i["c_cmp_w2_2"][0].reshape(2, 2, 128, 128).transpose(2, 0, 1, 3).reshape(1, 128, 512)
    out += [padded(w2), feature_chunks(i["c_w_out_2"][0]), moe(1)]
    return np.concatenate(out, axis=0)


def experts(gate, up, down):
    out = []
    for e in range(NEXP):
        g, u = feature_chunks(gate[e]), feature_chunks(up[e])
        out += [np.stack([g, u], 1).reshape(8, 128, 1024), grouped(down[e], 2)]
    return np.concatenate(out, axis=0)


def layout(widths):
    at, out = 0, {}
    for name, n in widths:
        out[name] = (at, n)
        at += n
    return out, at


PARAMS, NPAR = layout(
    [(f"{n}{l}", c) for l in range(DEPTH) for n, c in (
        ("norm1", 8), ("convw", 4 * CONV_K), ("convb", 4), ("clng", 4), ("clnb", 4), ("qa", 2), ("kva", 1),
        ("qn", 1), ("kn", 1), ("lb", 4), ("hn", 4), ("norm2", 8),
        ("lng0_", 8), ("lnb0_", 8), ("lng1_", 8), ("lnb1_", 8), ("router", KT * 20), ("rbias", 20))]
    + [("ibias", 1), ("fbias", 1), ("abconv", 8 * 4), ("abhead", 4), ("wif", KT * 8),
       ("pos", 64), ("wcg", KT * 24), ("cgbias", 24), ("rel", HEADS)])

CONSTS, NCONST = layout([
    ("ident", 128), ("flip", 128), ("ones", 128), ("causal", 528), ("logcount", 256), ("tri", SB),
    ("cos", T), ("sin", T), ("bucket", 384), ("rank", 4)])


def parameters(i):
    out = np.zeros((128, NPAR), np.float32)

    def put(name, a):
        at, n = PARAMS[name]
        a = np.asarray(a, np.float32)
        a = a.reshape(a.shape[0], -1)
        out[: a.shape[0], at : at + n] = a

    col = lambda v: np.asarray(v).reshape(-1, 128).T
    for l in range(DEPTH):
        put(f"norm1{l}", col(i["norm1_g"][l]))
        put(f"convw{l}", i["conv_w"][l].reshape(CONV_K, 4, 128).transpose(2, 1, 0))
        put(f"convb{l}", col(i["conv_b"][l]))
        put(f"clng{l}", col(i["conv_ln_g"][l]))
        put(f"clnb{l}", col(i["conv_ln_b"][l]))
        put(f"qa{l}", col(i["q_a_norm_g"][l]))
        put(f"kva{l}", col(i["kv_a_norm_g"][l]))
        put(f"qn{l}", i["q_norm_g"][l][:, None])
        put(f"kn{l}", i["k_norm_g"][l][:, None])
        put(f"lb{l}", col(i["hgrn_lb_logits"][l]))
        put(f"hn{l}", col(i["hgrn_norm_g"][l]))
        put(f"norm2{l}", col(i["norm2_g"][l]))
        for j in range(2):
            put(f"lng{j}_{l}", col(i["ln_g_2"][l, j]))
            put(f"lnb{j}_{l}", col(i["ln_b_2"][l, j]))
        r = np.concatenate([i["moe_wr_g_2"][l], i["moe_wr_e_2"][l].transpose(1, 0, 2).reshape(D, 16)], axis=1)
        put(f"router{l}", r.reshape(KT, 128, 20).transpose(1, 0, 2))
        put(f"rbias{l}", np.concatenate([i["moe_br_g_2"][l], i["moe_br_e_2"][l].reshape(-1)])[None])
    put("ibias", i["ab_gate_b_2"][0, :4][:, None])
    put("fbias", i["ab_gate_b_2"][0, 4:][:, None])
    put("abconv", i["ab_conv_2"][0].reshape(4, 8, 128).transpose(2, 1, 0))
    put("abhead", col(i["ab_head_norm_2"][0]))
    put("wif", i["ab_w_in_2"][0][:, 3584:3592].reshape(KT, 128, 8).transpose(1, 0, 2))
    put("pos", i["c_cmp_pos_2"][0].transpose(2, 0, 1))
    put("wcg", i["c_w_in_2"][0][:, 2560:2584].reshape(KT, 128, 24).transpose(1, 0, 2))
    put("cgbias", i["c_gate_b_2"][0][None])
    put("rel", i["rel_bias_2"])
    return out


def constants():
    out = np.zeros((128, NCONST), np.float32)

    def put(name, a, row=0):
        at, n = CONSTS[name]
        out[row : row + a.shape[0], at : at + n] = a.reshape(a.shape[0], -1)

    p = np.arange(128)
    put("ident", np.eye(128))
    put("flip", np.eye(128)[::-1])
    put("ones", np.ones((128, 128)))
    put("causal", np.where(np.arange(528)[None] - 256 <= p[:, None], 0.0, NEG))
    d = p[:, None] + 128 - np.arange(256)[None]
    n = ((d <= 128).astype(int) + (d % 4 == 0) + (d % 16 == 0)) * (d >= 0)
    put("logcount", np.where(n > 0, np.log(np.maximum(n, 1)), NEG))
    put("tri", (np.arange(SB)[None] <= (p % SB)[:, None]).astype(float))
    half = ROPE // 2
    inv = 10000.0 ** (-np.arange(half, dtype=np.float32) / np.float32(half))
    ang = (np.arange(T, dtype=np.float32)[None] * inv.astype(np.float32)[:, None]).astype(np.float32)
    put("cos", np.concatenate([np.cos(ang)] * 2), NOPE)
    put("sin", np.concatenate([-np.sin(ang), np.sin(ang)]), NOPE)
    n = np.maximum(255 - np.arange(384), 0)
    exact = BUCKETS // 2
    large = exact + (np.log(np.maximum(n, 1) / exact) / np.log(MAX_DIST / exact) * (BUCKETS - exact)).astype(int)
    put("bucket", (np.where(n < exact, n, np.minimum(large, BUCKETS - 1))[None] == np.arange(BUCKETS)[:, None]).astype(float))
    put("rank", np.tile([4.0, 3.0, 2.0, 1.0], (128, 1)))
    return out


class Lane:

    def __init__(self, eng, step):
        self.eng, self.step, self.count, self.loop = eng, step, {}, None

    def __call__(self, ins, sem=None):
        sem = sem or self.step
        n = self.count[sem.name] = self.count.get(sem.name, 0) + 1
        ins.then_inc(sem, 1)
        self.eng.wait_ge(sem, self.at(sem, n))

    def at(self, sem, n):
        return n if self.loop is None else n + self.loop[0] * self.loop[1][sem.name]

    def enter(self, i, per):
        self.loop, self.before = (i, per), dict(self.count)

    def leave(self, times):
        for name, n in self.loop[1].items():
            assert self.count.get(name, 0) - self.before.get(name, 0) == n, (name, self.count[name], self.before.get(name, 0))
            self.count[name] += n * (times - 1)
        self.loop = None


class Banks:

    def __init__(self, psum, full, free):
        self.psum, self.full, self.free = psum, full, free
        self.next, self.uses, self.of = 0, [0] * 8, {}
        self.loop = None

    def value(self, n, loop):
        return n if loop is None else n + loop

    def take(self, pe, key):
        b, n = self.next, self.uses[self.next]
        self.next, self.uses[b] = (b + 1) % 8, n + 1
        assert key not in self.of, key
        self.of[key] = (b, n)
        if n:
            pe.wait_ge(self.free[b], n if self.loop is None else n + self.loop)
        return self.psum[:, b, :]

    def filled(self, key):
        return self.full[self.of[key][0]]

    def await_(self, eng, key, loop=None):
        b, n = self.of[key]
        eng.wait_ge(self.full[b], n + 1 if loop is None else n + 1 + loop)
        return self.psum[:, b, :]

    def freed(self, key):
        return self.free[self.of[key][0]]

    def await_read(self, eng, key, loop=None):
        b, n = self.of[key]
        eng.wait_ge(self.free[b], n + 1 if loop is None else n + 1 + loop)


def build_program(nc, stream, params, consts, x_in, out, scratch):
    n_chunks = stream.shape[0] // 128
    with ExitStack() as ctx:
        def sb(name, *shape):
            return ctx.enter_context(nc.sbuf_tensor(name, [128, *shape], F32))

        sems = {}

        def sem(name):
            if name not in sems:
                sems[name] = ctx.enter_context(nc.semaphore(name))
            return sems[name]

        ring = sb("ring", RING, CHUNK)
        XT = sb("XT", KT, T)
        HN = sb("HN", KT, T)
        SQ = sb("SQ", 8 * TP)
        PAR = sb("PAR", NPAR)
        CST = sb("CST", NCONST)
        BIAS_C = sb("BIAS_C", HEADS, 256)
        BIAS_A = sb("BIAS_A", HEADS, 256)
        MIX = sb("MIX", KT, T)
        GATE = sb("GATE", KT, T)
        RS = sb("RS", TP)
        MU = sb("MU", TP)
        psum = ctx.enter_context(nc.psum_tensor("psum", [128, 8, 512], F32))

        used = [0]
        region = sb("region", (212000 - 4 * (RING * CHUNK + 4 * KT * T + 8 * TP + NPAR + NCONST + 16 * 256 + 2 * TP + 240 + 120 + 64)) // 4)

        def at_region(*shape):
            n = int(np.prod(shape))
            v = region[:, used[0] : used[0] + n]
            used[0] += n
            assert used[0] <= region.shape[1], (used[0], region.shape)
            if len(shape) == 2:
                return v.rearrange("p (a b) -> p a b", a=shape[0])
            if len(shape) == 3:
                return v.rearrange("p (a b c) -> p a b c", a=shape[0], b=shape[1])
            return v

        HC = at_region(4, T + CONV_K - 1)
        CO = at_region(4, T)
        HB = at_region(4, TP)
        HK = at_region(4, TP)
        HQ = at_region(4, TP)
        HG = at_region(4, T)
        HV = at_region(3, 512)
        HR = HV[:, :, :].rearrange("p a b -> p (a b)")[:, : 4 * T].rearrange("p (h t) -> p h t", h=4)
        CQ = at_region(2, T)
        CKV = at_region(T)
        MV = at_region(3, 512)
        KR = at_region(T)
        work = used[0]
        HKK = at_region(4, TP)
        HD = [at_region(1024 + 4 * 256) for _ in range(2)]
        HA = [at_region(TP + 96) for _ in range(2)]
        HAT = at_region(3, 4, TP)
        first = used[0]
        used[0] = work
        QH = at_region(HEADS, T)
        KH = at_region(HEADS, T)
        RSQ = at_region(HEADS, T)
        P2 = [at_region(3, T) for _ in range(2)]
        PT2 = [at_region(432) for _ in range(2)]
        first = max(first, used[0])
        used[0] = work
        F1 = at_region(FT, T)
        OT = CO
        HO = HB
        used[0] = 0
        YT = MIX[:, :, :256]
        AQ = at_region(KT, 256)
        AK = at_region(KT, 256)
        AV = at_region(2, 512)
        BV = at_region(2, 512)
        mixer = used[0]
        BIN = at_region(8, 259)
        BC = at_region(8, 256)
        SBO = at_region(4, 256)
        YAB = at_region(KT, 256)
        ROWS = at_region(8, 256)
        COLS = at_region(16)
        P = [at_region(2, 256) for _ in range(4)]
        PT = [at_region(384) for _ in range(4)]
        PC = [at_region(2, 16) for _ in range(2)]
        PCT = [at_region(256) for _ in range(2)]
        KC = at_region(30)
        VC = at_region(2, 128)
        CG = at_region(2, 24)
        BLK = ROWS[:, 0:4, :].rearrange("p a b -> p (a b)")[:, :960].rearrange("p (i n) -> p i n", i=32)
        CHID = BC
        used[0] = mixer
        GB = at_region(NEXP, 256)
        GATT = at_region(256)
        SGM = at_region(4, 256)
        HE = at_region(4, 256)
        SM = sb("SM", 240)
        RT = sb("RT", 120)
        ST = sb("ST", 64)

        def par(name, rows=128):
            at, n = PARAMS[name]
            return PAR[:rows, at : at + n]

        def cst(name, lo=0, n=None, rows=128):
            at, w = CONSTS[name]
            return CST[:rows, at + lo : at + lo + (w if n is None else n)]

        def ones(k, m):
            return cst("ones", 0, m, k)

        ident = lambda k: cst("ident", 0, k, k)
        HT = XT[:, :, N_META:T]

        banks = Banks(psum, [sem(f"bank_full{b}") for b in range(8)], [sem(f"bank_free{b}") for b in range(8)])
        arrived = [sem(f"weights_arrived{s}") for s in range(RING)]
        w_used = sem("weights_used")
        block = ctx.enter_context(nc.Block())
        SCHEDULE = schedule()

        @block.tensor
        def _(pe):
            state = {"n": 0, "held": False, "release": 0, "loop": None}

            def mm(dst, w, x, start=True, stop=True, done=None):
                ins = nc.tensor.matmul(dst, w, x, start=start, stop=stop, skip_group_check=True)
                if done is not None:
                    ins.then_inc(done, 1)
                elif state["release"]:
                    ins.then_inc(w_used, 1)
                    state["release"] -= 1

            def turn(dst, src, k, done=None):
                ins = nc.tensor.transpose(dst, src, ident(k))
                if done is not None:
                    ins.then_inc(done, 1)

            def chunk():
                n = state["n"]
                state["n"] += 1
                state["release"] += state["held"]
                state["held"] = True
                value = 16 * (n // RING + 1)
                pe.wait_ge(arrived[n % RING], value if state["loop"] is None else value + 16 * state["loop"])
                return ring[:, n % RING, :]

            def take(*key):
                return banks.take(pe, key), banks.filled(key)

            def project(key, x, n=T, chunks=1):
                dst, done = take(*key)
                for c in range(chunks):
                    w = chunk()
                    for k in range(KT):
                        last = c == chunks - 1 and k == KT - 1
                        mm(dst[:, :n], w[:, 128 * k : 128 * k + 128], x(8 * c + k), c + k == 0, last, done if last else None)

            def tokens(key, x, tiles):
                dsts = [take(*key, i) for i in range(len(tiles))]
                for c in range(4):
                    w = chunk()
                    for i, (lo, n) in enumerate(tiles):
                        for k in range(2):
                            last = c == 3 and k == 1
                            mm(dsts[i][0][:n, :], x(2 * c + k, lo, n), w[:, 512 * k : 512 * k + 512],
                               c + k == 0, last, dsts[i][1] if last else None)

            def half_projects(key, x, n):
                for c in range(4):
                    w = chunk()
                    for j in range(2):
                        dst, done = take(*key, 2 * c + j)
                        for k in range(4):
                            mm(dst[:, :n], w[:, 512 * j + 128 * k : 512 * j + 128 * k + 128], x(k), k == 0, k == 3, done if k == 3 else None)

            def column_sums(key, x, kt, n):
                dst, done = take(*key)
                for k in range(kt):
                    mm(dst[:, :n], ones(128, 128), x(k), k == 0, k == kt - 1, done if k == kt - 1 else None)

            sq = lambda k, n=T: SQ[:, n * k : n * k + n]
            hn = lambda k: HN[:, k, :]

            def start():
                pe.wait_ge(sem("loaded"), 48)
                dst, done = take("bucket_bias")
                mm(dst[:HEADS, :384], PAR[:BUCKETS, PARAMS["rel"][0] : PARAMS["rel"][0] + HEADS], cst("bucket", rows=BUCKETS), done=done)

            def bias():
                pe.wait_ge(sem("hankel"), 16)
                for g in range(4):
                    dst, done = take("bias", g)
                    mm(dst[:, :], cst("flip"), SQ[:, 512 * g : 512 * g + 512], done=done)

            def norm(r):
                pe.wait_ge(sem("norm_squares"), r + 1)
                column_sums(("norm", r), sq, KT, T)

            def conv_in(l):
                pe.wait_ge(sem("normed"), 2 * l + 1)
                for j in range(4):
                    project(("conv_a", l, j), hn)
                    project(("conv_g", l, j), hn)

            def hgrn_in(l):
                for name in ("hf", "hq", "hg"):
                    for j in range(4):
                        project((name, l, j), hn)
                tokens(("hi", l), lambda k, lo, n: HN[:, k, lo : lo + n], TOK1)

            def mla_in(l):
                for j in range(2):
                    project(("cq", l, j), hn)
                project(("ckv", l), hn)
                project(("rope", l), hn)

            def conv_norm(l):
                pe.wait_ge(sem("conv_out"), l + 1)
                column_sums(("conv_mean", l), lambda k: CO[:, k, :], 4, T)
                pe.wait_ge(sem("conv_squares"), l + 1)
                column_sums(("conv_var", l), sq, 4, T)

            def gate(l, b, m):
                project(("gate", l, b, m), hn)

            def branch_out(l, b):
                src, ready = ((CO, "conv_done"), (HO, "hgrn_done"), (OT, None))[b]
                if ready:
                    pe.wait_ge(sem(ready), l + 1)
                else:
                    for p in range(4):
                        banks.await_read(pe, ("pv", l, p))
                half_projects(("branch", l, b), lambda k: src[:, k, :T], T)

            def hgrn_block(l, i):
                pe.wait_ge(sem("decayed"), NB * l + i + 1)
                d = HD[i % 2]
                qq = d[:, 0:1024].rearrange("p (j h t) -> p j h t", j=8, h=4)
                dst, done = take("scores", l, i)
                for h in range(4):
                    row = dst[SB * h : SB * h + SB, :]
                    if i:
                        mm(row[:, : SB * i], qq[:, 0, h, :], d[:, 1024 + SB * i * h : 1024 + SB * i * (h + 1)])
                    for j in range(8):
                        lo = SB * i + SS * j
                        mm(row[:, lo : lo + SS], qq[:, j, h, :], HKK[:, h, lo : lo + SS], done=done if (h, j) == (3, 7) else None)

            def hgrn_turn(l, i):
                banks.await_read(pe, ("scores", l, i))
                dst, done = take("turned", l, i)
                n = -(-SB * (i + 1) // 128)
                for s in range(n):
                    turn(dst[:, 128 * s : 128 * s + 128], HA[i % 2][:, 128 * s : 128 * s + 128], 128, done if s == n - 1 else None)

            def hgrn_values(l):
                banks.await_read(pe, ("turned", l, NB - 1))
                banks.await_read(pe, ("hi", l, 2))
                for h in range(4):
                    dst, done = take("ho", l, h)
                    for s, (lo, k) in enumerate(TOK1):
                        mm(dst[:, lo:TP], HV[:k, s, 128 * h : 128 * h + 128], HAT[:k, s, h, lo:TP], s == 0, s == 2, done if s == 2 else None)

            def hgrn_norm(l):
                pe.wait_ge(sem("hgrn_squares"), l + 1)
                for h in range(4):
                    column_sums(("hgrn_var", l, h), lambda k: sq(h), 1, T)

            def mla_norm(l):
                pe.wait_ge(sem("latent_squares"), 2 * l + 1)
                column_sums(("cq_var", l), lambda k: sq(4 + k), 2, T)
                pe.wait_ge(sem("latent_squares"), 2 * l + 2)
                column_sums(("ckv_var", l), lambda k: sq(6), 1, T)

            def mla_up(l):
                pe.wait_ge(sem("latents"), 2 * l + 1)
                for g in range(2):
                    w = chunk()
                    for h in range(4):
                        dst, done = take("q", l, 4 * g + h)
                        for k in range(2):
                            mm(dst[:QK, :T], w[:, 192 * h + 96 * k : 192 * h + 96 * k + 96], CQ[:, k, :], k == 0, k == 1, done if k else None)
                pe.wait_ge(sem("latents"), 2 * l + 2)
                w = chunk()
                for h in range(HEADS):
                    dst, done = take("k", l, h)
                    mm(dst[:NOPE, :T], w[:, 64 * h : 64 * h + 64], CKV[:, :], done=done)
                for i, (lo, n) in enumerate(TOK1):
                    dst, done = take("v", l, i)
                    mm(dst[:n, :], CKV[:, lo : lo + n], w[:, 512:1024], done=done)

            def head_norm(l, which):
                pe.wait_ge(sem("head_squares"), 2 * l + which + 1)
                for h in range(HEADS):
                    dst, done = take("head_var", l, which, h)
                    mm(dst[:QK, :T], ones(QK, QK), SQ[:QK, T * h : T * h + T], done=done)

            def att_scores(l, h):
                if h == 0:
                    pe.wait_ge(sem("heads_ready"), 2 * l + 2)
                for i, (lo, n) in enumerate(TOK1):
                    dst, done = take("att", l, h, i)
                    mm(dst[:n, : lo + n], QH[:QK, h, lo : lo + n], KH[:QK, h, : lo + n], done=done)

            def att_turn(l, h):
                pe.wait_ge(sem("att_probs"), HEADS * l + h + 1)
                dst, done = take("att_turned", l, h)
                base = (0, T, T + T - 128)
                for i, (lo, n) in enumerate(TOK1):
                    for s in range(i + 1):
                        k = TOK1[s][1]
                        turn(dst[:k, base[s] + lo - 128 * s : base[s] + lo - 128 * s + n], P2[h % 2][:n, i, 128 * s : 128 * s + k], n,
                             done if (i, s) == (2, 2) else None)

            def att_values(l, p):
                dst, done = take("pv", l, p)
                for h in (2 * p, 2 * p + 1):
                    banks.await_read(pe, ("att_turned", l, h))
                    row = dst[64 * (h % 2) : 64 * (h % 2) + 64, :]
                    for s, (lo, k) in enumerate(TOK1):
                        b = (0, T, T + T - 128)[s]
                        mm(row[:, lo:T], MV[:k, s, 64 * h : 64 * h + 64], PT2[h % 2][:k, b : b + T - lo], s == 0, s == 2,
                           done if (h % 2, s) == (1, 2) else None)

            def mix_out(l):
                pe.wait_ge(sem("mixed"), KT * (l + 1))
                for m in range(KT):
                    project(("mix_out", l, m), lambda k: MIX[:, k, :])

            def ff1(l):
                pe.wait_ge(sem("normed"), 2 * l + 2)
                for m in range(FT):
                    project(("ff1", l, m), hn)

            def ff2(l):
                pe.wait_ge(sem("squared"), FT * (l + 1))
                for m in range(KT):
                    project(("ff2", l, m), lambda k: F1[:, k, :], chunks=4)

            ht = lambda k: HT[:, k, :]
            ht_tok = lambda k, lo, n: HT[:, k, lo : lo + n]
            TOK2 = [(0, 128), (128, 128)]

            def ab_in():
                banks.await_read(pe, ("ff2", DEPTH - 1, KT - 1))
                for name in ("aq", "ak"):
                    for j in range(4):
                        project((name, j), ht, 256)
                tokens(("av",), ht_tok, TOK2)

            def ab_in2():
                for j in range(8):
                    project(("bqk", j), ht, 256)
                tokens(("bv",), ht_tok, TOK2)
                for j in range(4):
                    project(("bo", j), ht, 256)
                at = PARAMS["wif"][0]
                for g in range(2):
                    dst, done = take("if", g)
                    for k in range(KT):
                        mm(dst[:4, :256], PAR[:, at + 8 * k + 4 * g : at + 8 * k + 4 * g + 4], ht(k), k == 0, k == 7, done if k == 7 else None)

            def gate_rows():
                pe.wait_ge(sem("gate_rows"), 1)
                dst, done = take("gate_cols")
                for i in range(2):
                    for a in range(2):
                        turn(dst[:, 8 * i + 4 * a : 8 * i + 4 * a + 4], ROWS[:4, 1 + a, 128 * i : 128 * i + 128], 4,
                             done if (i, a) == (1, 1) else None)

            def a_scores(h):
                if h == 0:
                    banks.await_read(pe, ("aq", 3))
                    banks.await_read(pe, ("ak", 3))
                rows = slice(64 * (h % 2), 64 * (h % 2) + 64)
                for i in range(2):
                    dst, done = take("a", h, i)
                    mm(dst[:, : 128 * i + 128], AQ[rows, h // 2, 128 * i : 128 * i + 128], AK[rows, h // 2, : 128 * i + 128], done=done)

            def turn_probs(key, ready, count, p):
                pe.wait_ge(sem(ready), count)
                dst, done = take(*key)
                for i, s, b in ((0, 0, 0), (1, 0, 128), (1, 1, 256)):
                    turn(dst[:, b : b + 128], p[:, i, 128 * s : 128 * s + 128], 128, done if s else None)

            def a_turn(h):
                turn_probs(("a_turned", h), "a_probs", h + 1, P[h % 2])

            def a_values(p):
                dst, done = take("a_pv", p)
                for h in (2 * p, 2 * p + 1):
                    banks.await_read(pe, ("a_turned", h))
                    row = dst[64 * (h % 2) : 64 * (h % 2) + 64, :]
                    mm(row[:, 0:256], AV[:, 0, 64 * h : 64 * h + 64], PT[h % 2][:, 0:256], True, False)
                    mm(row[:, 128:256], AV[:, 1, 64 * h : 64 * h + 64], PT[h % 2][:, 256:384], False, True, done if h % 2 else None)

            def b_scores(h):
                if h == 0:
                    pe.wait_ge(sem("bqk_ready"), 1)
                for i in range(2):
                    dst, done = take("b_row", h, i)
                    mm(dst[:, :256], ident(4)[:, h : h + 1].to_broadcast([4, 128]), ROWS[:4, 0, :], done=done)
                    dst, done = take("b", h, i)
                    mm(dst[:, : 128 * i + 128], BC[:, h, 128 * i : 128 * i + 128], BC[:, 4 + h, : 128 * i + 128], done=done)

            def b_turn(h):
                turn_probs(("b_turned", h), "b_weights", h + 1, P[2 + h % 2])

            def b_values(h):
                banks.await_read(pe, ("b_turned", h))
                dst, done = take("b_pv", h)
                mm(dst[:, 0:256], BV[:, 0, 128 * h : 128 * h + 128], PT[2 + h % 2][:, 0:256], True, False)
                mm(dst[:, 128:256], BV[:, 1, 128 * h : 128 * h + 128], PT[2 + h % 2][:, 256:384], False, True, done)

            def b_norm():
                for h in range(4):
                    banks.await_read(pe, ("b_pv", h))
                for g in range(2):
                    dst, done = take("b_mean", g)
                    mm(dst[:, :], ones(128, 128), YAB[:, 4 + 2 * g : 6 + 2 * g, :], done=done)
                pe.wait_ge(sem("b_squares"), 1)
                for g in range(2):
                    dst, done = take("b_var", g)
                    mm(dst[:, :], ones(128, 128), SQ[:, 512 * g : 512 * g + 512], done=done)

            def y_out(l):
                if l == 0:
                    pe.wait_ge(sem("y_ready"), 1)
                    banks.await_read(pe, ("a_pv", 3))
                else:
                    banks.await_read(pe, ("c_pv", HEADS - 1))
                for m in range(KT):
                    project(("y_out", l, m), lambda k: YAB[:, k, :], 256)

            def layer_norm(r):
                if r % 2:
                    pe.wait_ge(sem("moe_done"), r // 2 + 1)
                else:
                    banks.await_read(pe, ("y_out", r // 2, KT - 1))
                column_sums(("ln_mean", r), ht, KT, 256)
                pe.wait_ge(sem("ln_squares"), r + 1)
                column_sums(("ln_var", r), lambda k: sq(k, 256), KT, 256)

            def router(l):
                pe.wait_ge(sem("ln_done"), KT * (2 * l + 1))
                at = PARAMS[f"router{l}"][0]
                for i in range(2):
                    dst, done = take("router", l, i)
                    mm(dst[:, :20], ones(1, 128), par(f"rbias{l}", 1), True, False)
                    for k in range(KT):
                        mm(dst[:, :20], ht_tok(k, 128 * i, 128), PAR[:, at + 20 * k : at + 20 * k + 20], False, k == 7, done if k == 7 else None)

            def expert_gates(l):
                pe.wait_ge(sem("expert_gates"), 2 * l + 2)
                dst, done = take("gates_turned", l)
                for i in range(2):
                    turn(dst[:16, 128 * i : 128 * i + 128], SM[:, 200 + 16 * i : 216 + 16 * i], 128, done if i else None)
                banks.await_read(pe, ("gates_turned", l))
                for e in range(NEXP):
                    dst, done = take("gate_row", l, e)
                    mm(dst[:, :256], ident(16)[:, e : e + 1].to_broadcast([16, 128]), GATT[:16, :], done=done)

            def moe(l):
                with pe.Fori(0, NEXP) as e:
                    state["loop"], banks.loop = e, 2 * e
                    for j in range(4):
                        project(("moe_gate", l, j), ht, 256)
                        project(("moe_up", l, j), ht, 256)
                    pe.wait_ge(sem("hidden"), (4 * NEXP + 4) * l + 8 + 4 * e)
                    half_projects(("moe_down", l), lambda k: HE[:, k, :], 256)
                state["loop"] = banks.loop = None
                state["n"] += RING * (NEXP - 1)
                banks.uses = [n + 2 * (NEXP - 1) for n in banks.uses]

            def c_in():
                pe.wait_ge(sem("ln_done"), KT * 2)
                for j in range(4):
                    project(("c_src", j), ht, 256)
                for j in range(8):
                    project(("c_q", j), ht, 256)
                for j in range(4):
                    project(("c_k", j), ht, 256)
                tokens(("c_v",), ht_tok, TOK2)
                at = PARAMS["wcg"][0]
                for i in range(2):
                    dst, done = take("c_gate", i)
                    mm(dst[:, :24], ones(1, 128), par("cgbias", 1), True, False)
                    for k in range(KT):
                        mm(dst[:, :24], ht_tok(k, 128 * i, 128), PAR[:, at + 24 * k : at + 24 * k + 24], False, k == 7, done if k == 7 else None)

            def compress(s):
                pe.wait_ge(sem("blocks"), s + 1)
                dst, done = take("c_hidden", s)
                for c in range(8):
                    w = chunk()
                    for j in range(4):
                        n = 4 * c + j
                        mm(dst[:30, :256], BLK[:, n, :], w[:, 256 * j : 256 * j + 256], n == 0, n == 31, done if n == 31 else None)

            def compress2():
                w = chunk()
                for s in range(2):
                    pe.wait_ge(sem("c_gelu"), s + 1)
                    dst, done = take("c_hidden_turned", s)
                    for j in range(2):
                        turn(dst[:, 32 * j : 32 * j + 30], CHID[:30, 2 * s, 128 * j : 128 * j + 128], 30, done if j else None)
                    banks.await_read(pe, ("c_hidden_turned", s))
                    hid = CHID[:, 2 * s + 1, :]
                    for g in range(1 + s):
                        dst, done = take("c_cmp", s, g)
                        for j in range(2):
                            wt = w[:, 256 * s + 128 * j : 256 * s + 128 * j + 128]
                            if s == 0:
                                mm(dst[:, :30], wt, hid[:, 32 * j : 32 * j + 30], j == 0, j == 1, done if j else None)
                            else:
                                mm(dst[:15, :128], hid[:, 32 * j + 15 * g : 32 * j + 15 * g + 15], wt, j == 0, j == 1, done if j else None)

            def c_scores(h):
                g = h // 4
                if h == 0:
                    for key in (("c_q", 7), ("c_k", 3), ("c_cmp", 0, 0), ("c_cmp", 1, 1)):
                        banks.await_read(pe, key)
                for i in range(2):
                    q = AQ[:, h, 128 * i : 128 * i + 128]
                    for b in range(2):
                        dst, done = take("c", h, i, b)
                        mm(dst[:, : 128 * i + 128], q, AK[:, 2 * b + g, : 128 * i + 128], done=done)
                dst, done = take("c_c", h)
                for i in range(2):
                    mm(dst[:, 16 * i : 16 * i + 15], AQ[:, h, 128 * i : 128 * i + 128], KC[:, 15 * g : 15 * g + 15], done=done if i else None)

            def c_turn(h):
                for b in range(2):
                    turn_probs(("c_turned", h, b), "c_probs", 3 * h + b + 1, P[2 * (h % 2) + b])
                pe.wait_ge(sem("c_probs"), 3 * h + 3)
                dst, done = take("c_turned", h, 2)
                for i in range(2):
                    turn(dst[:15, 128 * i : 128 * i + 128], PC[h % 2][:, i, :15], 128, done if i else None)

            def c_values(h):
                g = h // 4
                dst, done = take("c_pv", h)
                for b in range(2):
                    banks.await_read(pe, ("c_turned", h, b))
                    v = 256 * b + 128 * g
                    mm(dst[:, 0:256], AV[:, 0, v : v + 128], PT[2 * (h % 2) + b][:, 0:256], b == 0, False)
                    mm(dst[:, 128:256], AV[:, 1, v : v + 128], PT[2 * (h % 2) + b][:, 256:384], False, False)
                banks.await_read(pe, ("c_turned", h, 2))
                mm(dst[:, 0:256], VC[:15, g, :], PCT[h % 2][:15, :], False, True, done)

            steps = locals()
            for name, *args in SCHEDULE:
                if name in steps:
                    steps[name](*args)
            assert state["n"] == n_chunks, (state["n"], n_chunks)

        def bc(ap, shape):
            return ap.to_broadcast(shape)

        SCALE_MLA = QK ** -0.5

        @block.scalar
        def _(act):
            lane = Lane(act, sem("scalar_step"))
            loop = {"v": None}

            def fn(dst, src, f, sem_=None, **kw):
                lane(nc.scalar.activation(dst, src, f, **kw), sem_)

            def fn_free(dst, src, f, key, **kw):
                nc.scalar.activation(dst, src, f, **kw).then_inc(banks.freed(key), 1)
                banks.await_read(act, key, loop["v"])

            def wait_bank(*key):
                return banks.await_(act, key, loop["v"])

            def evacuate(key, dst, n=T, f=ACT.Copy, rows=128, **kw):
                fn_free(dst, wait_bank(*key)[:rows, :n], f, key, **kw)

            def root(ap):
                fn(ap, ap, ACT.Sqrt, sem("root"))

            def start():
                act.wait_ge(sem("lower_bound_args"), 1)
                fn(ST[:, 8:16], ST[:, 8:16], ACT.Exp, sem("lower_bound_exps"))

            def bias():
                banks.await_read(act, ("bucket_bias",))
                act.dma_start(scratch, MIX[:HEADS, 0:2, :].rearrange("p a b -> p (a b)")[:, :384]).then_inc(sem("bias_stored"), 16)
                act.wait_ge(sem("bias_stored"), 16)
                hankel = bass.AP(scratch.tensor, 0, [[1, 128], [384, HEADS], [1, 256]])
                act.dma_start(SQ[:, : 8 * 256].rearrange("p (h c) -> p h c", h=8), hankel).then_inc(sem("hankel"), 16)

            def norm(r):
                if r == 0:
                    act.wait_ge(sem("loaded"), 48)
                    wait_bank("bias", 3)
                elif r % 2:
                    banks.await_read(act, ("mix_out", r // 2, KT - 1))
                else:
                    banks.await_read(act, ("ff2", r // 2 - 1, KT - 1))
                fn(SQ[:, : KT * T], XT[:, :, :].rearrange("p k t -> p (k t)"), ACT.Square, sem("norm_squares"))
                banks.await_read(act, ("norm", r))
                root(RS[:, :T])

            def conv_in(l):
                for j in range(4):
                    evacuate(("conv_g", l, j), MIX[:, j, :], f=ACT.Sigmoid)

            def hgrn_in(l):
                for j in range(4):
                    evacuate(("hf", l, j), HK[:, j, :T], f=ACT.Sigmoid, scale=-1.0)
                for j in range(4):
                    evacuate(("hq", l, j), HQ[:, j, :T])
                for j in range(4):
                    evacuate(("hg", l, j), HG[:, j, :], f=ACT.Silu)
                for i, (_, n) in enumerate(TOK1):
                    evacuate(("hi", l, i), HV[:n, i, :], 512, ACT.Silu, n)

            def mla_in(l):
                for j in range(2):
                    src = wait_bank("cq", l, j)
                    fn(SQ[:, T * (4 + j) : T * (5 + j)], src[:, :T], ACT.Square, sem("latent_squares") if j else None)
                    fn_free(CQ[:, j, :], src[:, :T], ACT.Copy, ("cq", l, j))
                src = wait_bank("ckv", l)
                fn(SQ[:, T * 6 : T * 7], src[:, :T], ACT.Square, sem("latent_squares"))
                fn_free(CKV[:, :], src[:, :T], ACT.Copy, ("ckv", l))
                fn_free(KR[NOPE:QK, :], wait_bank("rope", l)[NOPE:QK, :T], ACT.Copy, ("rope", l))

            def gate(l, b, m):
                if b == 0 and l:
                    act.wait_ge(sem("mixed"), KT * (l - 1) + m + 1)
                elif b == 1:
                    banks.await_read(act, ("branch", l, 0, m))
                elif b == 2:
                    act.wait_ge(sem("gated"), KT * l + m + 1)
                evacuate(("gate", l, b, m), GATE[:, m, :], f=ACT.Sigmoid)

            def conv_norm(l):
                act.wait_ge(sem("conv_centered"), l + 1)
                fn(SQ[:, : 4 * T], CO[:, :, :].rearrange("p k t -> p (k t)"), ACT.Square, sem("conv_squares"))
                banks.await_read(act, ("conv_var", l))
                root(RS[:, :T])
                act.wait_ge(sem("conv_scaled"), l + 1)
                for j in range(4):
                    fn(CO[:, j, :], CO[:, j, :], ACT.Silu, sem("conv_done") if j == 3 else None,
                       scale=par(f"clng{l}")[:, j : j + 1], bias=par(f"clnb{l}")[:, j : j + 1])

            def hgrn_prep(l):
                act.wait_ge(sem("clamped"), l + 1)
                fn(HB[:, :, :T], HB[:, :, :T], ACT.Ln, sem("logs"), scale=-1.0, bias=1.0)
                act.wait_ge(sem("strip_args"), l + 1)
                fn(HKK[:, :, :], HKK[:, :, :], ACT.Exp, sem("strip_exps"))

            def hgrn_args(l, i):
                act.wait_ge(sem("decay_args"), NB * l + i + 1)
                n = 1024 + 4 * SB * i
                fn(HD[i % 2][:, :n], HD[i % 2][:, :n], ACT.Exp, sem("decay_exps"))

            def hgrn_turn(l, i):
                n = -(-SB * (i + 1) // 128)
                src = wait_bank("turned", l, i)[:, : 128 * n].rearrange("p (s h t) -> p s h t", s=n, h=4)
                fn_free(HAT[:, :n, :, SB * i : SB * i + SB], src, ACT.Copy, ("turned", l, i))

            def hgrn_values(l):
                for h in range(4):
                    evacuate(("ho", l, h), HO[:, h, :T])
                fn(SQ[:, : 4 * T].rearrange("p (h t) -> p h t", h=4), HO[:, :, :T], ACT.Square, sem("hgrn_squares"))

            def hgrn_norm(l):
                banks.await_read(act, ("hgrn_var", l, 3))
                root(HR)

            def mla_norm(l):
                for key in ("cq_var", "ckv_var"):
                    banks.await_read(act, (key, l))
                    root(RS[:, :T])

            def mla_up(l):
                for h in range(HEADS):
                    evacuate(("q", l, h), QH[:QK, h, :], rows=QK)
                fn(KH[NOPE:QK, :, :], bc(KR[NOPE:QK, None, :], [ROPE, HEADS, T]), ACT.Copy)
                for h in range(HEADS):
                    evacuate(("k", l, h), KH[:NOPE, h, :], rows=NOPE)
                for i, (_, n) in enumerate(TOK1):
                    evacuate(("v", l, i), MV[:n, i, :], 512, rows=n)

            def head_norm(l, which):
                src = (QH, KH)[which][:QK, :, :].rearrange("p h t -> p (h t)")
                if which:
                    wait_bank("head_var", l, 0, HEADS - 1)
                fn(SQ[:QK, : HEADS * T], src, ACT.Square, sem("head_squares"))
                banks.await_read(act, ("head_var", l, which, HEADS - 1))
                root(RSQ[:QK, :, :])

            def att_scores(l, h):
                act.wait_ge(sem("att_max"), HEADS * l + h + 1)
                s = 16 * (h % 2)
                for i, (lo, n) in enumerate(TOK1):
                    p = P2[h % 2][:n, i, : lo + n]
                    fn(p, p, ACT.Exp, sem("att_exps"), scale=SCALE_MLA, bias=SM[:n, s + 4 + i : s + 5 + i], accum_out=SM[:n, s + 8 + i : s + 9 + i])

            def att_turn(l, h):
                src = wait_bank("att_turned", l, h)
                if h >= 2:
                    wait_bank("pv", l, h // 2 - 1)
                n = T + T - 128
                fn(PT2[h % 2][:, :n], src[:, :n], ACT.Copy)
                fn_free(PT2[h % 2][:16, n : n + 16], src[:16, n : n + 16], ACT.Copy, ("att_turned", l, h))

            def att_values(l, p):
                evacuate(("pv", l, p), OT[:, p, :])

            def ff1(l):
                for m in range(FT):
                    evacuate(("ff1", l, m), F1[:, m, :], f=ACT.Relu)

            def ab_in():
                for j in range(4):
                    evacuate(("aq", j), AQ[:, j, :], 256, scale=A_SCALE)
                for j in range(4):
                    evacuate(("ak", j), AK[:, j, :], 256)
                for i in range(2):
                    evacuate(("av", i), AV[:, i, :], 512)

            def ab_in2():
                for j in range(8):
                    evacuate(("bqk", j), BIN[:, j, 3:259], 256)
                for i in range(2):
                    evacuate(("bv", i), BV[:, i, :], 512)
                for j in range(4):
                    evacuate(("bo", j), SBO[:, j, :], 256, ACT.Sigmoid)

            def b_gates():
                act.wait_ge(sem("forget_abs"), 1)
                fn(ROWS[:4, 5, :], ROWS[:4, 5, :], ACT.Exp, scale=-1.0)
                fn(ROWS[:4, 5, :], ROWS[:4, 5, :], ACT.Ln, sem("forget_logs"), bias=1.0)

            def gate_rows():
                banks.await_read(act, ("gate_cols",))
                floors = COLS[:, :].rearrange("p (i c) -> p i c", i=2)[:, :, 4:8]
                fn(floors, floors, ACT.Exp, sem("floors"))

            def b_conv():
                act.wait_ge(sem("b_convolved"), 1)
                fn(BC[:, :, :], BC[:, :, :], ACT.Silu, sem("b_silu"))

            def a_scores(h):
                act.wait_ge(sem("a_max"), h + 1)
                s = 32 + 16 * (h % 2)
                for i in range(2):
                    p = P[h % 2][:, i, : 128 * i + 128]
                    fn(p, p, ACT.Exp, sem("a_exps"), bias=SM[:, s + 4 + i : s + 5 + i], accum_out=SM[:, s + 8 + i : s + 9 + i])

            def turned(key, dst, before):
                src = wait_bank(*key)
                if before is not None:
                    wait_bank(*before)
                fn_free(dst[:, :384], src[:, :384], ACT.Copy, key)

            def a_turn(h):
                turned(("a_turned", h), PT[h % 2], ("a_pv", h // 2 - 1) if h >= 2 else None)

            def a_values(p):
                evacuate(("a_pv", p), YAB[:, p, :], 256)

            def b_scores(h):
                if h == 0:
                    act.wait_ge(sem("floors"), 1)
                for i in range(2):
                    act.wait_ge(sem("b_masked"), 2 * h + i + 1)
                    p = P[2 + h % 2][:, i, : 128 * i + 128]
                    fn(p, p, ACT.Exp, sem("b_exps"), bias=COLS[:, 8 * i + h : 8 * i + h + 1])

            def b_turn(h):
                turned(("b_turned", h), PT[2 + h % 2], ("b_pv", h - 2) if h >= 2 else None)

            def b_values(h):
                evacuate(("b_pv", h), YAB[:, 4 + h, :], 256)

            def b_norm():
                act.wait_ge(sem("b_centered"), 1)
                fn(SQ[:, :1024], YAB[:, 4:8, :].rearrange("p h t -> p (h t)"), ACT.Square, sem("b_squares"))
                banks.await_read(act, ("b_var", 1))
                root(AQ[:, 0:4, :])

            def layer_norm(r):
                act.wait_ge(sem("ln_centered"), r + 1)
                fn(SQ[:, :2048].rearrange("p (k t) -> p k t", k=KT), HT, ACT.Square, sem("ln_squares"))
                banks.await_read(act, ("ln_var", r))
                root(RS[:, :256])
                act.wait_ge(sem("ln_scaled"), r + 1)
                l, j = r // 2, r % 2
                for k in range(KT):
                    fn(HT[:, k, :], HT[:, k, :], ACT.Identity, sem("ln_done"),
                       scale=par(f"lng{j}_{l}")[:, k : k + 1], bias=par(f"lnb{j}_{l}")[:, k : k + 1])

            def router(l):
                for i in range(2):
                    act.wait_ge(sem("group_max"), l + 1)
                    s = RT[:, 56 + 4 * i : 60 + 4 * i]
                    fn(s, RT[:, 20 * i : 20 * i + 4], ACT.Exp, sem("group_exps"), bias=RT[:, 42 + i : 43 + i], accum_out=RT[:, 44 + i : 45 + i])
                act.wait_ge(sem("top_gap"), l + 1)
                fn(RT[:, 46:48], RT[:, 46:48], ACT.Exp, sem("top_exps"))

            def expert_gates(l):
                evacuate(("gates_turned", l), GATT[:16, :], 256, rows=16)
                for e in range(NEXP):
                    evacuate(("gate_row", l, e), GB[:, e, :], 256)

            def moe(l):
                with act.Fori(0, NEXP) as e:
                    loop["v"] = 2 * e
                    for j in range(4):
                        act.wait_ge(sem("hidden"), (4 * NEXP + 4) * l + j + 1 + 4 * e)
                        evacuate(("moe_gate", l, j), SGM[:, j, :], 256, ACT.Silu)
                loop["v"] = None

            def c_in():
                for j in range(4):
                    evacuate(("c_src", j), BIN[:, j, :256], 256)
                for j in range(8):
                    evacuate(("c_q", j), AQ[:, j, :], 256, scale=C_SCALE)
                for j in range(4):
                    evacuate(("c_k", j), AK[:, j, :], 256)
                for i in range(2):
                    evacuate(("c_v", i), AV[:, i, :], 512)
                for i in range(2):
                    evacuate(("c_gate", i), CG[:, i, :], 24, ACT.Sigmoid)

            def compress(s):
                src = wait_bank("c_hidden", s)
                fn(CHID[:30, 2 * s, :], src[:30, :256], ACT.Gelu_apprx_tanh, sem("c_gelu"))

            def compress2():
                for s in range(2):
                    src = wait_bank("c_hidden_turned", s)[:, :64].rearrange("p (j n) -> p j n", j=2)[:, :, :30]
                    fn_free(CHID[:, 2 * s + 1, :64].rearrange("p (j n) -> p j n", j=2)[:, :, :30], src, ACT.Copy, ("c_hidden_turned", s))
                    for g in range(1 + s):
                        if s == 0:
                            evacuate(("c_cmp", s, g), KC[:, :], 30)
                        else:
                            evacuate(("c_cmp", s, g), VC[:15, g, :], 128, rows=15)

            def c_scores(h):
                act.wait_ge(sem("c_max"), h + 1)
                s = 64 + 20 * (h % 2)
                for b in range(3):
                    for i in range(2):
                        p = PC[h % 2][:, i, : 7 + 8 * i] if b == 0 else P[2 * (h % 2) + b - 1][:, i, : 128 * i + 128]
                        c = 2 * b + i
                        fn(p, p, ACT.Exp, sem("c_exps"), bias=SM[:, s + 6 + c : s + 7 + c], accum_out=SM[:, s + 12 + c : s + 13 + c])

            def c_turn(h):
                before = ("c_pv", h - 2) if h >= 2 else None
                for b in range(2):
                    turned(("c_turned", h, b), PT[2 * (h % 2) + b], before)
                evacuate(("c_turned", h, 2), PCT[h % 2][:15, :], 256, rows=15)

            def c_values(h):
                evacuate(("c_pv", h), YAB[:, h, :], 256)

            steps = locals()
            for name, *args in SCHEDULE:
                if name in steps:
                    steps[name](*args)

        @block.vector
        def _(dve):
            lane = Lane(dve, sem("vector_step"))
            loop = {"v": None}
            roots = [0]

            def tt(dst, a, b, op, done=None):
                lane(nc.vector.tensor_tensor(dst, a, b, op), done)

            def ts(dst, a, s1, s2, op0, op1=None, done=None):
                ins = nc.vector.tensor_scalar(dst, a, s1, s2, op0) if op1 is None else nc.vector.tensor_scalar(dst, a, s1, s2, op0, op1)
                lane(ins, done)

            def stt(dst, a, s, b, op0, op1, done=None):
                lane(nc.vector.scalar_tensor_tensor(dst, a, s, b, op0, op1), done)

            def ttr(dst, a, b, op0, op1, init, acc, done=None):
                lane(nc.vector.tensor_tensor_reduce(dst, a, b, 1.0, init, op0, op1, acc), done)

            def wait_bank(*key):
                return banks.await_(dve, key, loop["v"])

            def free(ins, *key):
                ins.then_inc(banks.freed(key), 1)
                banks.await_read(dve, key, loop["v"])

            def mean_eps(key, dst, n, count, eps, rows=128):
                src = wait_bank(*key)
                free(nc.vector.tensor_scalar(dst, src[:rows, :n], 1.0 / count, eps, ALU.mult, ALU.add), *key)

            def reciprocal_root(ap):
                roots[0] += 1
                dve.wait_ge(sem("root"), roots[0])
                lane(nc.vector.reciprocal(ap, ap))

            def start():
                lane(nc.vector.memset(HC[:, :, : CONV_K - 1], 0.0))
                for t in (HB, HK, HQ):
                    lane(nc.vector.memset(t[:, :, T:TP], 0.0))
                lane(nc.vector.memset(SM[:, :], 0.0))
                dve.wait_ge(sem("loaded"), 48)
                l0, l1 = par("lb0"), par("lb1")
                tt(ST[:, 16:20], l0, l1, ALU.max)
                tt(ST[:, 8:12], l0, ST[:, 16:20], ALU.subtract)
                tt(ST[:, 12:16], l1, ST[:, 16:20], ALU.subtract, sem("lower_bound_args"))
                dve.wait_ge(sem("lower_bound_exps"), 1)
                tt(ST[:, 16:20], ST[:, 8:12], ST[:, 12:16], ALU.add)
                lane(nc.vector.reciprocal(ST[:, 16:20], ST[:, 16:20]))
                tt(ST[:, 8:12], ST[:, 8:12], ST[:, 16:20], ALU.mult)
                tt(ST[:, 12:16], ST[:, 12:16], ST[:, 16:20], ALU.mult)
                tt(ST[:, 12:16], ST[:, 8:12], ST[:, 12:16], ALU.add)
                tt(ST[:, 20:24], ST[:, 8:12], ST[:, 8:12], ALU.subtract)
                tt(ST[:, 24:28], ST[:, 12:16], ST[:, 8:12], ALU.subtract)
                ts(ST[:, 0:8], ST[:, 20:28], -1.0, 1.0, ALU.mult, ALU.add)
                src = wait_bank("bucket_bias")
                flat = MIX[:HEADS, 0:2, :].rearrange("p a b -> p (a b)")[:, :384]
                free(nc.vector.tensor_copy(flat, src[:HEADS, :384]), "bucket_bias")

            def bias():
                for g in range(4):
                    src = wait_bank("bias", g)[:, :].rearrange("p (h c) -> p h c", h=2)
                    mask = bc(cst("causal", 128, 256)[:, None, :], [128, 2, 256])
                    count = bc(cst("logcount")[:, None, :], [128, 2, 256])
                    tt(BIAS_C[:, 2 * g : 2 * g + 2, :], src, mask, ALU.add)
                    free(nc.vector.tensor_tensor(BIAS_A[:, 2 * g : 2 * g + 2, :], src, count, ALU.add), "bias", g)

            def norm(r):
                mean_eps(("norm", r), RS[:, :T], T, D, EPS)
                reciprocal_root(RS[:, :T])
                g = par(f"norm{1 + r % 2}{r // 2}")
                for k in range(KT):
                    stt(HN[:, k, :], XT[:, k, :], g[:, k : k + 1], RS[:, :T], ALU.mult, ALU.mult, sem("normed") if k == KT - 1 else None)

            def conv_in(l):
                for j in range(4):
                    src = wait_bank("conv_a", l, j)
                    banks.await_read(dve, ("conv_g", l, j))
                    free(nc.vector.tensor_tensor(HC[:, j, CONV_K - 1 :], src[:, :T], MIX[:, j, :], ALU.mult), "conv_a", l, j)

            def conv_taps(l):
                w, b = par(f"convw{l}"), par(f"convb{l}")
                for j in range(4):
                    for i in range(CONV_K):
                        x, wi = HC[:, j, i : i + T], w[:, CONV_K * j + i : CONV_K * j + i + 1]
                        if i == 0:
                            ts(CO[:, j, :], x, wi, b[:, j : j + 1], ALU.mult, ALU.add)
                        else:
                            stt(CO[:, j, :], x, wi, CO[:, j, :], ALU.mult, ALU.add, sem("conv_out") if (i, j) == (CONV_K - 1, 3) else None)

            def conv_norm(l):
                mean_eps(("conv_mean", l), MU[:, :T], T, 512, 0.0)
                tt(CO[:, :, :], CO[:, :, :], bc(MU[:, None, :T], [128, 4, T]), ALU.subtract, sem("conv_centered"))
                mean_eps(("conv_var", l), RS[:, :T], T, 512, EPS)
                reciprocal_root(RS[:, :T])
                tt(CO[:, :, :], CO[:, :, :], bc(RS[:, None, :T], [128, 4, T]), ALU.mult, sem("conv_scaled"))

            def branch_out(l, b):
                for m in range(KT):
                    src = wait_bank("branch", l, b, m)
                    banks.await_read(dve, ("gate", l, b, m))
                    dst = GATE if b else MIX
                    free(nc.vector.tensor_tensor(dst[:, m, :], src[:, :T], GATE[:, m, :], ALU.mult), "branch", l, b, m)
                    if b:
                        tt(MIX[:, m, :], MIX[:, m, :], GATE[:, m, :], ALU.add, sem(("gated", "mixed")[b - 1]))

            def hgrn_prep(l):
                for j in range(4):
                    banks.await_read(dve, ("hf", l, j))
                    ts(HK[:, j, :T], HK[:, j, :T], ST[:, 4 * l + j : 4 * l + j + 1], None, ALU.mult)
                ts(HB[:, :, :T], HK[:, :, :T], CLAMP, None, ALU.min, done=sem("clamped"))
                for a in HA:
                    lane(nc.vector.memset(a, 0.0))
                if l:
                    lane(nc.vector.memset(HB[:, :, T:TP], 0.0))
                dve.wait_ge(sem("logs"), l + 1)
                one = bc(cst("ones", 0, 1), [128, TP])
                for j in range(4):
                    lane(nc.vector.tensor_tensor_scan(HB[:, j, :], one, HB[:, j, :], 0.0, ALU.mult, ALU.add), sem("summed") if j == 3 else None)
                s4 = HB[:, :, :].rearrange("p h (g f) -> p (h g) f", f=SS)
                k4 = HKK[:, :, :].rearrange("p h (g f) -> p (h g) f", f=SS)
                tt(k4, bc(s4[:, :, 0:1], [128, 4 * TP // SS, SS]), s4, ALU.subtract, sem("strip_args"))
                dve.wait_ge(sem("strip_exps"), l + 1)
                tt(HKK[:, :, :], HKK[:, :, :], HK[:, :, :], ALU.mult)
                banks.await_read(dve, ("hq", l, 3))

            def hgrn_args(l, i):
                dve.wait_ge(sem("decay_exps"), NB * l + i + 1)
                d = HD[i % 2]
                qq = d[:, :1024].rearrange("p (j h t) -> p j h t", j=8, h=4)
                q = bc(HQ[:, None, :, SB * i : SB * i + SB], [128, 8, 4, SB])
                tt(qq, qq, q, ALU.mult, None if i else sem("decayed"))
                if i:
                    n = SB * i
                    kk = d[:, 1024 : 1024 + 4 * n].rearrange("p (h s) -> p h s", h=4)
                    tt(kk, kk, HK[:, :, :n], ALU.mult, sem("decayed"))

            def hgrn_block(l, i):
                src = wait_bank("scores", l, i)
                if i >= 2:
                    wait_bank("turned", l, i - 2)
                n = SB * i
                if i:
                    lane(nc.vector.tensor_copy(HA[i % 2][:, :n], src[:, :n]))
                free(nc.vector.tensor_tensor(HA[i % 2][:, n : n + SB], src[:, n : n + SB], cst("tri"), ALU.mult), "scores", l, i)

            def hgrn_norm(l):
                for h in range(4):
                    mean_eps(("hgrn_var", l, h), HR[:, h, :], T, 128, EPS)
                reciprocal_root(HR)
                tt(HO[:, :, :T], HO[:, :, :T], HR, ALU.mult)
                for h in range(4):
                    stt(HO[:, h, :T], HO[:, h, :T], par(f"hn{l}")[:, h : h + 1], HG[:, h, :], ALU.mult, ALU.mult, sem("hgrn_done") if h == 3 else None)

            def mla_norm(l):
                mean_eps(("cq_var", l), RS[:, :T], T, 256, EPS)
                reciprocal_root(RS[:, :T])
                for k in range(2):
                    stt(CQ[:, k, :], CQ[:, k, :], par(f"qa{l}")[:, k : k + 1], RS[:, :T], ALU.mult, ALU.mult, sem("latents") if k else None)
                mean_eps(("ckv_var", l), RS[:, :T], T, 128, EPS)
                reciprocal_root(RS[:, :T])
                stt(CKV[:, :], CKV[:, :], par(f"kva{l}"), RS[:, :T], ALU.mult, ALU.mult, sem("latents"))

            def head_norm(l, which):
                x = (QH, KH)[which]
                for h in range(HEADS):
                    mean_eps(("head_var", l, which, h), RSQ[:QK, h, :], T, QK, EPS, QK)
                reciprocal_root(RSQ[:QK, :, :])
                flat = lambda a: a[:QK, :, :].rearrange("p h t -> p (h t)")
                stt(flat(x), flat(x), par(f"{'qk'[which]}n{l}", QK), flat(RSQ), ALU.mult, ALU.mult)
                r = slice(NOPE, QK)
                half = ROPE // 2
                shape = [ROPE, HEADS, T]
                c, s = CONSTS["cos"][0], CONSTS["sin"][0]
                lane(nc.vector.stream_shuffle(RSQ[r, :, :], x[r, :, :], [(i + half) % ROPE for i in range(ROPE)]))
                tt(RSQ[r, :, :], RSQ[r, :, :], bc(CST[r, None, s : s + T], shape), ALU.mult)
                tt(x[r, :, :], x[r, :, :], bc(CST[r, None, c : c + T], shape), ALU.mult)
                tt(x[r, :, :], x[r, :, :], RSQ[r, :, :], ALU.add, sem("heads_ready"))

            def att_scores(l, h):
                s = 16 * (h % 2)
                for i, (lo, n) in enumerate(TOK1):
                    src = wait_bank("att", l, h, i)
                    if i == 0 and h >= 2:
                        wait_bank("att_turned", l, h - 2)
                    ins = nc.vector.tensor_tensor_reduce(P2[h % 2][:n, i, : lo + n], src[:n, : lo + n], cst("causal", 256 - lo, lo + n)[:n, :],
                                                         1.0, NEG, ALU.add, ALU.max, SM[:n, s + i : s + i + 1])
                    free(ins, "att", l, h, i)
                ts(SM[:, s + 4 : s + 7], SM[:, s : s + 3], -SCALE_MLA, None, ALU.mult, done=sem("att_max"))

            def att_norm(l, h):
                s = 16 * (h % 2)
                dve.wait_ge(sem("att_exps"), 3 * (HEADS * l + h + 1))
                lane(nc.vector.reciprocal(SM[:128, s + 12 : s + 14], SM[:, s + 8 : s + 10]))
                lane(nc.vector.reciprocal(SM[:16, s + 14 : s + 15], SM[:16, s + 10 : s + 11]))
                for i, (lo, n) in enumerate(TOK1):
                    p = P2[h % 2][:n, i, : lo + n]
                    ts(p, p, SM[:n, s + 12 + i : s + 13 + i], None, ALU.mult, done=sem("att_probs") if i == 2 else None)

            def mix_out(l):
                for m in range(KT):
                    src = wait_bank("mix_out", l, m)
                    free(nc.vector.tensor_tensor(XT[:, m, :], src[:, :T], XT[:, m, :], ALU.add), "mix_out", l, m)

            def ff2(l):
                for m in range(KT):
                    src = wait_bank("ff2", l, m)
                    free(nc.vector.tensor_tensor(XT[:, m, :], src[:, :T], XT[:, m, :], ALU.add), "ff2", l, m)

            def b_gates():
                for row, g, name in ((4, 0, "ibias"), (3, 1, "fbias")):
                    src = wait_bank("if", g)
                    free(nc.vector.tensor_scalar(ROWS[:4, row, :], src[:4, :256], par(name, 4), None, ALU.add), "if", g)
                stt(ROWS[:4, 5, :], ROWS[:4, 3, :], -1.0, ROWS[:4, 3, :], ALU.mult, ALU.max, sem("forget_abs"))
                dve.wait_ge(sem("forget_logs"), 1)
                stt(ROWS[:4, 6, :], ROWS[:4, 3, :], 0.0, ROWS[:4, 5, :], ALU.min, ALU.subtract)
                lane(nc.vector.tensor_tensor_scan(ROWS[:4, 7, :], bc(cst("ones", 0, 1, 4), [4, 256]), ROWS[:4, 6, :], 0.0, ALU.mult, ALU.add))
                tt(ROWS[:4, 0, :], ROWS[:4, 4, :], ROWS[:4, 7, :], ALU.subtract)
                lane(nc.vector.tensor_tensor_scan(ROWS[:4, 1, :], ROWS[:4, 0, :], ROWS[:4, 0, :], 0.0, ALU.max, ALU.max))
                tt(ROWS[:4, 2, :], ROWS[:4, 7, :], ROWS[:4, 1, :], ALU.add)
                ts(ROWS[:4, 1:3, :], ROWS[:4, 1:3, :], -1.0, None, ALU.mult, done=sem("gate_rows"))

            def gate_rows():
                src = wait_bank("gate_cols")
                free(nc.vector.tensor_copy(COLS[:, :], src[:, :16]), "gate_cols")

            def b_conv():
                dve.wait_ge(sem("b_padding"), 1)
                w = par("abconv")
                for j in range(8):
                    banks.await_read(dve, ("bqk", j))
                    for i in range(4):
                        x, wi = BIN[:, j, i : i + 256], w[:, 4 * j + i : 4 * j + i + 1]
                        if i == 0:
                            ts(BC[:, j, :], x, wi, None, ALU.mult)
                        else:
                            stt(BC[:, j, :], x, wi, BC[:, j, :], ALU.mult, ALU.add, sem("b_convolved") if (i, j) == (3, 7) else None)
                dve.wait_ge(sem("b_silu"), 1)
                ts(BC[:, 0:4, :], BC[:, 0:4, :], C_SCALE, None, ALU.mult, done=sem("bqk_ready"))

            def masked_max(key, p, src, bias_, acc, first=None):
                if first is not None:
                    wait_bank(*first)
                lane(nc.vector.tensor_tensor_reduce(p, src, bias_, 1.0, NEG, ALU.add, ALU.max, acc))

            def a_scores(h):
                s = 32 + 16 * (h % 2)
                for i in range(2):
                    src = wait_bank("a", h, i)
                    if i == 0 and h >= 2:
                        wait_bank("a_turned", h - 2)
                    ins = nc.vector.tensor_tensor_reduce(P[h % 2][:, i, : 128 * i + 128], src[:, : 128 * i + 128], BIAS_A[:, h, 128 - 128 * i :],
                                                         1.0, NEG, ALU.add, ALU.max, SM[:, s + i : s + i + 1])
                    free(ins, "a", h, i)
                ts(SM[:, s + 4 : s + 6], SM[:, s : s + 2], -1.0, None, ALU.mult, done=sem("a_max"))

            def a_norm(h):
                s = 32 + 16 * (h % 2)
                dve.wait_ge(sem("a_exps"), 2 * (h + 1))
                lane(nc.vector.reciprocal(SM[:, s + 12 : s + 14], SM[:, s + 8 : s + 10]))
                for i in range(2):
                    p = P[h % 2][:, i, : 128 * i + 128]
                    ts(p, p, SM[:, s + 12 + i : s + 13 + i], None, ALU.mult, done=sem("a_probs") if i else None)

            def b_scores(h):
                for i in range(2):
                    src = wait_bank("b_row", h, i)
                    if i == 0 and h >= 2:
                        wait_bank("b_turned", h - 2)
                    n = 128 * i + 128
                    tt(P[2 + h % 2][:, i, :n], src[:, :n], cst("causal", 256 - 128 * i, n), ALU.add, sem("b_masked"))
                    free(nc.vector.memset(SM[:, 31:32], 0.0), "b_row", h, i)

            def b_norm_weights(h):
                s = 144
                for i in range(2):
                    p = P[2 + h % 2][:, i, : 128 * i + 128]
                    dve.wait_ge(sem("b_exps"), 2 * h + i + 1)
                    src = wait_bank("b", h, i)
                    free(nc.vector.tensor_tensor_reduce(p, src[:, : 128 * i + 128], p, 1.0, 0.0, ALU.mult, ALU.add, SM[:, s + i : s + i + 1]), "b", h, i)
                stt(SM[:, s : s + 2], SM[:, s : s + 2], -1.0, SM[:, s : s + 2], ALU.mult, ALU.max)
                floors = COLS[:, :].rearrange("p (i c) -> p i c", i=2)[:, :, 4 + h]
                tt(SM[:, s : s + 2], SM[:, s : s + 2], floors, ALU.max)
                lane(nc.vector.reciprocal(SM[:, s : s + 2], SM[:, s : s + 2]))
                for i in range(2):
                    p = P[2 + h % 2][:, i, : 128 * i + 128]
                    ts(p, p, SM[:, s + i : s + i + 1], None, ALU.mult, done=sem("b_weights") if i else None)

            def b_norm():
                y = YAB[:, 4:8, :]
                for g in range(2):
                    mean_eps(("b_mean", g), AQ[:, 2 * g : 2 * g + 2, :].rearrange("p h t -> p (h t)"), 512, 128, 0.0)
                tt(y, y, AQ[:, 0:4, :], ALU.subtract, sem("b_centered"))
                for g in range(2):
                    mean_eps(("b_var", g), AQ[:, 2 * g : 2 * g + 2, :].rearrange("p h t -> p (h t)"), 512, 128, LN_EPS)
                reciprocal_root(AQ[:, 0:4, :])
                tt(y, y, AQ[:, 0:4, :], ALU.mult)
                for h in range(4):
                    stt(YAB[:, 4 + h, :], YAB[:, 4 + h, :], par("abhead")[:, h : h + 1], SBO[:, h, :], ALU.mult, ALU.mult, sem("y_ready") if h == 3 else None)

            def y_out(l):
                for m in range(KT):
                    src = wait_bank("y_out", l, m)
                    free(nc.vector.scalar_tensor_tensor(HT[:, m, :], HT[:, m, :], ALPHA, src[:, :256], ALU.mult, ALU.add), "y_out", l, m)

            def layer_norm(r):
                shape = [128, KT, 256]
                mean_eps(("ln_mean", r), MU[:, :256], 256, D, 0.0)
                tt(HT, HT, bc(MU[:, None, :256], shape), ALU.subtract, sem("ln_centered"))
                mean_eps(("ln_var", r), RS[:, :256], 256, D, LN_EPS)
                reciprocal_root(RS[:, :256])
                tt(HT, HT, bc(RS[:, None, :256], shape), ALU.mult, sem("ln_scaled"))

            def first_of(dst, x, top, scratch_):
                s4 = [128, 2, 4]
                tt(scratch_, x, bc(top, s4), ALU.is_equal)
                tt(scratch_, scratch_, bc(cst("rank")[:, None, :], s4), ALU.mult)
                lane(nc.vector.tensor_reduce(RT[:, 48:50], scratch_, AX.X, ALU.max))
                tt(dst, scratch_, bc(RT[:, 48:50, None], s4), ALU.is_equal)

            def router(l):
                s4 = [128, 2, 4]
                pair = lambda a, n=4: RT[:, a : a + 2 * n].rearrange("p (i j) -> p i j", i=2)
                for i in range(2):
                    src = wait_bank("router", l, i)
                    free(nc.vector.tensor_copy(RT[:, 20 * i : 20 * i + 20], src[:, :20]), "router", l, i)
                logits = RT[:, 0:40].rearrange("p (i c) -> p i c", i=2)
                lane(nc.vector.tensor_reduce(RT[:, 40:42], logits[:, :, 0:4], AX.X, ALU.max))
                ts(RT[:, 42:44], RT[:, 40:42], -1.0, None, ALU.mult, done=sem("group_max"))
                group = pair(64)
                first_of(group, logits[:, :, 0:4], RT[:, 40:42, None], pair(72))
                for i in range(2):
                    e = RT[:, 80:96].rearrange("p (g j) -> p g j", g=4)
                    tt(e, RT[:, 20 * i + 4 : 20 * i + 20].rearrange("p (g j) -> p g j", g=4), bc(RT[:, 64 + 4 * i : 68 + 4 * i, None], [128, 4, 4]), ALU.mult)
                    lane(nc.vector.tensor_reduce(RT[:, 96 + 4 * i : 100 + 4 * i], e.rearrange("p g j -> p j g"), AX.X, ALU.add))
                chosen = pair(96)
                lane(nc.vector.tensor_reduce(RT[:, 50:52], chosen, AX.X, ALU.max))
                one, two = pair(104), pair(112)
                first_of(one, chosen, RT[:, 50:52, None], pair(72))
                stt(RT[:, 96:104], RT[:, 104:112], NEG, RT[:, 96:104], ALU.mult, ALU.add)
                lane(nc.vector.tensor_reduce(RT[:, 52:54], chosen, AX.X, ALU.max))
                first_of(two, chosen, RT[:, 52:54, None], pair(72))
                tt(RT[:, 46:48], RT[:, 52:54], RT[:, 50:52], ALU.subtract, sem("top_gap"))
                dve.wait_ge(sem("top_exps"), l + 1)
                dve.wait_ge(sem("group_exps"), 2 * (l + 1))
                ts(RT[:, 50:52], RT[:, 46:48], 1.0, None, ALU.add)
                tt(RT[:, 50:52], RT[:, 50:52], RT[:, 44:46], ALU.mult)
                lane(nc.vector.reciprocal(RT[:, 50:52], RT[:, 50:52]))
                tt(RT[:, 52:54], RT[:, 50:52], RT[:, 46:48], ALU.mult)
                tt(one, one, bc(RT[:, 50:52, None], s4), ALU.mult)
                tt(two, two, bc(RT[:, 52:54, None], s4), ALU.mult)
                tt(one, one, two, ALU.add)
                for i in range(2):
                    e = SM[:, 200 + 16 * i : 216 + 16 * i].rearrange("p (g j) -> p g j", g=4)
                    tt(e, bc(RT[:, 64 + 4 * i : 68 + 4 * i, None], [128, 4, 4]), bc(RT[:, None, 104 + 4 * i : 108 + 4 * i], [128, 4, 4]),
                       ALU.mult, sem("expert_gates"))

            def moe(l):
                banks.await_read(dve, ("gate_row", l, NEXP - 1))
                for j in range(4):
                    ts(YT[:, 2 * j : 2 * j + 2, :], HT[:, 2 * j : 2 * j + 2, :], ALPHA, None, ALU.mult, done=sem("hidden"))
                gates = GB[:, :, :].rearrange("p e t -> p (e t)")
                with dve.Fori(0, NEXP) as e:
                    loop["v"] = 2 * e
                    lane.enter(e, {"hidden": 4})
                    for j in range(4):
                        src = wait_bank("moe_up", l, j)
                        free(nc.vector.tensor_tensor(HE[:, j, :], src[:, :256], gates[:, bass.ds(256 * e, 256)], ALU.mult), "moe_up", l, j)
                        banks.await_read(dve, ("moe_gate", l, j), loop["v"])
                        tt(HE[:, j, :], HE[:, j, :], SGM[:, j, :], ALU.mult, sem("hidden"))
                    for m in range(KT):
                        src = wait_bank("moe_down", l, m)
                        free(nc.vector.tensor_tensor(YT[:, m, :], src[:, :256], YT[:, m, :], ALU.add), "moe_down", l, m)
                    lane.leave(NEXP)
                loop["v"] = None
                lane(nc.vector.tensor_copy(HT, YT[:, :, :]), sem("moe_done"))

            def blocks(s):
                for g in range(2):
                    banks.await_read(dve, ("c_src", 2 * s + g))
                if s:
                    wait_bank("c_hidden", 0)
                pos = par("pos")
                for g in range(2):
                    x = BIN[:, 2 * s + g, :256].rearrange("p (c r) -> p r c", r=16)
                    for a in range(2):
                        pv = pos[:, 32 * s + 16 * a : 32 * s + 16 * a + 16, None]
                        tt(BLK[:, 16 * a : 16 * a + 16, 15 * g : 15 * g + 15], x[:, :, a : a + 15], bc(pv, [128, 16, 15]), ALU.add,
                           sem("blocks") if (g, a) == (1, 1) else None)
                if s == 0:
                    for a in PC:
                        lane(nc.vector.memset(a, 0.0))

            def compress(s):
                dve.wait_ge(sem("c_gelu"), s + 1)
                free(nc.vector.memset(SM[:, 31:32], 0.0), "c_hidden", s)

            def c_scores(h):
                s = 64 + 20 * (h % 2)
                if h >= 2:
                    wait_bank("c_turned", h - 2, 2)
                for i in range(2):
                    n = 128 * i + 128
                    for b in range(2):
                        src = wait_bank("c", h, i, b)
                        c = s + 2 * (b + 1) + i
                        ins = nc.vector.tensor_tensor_reduce(P[2 * (h % 2) + b][:, i, :n], src[:, :n], BIAS_C[:, h, 256 - n :],
                                                             1.0, NEG, ALU.add, ALU.max, SM[:, c : c + 1])
                        free(ins, "c", h, i, b)
                src = wait_bank("c_c", h)
                for i in range(2):
                    n = 7 + 8 * i
                    bias_ = BIAS_C[:, h, 128 * (1 - i) + 31 :: 16]
                    ins = nc.vector.tensor_tensor_reduce(PC[h % 2][:, i, :n], src[:, 16 * i : 16 * i + n], bias_, 1.0, NEG, ALU.add, ALU.max, SM[:, s + i : s + i + 1])
                    if i:
                        free(ins, "c_c", h)
                    else:
                        lane(ins)
                ts(SM[:, s + 6 : s + 12], SM[:, s : s + 6], NEG / 10, -1.0, ALU.max, ALU.mult, sem("c_max"))

            def c_norm(h):
                s = 64 + 20 * (h % 2)
                dve.wait_ge(sem("c_exps"), 6 * (h + 1))
                banks.await_read(dve, ("c_gate", 1))
                ts(SM[:, s + 12 : s + 18], SM[:, s + 12 : s + 18], 1e-30, None, ALU.max)
                lane(nc.vector.reciprocal(SM[:, s : s + 6], SM[:, s + 12 : s + 18]))
                f = SM[:, s : s + 6].rearrange("p (b i) -> p b i", b=3)
                g = CG[:, :, :].rearrange("p i (b h) -> p b i h", b=3)[:, :, :, h]
                tt(f, f, g, ALU.mult)
                for b in (1, 2, 0):
                    for i in range(2):
                        p = PC[h % 2][:, i, : 7 + 8 * i] if b == 0 else P[2 * (h % 2) + b - 1][:, i, : 128 * i + 128]
                        ts(p, p, SM[:, s + 2 * b + i : s + 2 * b + i + 1], None, ALU.mult, done=sem("c_probs") if i else None)

            steps = locals()
            for name, *args in SCHEDULE:
                if name in steps:
                    steps[name](*args)

        @block.gpsimd
        def _(pool):
            lane = Lane(pool, sem("gpsimd_step"))

            def hgrn_args(l, i):
                pool.wait_ge(sem("summed"), l + 1)
                if i >= 2:
                    banks.await_(pool, ("scores", l, i - 2))
                d, lo = HD[i % 2], SB * i
                qq = d[:, :1024].rearrange("p (j h t) -> p j h t", j=8, h=4)
                shape = [128, 8, 4, SB]
                b = HB[:, :, lo : lo + SB]
                ref = b.rearrange("p h (j f) -> p j h f", f=SS)[:, :, :, 0:1]
                lane(nc.gpsimd.tensor_tensor(qq, bc(b[:, None, :, :], shape), bc(ref, shape), ALU.subtract))
                lane(nc.gpsimd.tensor_scalar(d[:, :1024], d[:, :1024], 0.0, None, ALU.min), None if i else sem("decay_args"))
                if i:
                    kk = d[:, 1024 : 1024 + 4 * lo].rearrange("p (h s) -> p h s", h=4)
                    lane(nc.gpsimd.tensor_tensor(kk, bc(HB[:, :, lo : lo + 1], [128, 4, lo]), HB[:, :, :lo], ALU.subtract), sem("decay_args"))

            def ff1(l):
                for m in range(FT):
                    banks.await_read(pool, ("ff1", l, m))
                    lane(nc.gpsimd.tensor_tensor(F1[:, m, :], F1[:, m, :], F1[:, m, :], ALU.mult), sem("squared"))

            def ab_in():
                banks.await_(pool, ("aq", 0))
                lane(nc.gpsimd.memset(BIN[:, :, 0:3], 0.0), sem("b_padding"))

            steps = locals()
            for name, *args in SCHEDULE:
                if name in steps:
                    steps[name](*args)

        @block.sync
        def _(sp):
            sp.dma_start(XT[:, :, :], x_in).then_inc(sem("loaded"), 16)
            sp.dma_start(PAR[:, :], params).then_inc(sem("loaded"), 16)
            sp.dma_start(CST[:, :], consts).then_inc(sem("loaded"), 16)

            def load(n, slot):
                sp.dma_start(ring[:, slot, :], stream[bass.ds(128 * n, 128), :]).then_inc(arrived[slot], 16)

            for s in range(RING):
                load(s, s)
            rounds = n_chunks // RING
            with sp.Fori(1, rounds) as r:
                for s in range(RING):
                    sp.wait_ge(w_used, RING * (r - 1) + s + 1)
                    load(RING * r + s, s)
            for n in range(RING * rounds, n_chunks):
                sp.wait_ge(w_used, n - RING + 1)
                load(n, n % RING)
            for k in range(KT):
                sp.wait_ge(sem("ln_done"), KT * 3 + k + 1)
                sp.dma_start(out[:, k, :], HT[:, k, :]).then_inc(sem("stored"), 16)
            sp.wait_ge(sem("stored"), 16 * KT)


def schedule():
    s = [("start",), ("bias",)]
    for l in range(DEPTH):
        s += [("norm", 2 * l), ("conv_in", l), ("hgrn_in", l), ("mla_in", l), ("hgrn_prep", l), ("conv_taps", l)]
        s += [("gate", l, 0, m) for m in range(KT)]
        s += [("conv_norm", l), ("branch_out", l, 0), ("mla_norm", l)]
        s += [("hgrn_args", l, 0)]
        for i in range(NB):
            s += [("hgrn_args", l, i + 1)] if i + 1 < NB else []
            s += [("hgrn_block", l, i)]
            s += [("gate", l, 1, i)] if i < KT else []
            s += [("hgrn_turn", l, i)]
        s += [("hgrn_values", l), ("mla_up", l), ("hgrn_norm", l), ("branch_out", l, 1), ("head_norm", l, 0), ("head_norm", l, 1)]
        s += [("att_scores", l, 0)]
        for h in range(HEADS):
            s += [("att_scores", l, h + 1)] if h + 1 < HEADS else []
            s += [("gate", l, 2, h), ("att_norm", l, h), ("att_turn", l, h)]
            s += [("att_values", l, h // 2)] if h % 2 else []
        s += [("branch_out", l, 2), ("mix_out", l), ("norm", 2 * l + 1), ("ff1", l), ("ff2", l)]
    s += [("ab_in",), ("ab_in2",), ("b_gates",), ("b_conv",), ("gate_rows",), ("a_scores", 0)]
    for h in range(HEADS):
        s += [("a_scores", h + 1)] if h + 1 < HEADS else []
        s += [("a_norm", h), ("a_turn", h)]
        s += [("a_values", h // 2)] if h % 2 else []
    s += [("b_scores", 0)]
    for h in range(H4):
        s += [("b_norm_weights", h)]
        s += [("b_scores", h + 1)] if h + 1 < H4 else []
        s += [("b_turn", h), ("b_values", h)]
    s += [("b_norm",)]
    for l in range(2):
        if l:
            s += [("c_in",), ("blocks", 0), ("compress", 0), ("blocks", 1), ("compress", 1), ("compress2",), ("c_scores", 0)]
            for h in range(HEADS):
                s += [("c_scores", h + 1)] if h + 1 < HEADS else []
                s += [("c_norm", h), ("c_turn", h), ("c_values", h)]
        s += [("y_out", l), ("layer_norm", 2 * l), ("router", l), ("expert_gates", l), ("moe", l), ("layer_norm", 2 * l + 1)]
    return s


def kernel(**inputs):
    from concourse import bacc, mybir as _mybir
    from concourse.bass_utils import run_bass_kernel_spmd

    i = {k: np.asarray(v) for k, v in inputs.items()}
    tokens = np.concatenate([i["meta"], i["x"][0]], axis=0)
    arrays = {
        "weights": np.ascontiguousarray(weight_stream(i).reshape(-1, CHUNK)),
        "params": parameters(i),
        "consts": constants(),
        "x": np.ascontiguousarray(tokens.T.reshape(KT, 128, T).transpose(1, 0, 2)),
    }
    nc = bacc.Bacc("TRN2", target_bir_lowering=False, num_devices=1)
    aps = {k: nc.dram_tensor(f"in_{k}", a.shape, _mybir.dt.from_np(a.dtype), kind="ExternalInput").ap() for k, a in arrays.items()}
    out = nc.dram_tensor("out", (128, KT, SEQ), F32, kind="ExternalOutput").ap()
    scratch = nc.dram_tensor("bias_by_distance", (HEADS, 384), F32, kind="Internal").ap()
    build_program(nc, aps["weights"], aps["params"], aps["consts"], aps["x"], out, scratch)
    r = run_bass_kernel_spmd(nc, [{f"in_{k}": a for k, a in arrays.items()}], core_ids=[0])
    y = np.asarray(r.results[0]["out"])
    return np.ascontiguousarray(y.transpose(2, 1, 0).reshape(1, SEQ, D))
```

```python
from contextlib import ExitStack

import numpy as np

import concourse.bass as bass
from concourse import mybir

F32 = mybir.dt.float32
F32R = mybir.dt.float32r
ALU = mybir.AluOpType
ACT = mybir.ActivationFunctionType
AX = mybir.AxisListType

D = 1024
KT = D // 128
DEPTH = 2
N_META = 16
SEQ = 256
T = SEQ + N_META
TOK1 = [(0, 128), (128, 128), (256, T - 256)]
TP = 288
EPS = 1e-6
CLAMP = 1.0 - 1e-6
CONV_K = 31
HEADS = 8
NOPE, ROPE, QK, VD = 64, 32, 96, 64
H4 = 4
SB, SS = 32, 4
NB = TP // SB
D_FF = 4 * D
FT = D_FF // 128
ALPHA = (2.0 * DEPTH) ** 0.25
LN_EPS = 1e-5
BUCKETS, MAX_DIST = 32, 2048
NCMP = (SEQ - 32) // 16 + 1
NEXP, EH = 16, D // 2
MOE_CHUNKS = 24
NEG = -1e30
A_SCALE, C_SCALE = 64 ** -0.5, 128 ** -0.5

CHUNK = 1024
RING = 4
SPLIT = 4
FH = FT // 2


def feature_chunks(w):
    k, m = w.shape
    return w.reshape(k // 128, 128, m // 128, 128).transpose(2, 1, 0, 3).reshape(m // 128, 128, k)


def grouped(w, n):
    t = feature_chunks(w)
    return t.reshape(t.shape[0] // n, n, 128, -1).transpose(0, 2, 1, 3).reshape(-1, 128, n * t.shape[2])


def token_chunks(w):
    return w.reshape(4, 2, 128, 512).transpose(0, 2, 1, 3).reshape(4, 128, 1024)


def padded(a):
    out = np.zeros((a.shape[0], 128, CHUNK), np.float32)
    out[:, :, : a.shape[2]] = a
    return out


def weight_stream(i):
    out = []
    for l in range(DEPTH):
        w = i["w_in"][l]
        at = np.cumsum([0, 1024, 256, 128, 32, 512, 512, 512, 512, 3072])
        conv, cq, ckv, rope, hq, hf, hi, hg, gate = (w[:, at[j] : at[j + 1]] for j in range(9))
        c = feature_chunks(conv)
        out += [c.reshape(2, 4, 128, 1024).transpose(1, 0, 2, 3).reshape(8, 128, 1024)]
        out += [feature_chunks(hf), feature_chunks(hq), feature_chunks(hg), token_chunks(hi)]
        out += [feature_chunks(cq), feature_chunks(ckv)]
        r = np.zeros((D, 128), np.float32)
        r[:, NOPE:QK] = rope
        out += [feature_chunks(r)]
        gates = [feature_chunks(gate[:, g * D : (g + 1) * D]) for g in range(3)]
        out += [gates[0], grouped(i["w_conv_out"][l], 2), gates[2]]
        uq = i["w_uq"][l].reshape(2, 128, HEADS, QK).transpose(2, 1, 0, 3)
        out += [padded(uq.reshape(2, 4, 128, 2 * QK).transpose(0, 2, 1, 3).reshape(2, 128, 8 * QK))]
        ukv = i["w_ukv"][l].reshape(128, HEADS, 2, 64).transpose(0, 2, 1, 3)
        out += [ukv.reshape(1, 128, 1024)]
        out += [gates[1], grouped(i["w_hgrn_out"][l], 2), grouped(i["w_attn_out"][l], 2)]
        out += [feature_chunks(i["w_out"][l])]
        f1, f2 = feature_chunks(i["w_ff1"][l]), feature_chunks(i["w_ff2"][l]).reshape(KT, 128, 4, 1024)
        for half in range(2):
            out += [f1[FH * half : FH * half + FH], f2[:, :, 2 * half : 2 * half + 2].transpose(0, 2, 1, 3).reshape(-1, 128, 1024)]
    w = i["ab_w_in_2"][0]
    part = lambda j: w[:, 512 * j : 512 * j + 512]
    out += [feature_chunks(part(0)), feature_chunks(part(1)), token_chunks(part(2))]
    out += [feature_chunks(part(3)), feature_chunks(part(4)), feature_chunks(part(6)), token_chunks(part(5))]
    out += [feature_chunks(i["ab_w_out_2"][0])]
    moe = lambda l: experts(i["moe_w_gate_2"][l], i["moe_w_up_2"][l], i["moe_w_down_2"][l])
    out += [moe(0)]
    w = i["c_w_in_2"][0]
    kv = w[:, D : D + 1536].reshape(D, 3, 2, 256)
    out += [feature_chunks(kv[:, 0].reshape(D, 512)), feature_chunks(w[:, :D])]
    out += [feature_chunks(kv[:, 1, 0]), feature_chunks(kv[:, 2, 0])]
    out += [token_chunks(kv[:, 1:, 1].reshape(D, 512))]
    for s in range(2):
        out += [i["c_cmp_w1_2"][0, s].reshape(8, 4, 128, 256).transpose(0, 2, 1, 3).reshape(8, 128, 1024)]
    w2 = i["c_cmp_w2_2"][0].reshape(2, 2, 128, 128).transpose(2, 0, 1, 3).reshape(1, 128, 512)
    out += [padded(w2), feature_chunks(i["c_w_out_2"][0]), moe(1)]
    return np.concatenate(out, axis=0)


def experts(gate, up, down):
    out = []
    for e in range(NEXP):
        g, u = feature_chunks(gate[e]), feature_chunks(up[e])
        out += [np.stack([g, u], 1).reshape(8, 128, 1024)]
        if e:
            out += [grouped(down[e - 1], 2)]
    return np.concatenate([*out, grouped(down[-1], 2)], axis=0)


def layout(widths):
    at, out = 0, {}
    for name, n in widths:
        out[name] = (at, n)
        at += n
    return out, at


PARAMS, NPAR = layout(
    [(f"{n}{l}", c) for l in range(DEPTH) for n, c in (
        ("norm1", 8), ("convw", 4 * CONV_K), ("convb", 4), ("clng", 4), ("clnb", 4), ("qa", 2), ("kva", 1),
        ("qn", 1), ("kn", 1), ("lb", 4), ("hn", 4), ("norm2", 8),
        ("lng0_", 8), ("lnb0_", 8), ("lng1_", 8), ("lnb1_", 8), ("router", KT * 20), ("rbias", 20))]
    + [("ibias", 1), ("fbias", 1), ("abconv", 8 * 4), ("abhead", 4), ("wif", KT * 8),
       ("pos", 64), ("wcg", KT * 24), ("cgbias", 24), ("rel", HEADS)])

CONSTS, NCONST = layout([
    ("ident", 128), ("flip", 128), ("ones", 128), ("causal", 528), ("logcount", 256), ("tri", SB),
    ("cos", T), ("sin", T), ("bucket", 384), ("rank", 4)])


def parameters(i):
    out = np.zeros((128, NPAR), np.float32)

    def put(name, a):
        at, n = PARAMS[name]
        a = np.asarray(a, np.float32)
        a = a.reshape(a.shape[0], -1)
        out[: a.shape[0], at : at + n] = a

    col = lambda v: np.asarray(v).reshape(-1, 128).T
    for l in range(DEPTH):
        put(f"norm1{l}", col(i["norm1_g"][l]))
        put(f"convw{l}", i["conv_w"][l].reshape(CONV_K, 4, 128).transpose(2, 1, 0))
        put(f"convb{l}", col(i["conv_b"][l]))
        put(f"clng{l}", col(i["conv_ln_g"][l]))
        put(f"clnb{l}", col(i["conv_ln_b"][l]))
        put(f"qa{l}", col(i["q_a_norm_g"][l]))
        put(f"kva{l}", col(i["kv_a_norm_g"][l]))
        put(f"qn{l}", i["q_norm_g"][l][:, None])
        put(f"kn{l}", i["k_norm_g"][l][:, None])
        put(f"lb{l}", col(i["hgrn_lb_logits"][l]))
        put(f"hn{l}", col(i["hgrn_norm_g"][l]))
        put(f"norm2{l}", col(i["norm2_g"][l]))
        for j in range(2):
            put(f"lng{j}_{l}", col(i["ln_g_2"][l, j]))
            put(f"lnb{j}_{l}", col(i["ln_b_2"][l, j]))
        r = np.concatenate([i["moe_wr_g_2"][l], i["moe_wr_e_2"][l].transpose(1, 0, 2).reshape(D, 16)], axis=1)
        put(f"router{l}", r.reshape(KT, 128, 20).transpose(1, 0, 2))
        put(f"rbias{l}", np.concatenate([i["moe_br_g_2"][l], i["moe_br_e_2"][l].reshape(-1)])[None])
    put("ibias", i["ab_gate_b_2"][0, :4][:, None])
    put("fbias", i["ab_gate_b_2"][0, 4:][:, None])
    put("abconv", i["ab_conv_2"][0].reshape(4, 8, 128).transpose(2, 1, 0))
    put("abhead", col(i["ab_head_norm_2"][0]))
    put("wif", i["ab_w_in_2"][0][:, 3584:3592].reshape(KT, 128, 8).transpose(1, 0, 2))
    put("pos", i["c_cmp_pos_2"][0].transpose(2, 0, 1))
    put("wcg", i["c_w_in_2"][0][:, 2560:2584].reshape(KT, 128, 24).transpose(1, 0, 2))
    put("cgbias", i["c_gate_b_2"][0][None])
    put("rel", i["rel_bias_2"])
    return out


def constants():
    out = np.zeros((128, NCONST), np.float32)

    def put(name, a, row=0):
        at, n = CONSTS[name]
        out[row : row + a.shape[0], at : at + n] = a.reshape(a.shape[0], -1)

    p = np.arange(128)
    put("ident", np.eye(128))
    put("flip", np.eye(128)[::-1])
    put("ones", np.ones((128, 128)))
    put("causal", np.where(np.arange(528)[None] - 256 <= p[:, None], 0.0, NEG))
    d = p[:, None] + 128 - np.arange(256)[None]
    n = ((d <= 128).astype(int) + (d % 4 == 0) + (d % 16 == 0)) * (d >= 0)
    put("logcount", np.where(n > 0, np.log(np.maximum(n, 1)), NEG))
    put("tri", (np.arange(SB)[None] <= (p % SB)[:, None]).astype(float))
    half = ROPE // 2
    inv = 10000.0 ** (-np.arange(half, dtype=np.float32) / np.float32(half))
    ang = (np.arange(T, dtype=np.float32)[None] * inv.astype(np.float32)[:, None]).astype(np.float32)
    put("cos", np.concatenate([np.cos(ang)] * 2), NOPE)
    put("sin", np.concatenate([-np.sin(ang), np.sin(ang)]), NOPE)
    n = np.maximum(255 - np.arange(384), 0)
    exact = BUCKETS // 2
    large = exact + (np.log(np.maximum(n, 1) / exact) / np.log(MAX_DIST / exact) * (BUCKETS - exact)).astype(int)
    put("bucket", (np.where(n < exact, n, np.minimum(large, BUCKETS - 1))[None] == np.arange(BUCKETS)[:, None]).astype(float))
    put("rank", np.tile([4.0, 3.0, 2.0, 1.0], (128, 1)))
    return out


class Lane:

    def __init__(self, eng, step):
        self.eng, self.step, self.count, self.loop = eng, step, {}, None

    def __call__(self, ins, sem=None):
        sem = sem or self.step
        n = self.count[sem.name] = self.count.get(sem.name, 0) + 1
        ins.then_inc(sem, 1)
        self.eng.wait_ge(sem, self.at(sem, n))

    def at(self, sem, n):
        return n if self.loop is None else n + self.loop[0] * self.loop[1][sem.name]

    def enter(self, i, per):
        self.loop, self.before = (i, per), dict(self.count)

    def leave(self, times):
        for name, n in self.loop[1].items():
            assert self.count.get(name, 0) - self.before.get(name, 0) == n, (name, self.count[name], self.before.get(name, 0))
            self.count[name] += n * (times - 1)
        self.loop = None


class Splits:

    def __init__(self):
        self.chunks, self.marks, self.known = [], {}, ()

    def limit(self, mark):
        begun, n = self.marks[mark]
        count = min(begun - 1 + SPLIT, len(self.chunks))
        while count and self.chunks[count - 1] > n - 2 + RING and self.chunks[count - 1] - RING not in self.known:
            count -= 1
        return count


class Follower:

    def __init__(self, splits, split):
        self.splits, self.split, self.next = splits, split, 0

    def __call__(self, mark):
        while self.next < self.splits.limit(mark):
            self.split(self.next, self.splits.chunks[self.next])
            self.next += 1


class Banks:

    def __init__(self, psum, full, free):
        self.psum, self.full, self.free = psum, full, free
        self.next, self.uses, self.of = 0, [0] * 8, {}
        self.loop = None

    def value(self, n, loop):
        return n if loop is None else n + loop

    def take(self, pe, key):
        b, n = self.next, self.uses[self.next]
        self.next, self.uses[b] = (b + 1) % 8, n + 1
        assert key not in self.of, key
        self.of[key] = (b, n)
        if n:
            pe.wait_ge(self.free[b], n if self.loop is None else n + self.loop)
        return self.psum[:, b, :]

    def filled(self, key):
        return self.full[self.of[key][0]]

    def await_(self, eng, key, loop=None):
        b, n = self.of[key]
        eng.wait_ge(self.full[b], n + 1 if loop is None else n + 1 + loop)
        return self.psum[:, b, :]

    def freed(self, key):
        return self.free[self.of[key][0]]

    def await_read(self, eng, key, loop=None):
        b, n = self.of[key]
        eng.wait_ge(self.free[b], n + 1 if loop is None else n + 1 + loop)


def build_program(nc, stream, params, consts, x_in, out, scratch):
    n_chunks = stream.shape[0] // 128
    with ExitStack() as ctx:
        def sb(name, *shape, dtype=F32, stack=ctx):
            return stack.enter_context(nc.sbuf_tensor(name, [128, *shape], dtype))

        sems = {}

        def sem(name):
            if name not in sems:
                sems[name] = ctx.enter_context(nc.semaphore(name))
            return sems[name]

        ring = sb("ring", RING, CHUNK)
        W_HI = sb("W_HI", SPLIT, CHUNK, dtype=F32R)
        W_LO = sb("W_LO", SPLIT, CHUNK, dtype=F32R)
        XT = sb("XT", KT, T)
        HN = sb("HN", KT, T)
        SQ = sb("SQ", 8 * TP)
        PAR = sb("PAR", NPAR)
        CST = sb("CST", NCONST)
        BIAS_C = sb("BIAS_C", HEADS, 256)
        BIAS_A = sb("BIAS_A", HEADS, 256)
        MIX = sb("MIX", KT, T)
        GATES = [sb(f"GATE{b}", KT, T) for b in range(2)]
        RS = sb("RS", TP)
        MU = sb("MU", TP)
        psum = ctx.enter_context(nc.psum_tensor("psum", [128, 8, 512], F32))

        used = [0]
        SM = sb("SM", 240)
        RT = sb("RT", 120)
        ST = sb("ST", 64)
        size = 212000 // 4 - ((RING + 2 * SPLIT) * CHUNK + 5 * KT * T + 8 * TP + NPAR + NCONST + 16 * 256 + 2 * TP + 240 + 120 + 64)
        with ExitStack() as phase:
            region = sb("region", size, stack=phase)
        with ExitStack() as phase:
            FN_HI, FN_LO = (sb(f"FN_{p}", KT, T, dtype=F32R, stack=phase) for p in ("HI", "LO"))
            F1_HI, F1_LO = (sb(f"F1_{p}", FH, T, dtype=F32R, stack=phase) for p in ("HI", "LO"))
            F1 = sb("F1", 4, T, stack=phase)
            assert (2 * (KT + FH) + 4) * T <= size
        with ExitStack() as phase:
            X_HI, X_LO = (sb(f"X_{p}", KT, 256, dtype=F32R, stack=phase) for p in ("HI", "LO"))
            HE_HI, HE_LO = (sb(f"HE_{p}", 2, 4, 256, dtype=F32R, stack=phase) for p in ("HI", "LO"))
            HE = sb("HE", 4, 256, stack=phase)
            GB = sb("GB", NEXP, 256, stack=phase)
            GATT = sb("GATT", 256, stack=phase)
            SGM = sb("SGM", 4, 256, stack=phase)
            assert (2 * KT + 16 + 4 + NEXP + 1 + 4) * 256 <= size

        def at_region(*shape):
            n = int(np.prod(shape))
            v = region[:, used[0] : used[0] + n]
            used[0] += n
            assert used[0] <= region.shape[1], (used[0], region.shape)
            if len(shape) == 2:
                return v.rearrange("p (a b) -> p a b", a=shape[0])
            if len(shape) == 3:
                return v.rearrange("p (a b c) -> p a b c", a=shape[0], b=shape[1])
            return v

        HC = at_region(4, T + CONV_K - 1)
        CO = at_region(4, T)
        HB = at_region(4, TP)
        HK = at_region(4, TP)
        HQ = at_region(4, TP)
        HG = at_region(4, T)
        HV = at_region(3, 512)
        HR = HK[:, :, :T]
        CQ = at_region(2, T)
        CKV = at_region(T)
        MV = HV
        KR = at_region(T)
        work = used[0]
        HKK = at_region(4, TP)
        HD = [at_region(1024 + 4 * 256) for _ in range(2)]
        HA = [at_region(TP + 96) for _ in range(2)]
        HAT = at_region(3, 4, TP)
        first = used[0]
        used[0] = work
        QH = at_region(HEADS, T)
        KH = at_region(HEADS, T)
        RSQ = at_region(HEADS, T)
        P2 = [at_region(3, T) for _ in range(2)]
        PT2 = [at_region(432) for _ in range(2)]
        first = max(first, used[0])
        OT = CO
        HO = HB
        used[0] = 0
        YT = MIX[:, :, :256]
        AQ = at_region(KT, 256)
        AK = at_region(KT, 256)
        AV = at_region(2, 512)
        BV = at_region(2, 512)
        BIN = at_region(8, 259)
        BC = at_region(8, 256)
        SBO = at_region(4, 256)
        YAB = at_region(KT, 256)
        ROWS = SQ[:, :2048].rearrange("p (r t) -> p r t", r=8)
        COLS = at_region(16)
        P = [GATES[1][:, :, :].rearrange("p k t -> p (k t)")[:, 512 * j : 512 * j + 512].rearrange("p (i t) -> p i t", i=2) for j in range(4)]
        PT = [at_region(384) for _ in range(4)]
        PC = [at_region(2, 16) for _ in range(2)]
        PCT = [at_region(256) for _ in range(2)]
        KC = at_region(30)
        VC = at_region(2, 128)
        CG = at_region(2, 24)
        BLK = at_region(960).rearrange("p (i n) -> p i n", i=32)
        CHID = BC

        def par(name, rows=128):
            at, n = PARAMS[name]
            return PAR[:rows, at : at + n]

        def cst(name, lo=0, n=None, rows=128):
            at, w = CONSTS[name]
            return CST[:rows, at + lo : at + lo + (w if n is None else n)]

        def ones(k, m):
            return cst("ones", 0, m, k)

        ident = lambda k: cst("ident", 0, k, k)
        HT = XT[:, :, N_META:T]

        banks = Banks(psum, [sem(f"bank_full{b}") for b in range(8)], [sem(f"bank_free{b}") for b in range(8)])
        arrived = [sem(f"weights_arrived{s}") for s in range(RING)]
        w_used, split_hi, split_lo, split_used = (sem(n) for n in ("weights_used", "split_hi", "split_lo", "split_used"))
        splits = Splits()
        block = ctx.enter_context(nc.Block())
        SCHEDULE = schedule()

        @block.tensor
        def _(pe):
            state = {"n": 0, "held": None, "release": [], "loop": None}
            keys = {}

            def filled(done):
                splits.marks[keys.pop(done.name)] = (len(splits.chunks), state["n"])

            def mm(dst, w, x, start=True, stop=True, done=None):
                if isinstance(w, tuple):
                    mm(dst, w[0], x[0], start, False)
                    mm(dst, w[0], x[1], False, False)
                    mm(dst, w[1], x[0], False, stop, done)
                    return
                ins = nc.tensor.matmul(dst, w, x, start=start, stop=stop, skip_group_check=True)
                if done is not None:
                    ins.then_inc(done, 1)
                    filled(done)
                elif state["release"]:
                    ins.then_inc(state["release"].pop(0), 1)

            def turn(dst, src, k, done=None):
                ins = nc.tensor.transpose(dst, src, ident(k))
                if done is not None:
                    ins.then_inc(done, 1)
                    filled(done)

            def columns(w, lo, n):
                return tuple(p[:, lo : lo + n] for p in w) if isinstance(w, tuple) else w[:, lo : lo + n]

            def chunk(split=False):
                n = state["n"]
                state["n"] += 1
                state["release"] += [state["held"]] if state["held"] is not None else []
                state["held"] = split_used if split else w_used
                if split:
                    i = len(splits.chunks)
                    splits.chunks.append(n)
                    pe.wait_ge(split_lo, i + 1 if state["loop"] is None else i + 1 + MOE_CHUNKS * state["loop"])
                    return W_HI[:, i % SPLIT, :], W_LO[:, i % SPLIT, :]
                pe.wait_ge(arrived[n % RING], 16 * (n // RING + 1))
                return ring[:, n % RING, :]

            def take(*key):
                dst = banks.take(pe, key)
                keys[banks.filled(key).name] = key
                return dst, banks.filled(key)

            def project(key, x, n=T, chunks=1, ready=None):
                dst, done = take(*key)
                for c in range(chunks):
                    w = chunk(isinstance(x(0), tuple))
                    for k in range(KT):
                        last = c == chunks - 1 and k == KT - 1
                        if ready is not None:
                            ready(8 * c + k)
                        mm(dst[:, :n], columns(w, 128 * k, 128), x(8 * c + k), c + k == 0, last, done if last else None)

            def tokens(key, x, tiles):
                dsts = [take(*key, i) for i in range(len(tiles))]
                for c in range(4):
                    w = chunk()
                    for i, (lo, n) in enumerate(tiles):
                        for k in range(2):
                            last = c == 3 and k == 1
                            mm(dsts[i][0][:n, :], x(2 * c + k, lo, n), w[:, 512 * k : 512 * k + 512],
                               c + k == 0, last, dsts[i][1] if last else None)

            def half_projects(key, x, n, parts=range(4), ready=None):
                for c in parts:
                    w = chunk(isinstance(x(0), tuple))
                    for j in range(2):
                        dst, done = take(*key, 2 * c + j)
                        for k in range(4):
                            if ready is not None and (c, j) == (parts[0], 0):
                                ready(k)
                            mm(dst[:, :n], columns(w, 512 * j + 128 * k, 128), x(k), k == 0, k == 3, done if k == 3 else None)

            def column_sums(key, x, kt, n, ready=None):
                dst, done = take(*key)
                for k in range(kt):
                    if ready is not None:
                        ready(k)
                    mm(dst[:, :n], ones(128, 128), x(k), k == 0, k == kt - 1, done if k == kt - 1 else None)

            sq = lambda k, n=T: SQ[:, n * k : n * k + n]
            hn = lambda k: HN[:, k, :]

            def start():
                pe.wait_ge(sem("loaded"), 48)
                dst, done = take("bucket_bias")
                mm(dst[:HEADS, :384], PAR[:BUCKETS, PARAMS["rel"][0] : PARAMS["rel"][0] + HEADS], cst("bucket", rows=BUCKETS), done=done)

            def till(name, before):
                return lambda k: pe.wait_ge(sem(name), before + k + 1)

            def bias():
                pe.wait_ge(sem("hankel"), 16)
                for g in range(4):
                    dst, done = take("bias", g)
                    mm(dst[:, :], cst("flip"), SQ[:, 512 * g : 512 * g + 512], done=done)

            def norm(r):
                column_sums(("norm", r), sq, KT, T, till("norm_squares", KT * r))

            def conv_in(l):
                for j in range(4):
                    project(("conv_a", l, j), hn, ready=None if j else till("normed", KT * l))
                    project(("conv_g", l, j), hn)

            def hgrn_in(l):
                for name in ("hf", "hq", "hg"):
                    for j in range(4):
                        project((name, l, j), hn)
                tokens(("hi", l), lambda k, lo, n: HN[:, k, lo : lo + n], TOK1)

            def mla_in(l):
                for j in range(2):
                    project(("cq", l, j), hn)
                project(("ckv", l), hn)
                project(("rope", l), hn)

            def conv_norm(l):
                pe.wait_ge(sem("conv_out"), l + 1)
                column_sums(("conv_mean", l), lambda k: CO[:, k, :], 4, T)
                pe.wait_ge(sem("conv_squares"), l + 1)
                column_sums(("conv_var", l), sq, 4, T)

            def gate(l, b, m):
                project(("gate", l, b, m), hn)

            def branch_out(l, b, c):
                src, name = ((CO, "conv_done"), (HO, "hgrn_done"), (OT, None))[b]
                ready = till(name, 4 * l) if name else lambda k: banks.await_read(pe, ("pv", l, k))
                half_projects(("branch", l, b), lambda k: src[:, k, :T], T, (c,), None if c else ready)

            def hgrn_block(l, i):
                pe.wait_ge(sem("decayed"), NB * l + i + 1)
                d = HD[i % 2]
                qq = d[:, 0:1024].rearrange("p (j h t) -> p j h t", j=8, h=4)
                dst, done = take("scores", l, i)
                for h in range(4):
                    row = dst[SB * h : SB * h + SB, :]
                    if i:
                        mm(row[:, : SB * i], qq[:, 0, h, :], d[:, 1024 + SB * i * h : 1024 + SB * i * (h + 1)])
                    for j in range(8):
                        lo = SB * i + SS * j
                        mm(row[:, lo : lo + SS], qq[:, j, h, :], HKK[:, h, lo : lo + SS], done=done if (h, j) == (3, 7) else None)

            def hgrn_turn(l, i):
                banks.await_read(pe, ("scores", l, i))
                dst, done = take("turned", l, i)
                n = -(-SB * (i + 1) // 128)
                for s in range(n):
                    turn(dst[:, 128 * s : 128 * s + 128], HA[i % 2][:, 128 * s : 128 * s + 128], 128, done if s == n - 1 else None)

            def hgrn_values(l):
                banks.await_read(pe, ("turned", l, NB - 1))
                banks.await_read(pe, ("hi", l, 2))
                for h in range(4):
                    dst, done = take("ho", l, h)
                    for s, (lo, k) in enumerate(TOK1):
                        mm(dst[:, lo:TP], HV[:k, s, 128 * h : 128 * h + 128], HAT[:k, s, h, lo:TP], s == 0, s == 2, done if s == 2 else None)

            def hgrn_norm(l):
                pe.wait_ge(sem("hgrn_squares"), l + 1)
                for h in range(4):
                    column_sums(("hgrn_var", l, h), lambda k: sq(h), 1, T)

            def mla_norm(l):
                pe.wait_ge(sem("latent_squares"), 2 * l + 1)
                column_sums(("cq_var", l), lambda k: sq(4 + k), 2, T)
                pe.wait_ge(sem("latent_squares"), 2 * l + 2)
                column_sums(("ckv_var", l), lambda k: sq(6), 1, T)

            def mla_up(l):
                pe.wait_ge(sem("latents"), 2 * l + 1)
                for g in range(2):
                    w = chunk()
                    for h in range(4):
                        dst, done = take("q", l, 4 * g + h)
                        for k in range(2):
                            mm(dst[:QK, :T], w[:, 192 * h + 96 * k : 192 * h + 96 * k + 96], CQ[:, k, :], k == 0, k == 1, done if k else None)
                pe.wait_ge(sem("latents"), 2 * l + 2)
                w = chunk()
                for h in range(HEADS):
                    dst, done = take("k", l, h)
                    mm(dst[:NOPE, :T], w[:, 64 * h : 64 * h + 64], CKV[:, :], done=done)
                for i, (lo, n) in enumerate(TOK1):
                    dst, done = take("v", l, i)
                    mm(dst[:n, :], CKV[:, lo : lo + n], w[:, 512:1024], done=done)

            def head_norm(l, which):
                pe.wait_ge(sem("head_squares"), 2 * l + which + 1)
                for h in range(HEADS):
                    dst, done = take("head_var", l, which, h)
                    mm(dst[:QK, :T], ones(QK, QK), SQ[:QK, T * h : T * h + T], done=done)

            def att_scores(l, h):
                if h == 0:
                    pe.wait_ge(sem("heads_ready"), 2 * l + 2)
                for i, (lo, n) in enumerate(TOK1):
                    dst, done = take("att", l, h, i)
                    mm(dst[:n, : lo + n], QH[:QK, h, lo : lo + n], KH[:QK, h, : lo + n], done=done)

            def att_turn(l, h):
                pe.wait_ge(sem("att_probs"), HEADS * l + h + 1)
                dst, done = take("att_turned", l, h)
                base = (0, T, T + T - 128)
                for i, (lo, n) in enumerate(TOK1):
                    for s in range(i + 1):
                        k = TOK1[s][1]
                        turn(dst[:k, base[s] + lo - 128 * s : base[s] + lo - 128 * s + n], P2[h % 2][:n, i, 128 * s : 128 * s + k], n,
                             done if (i, s) == (2, 2) else None)

            def att_values(l, p):
                dst, done = take("pv", l, p)
                for h in (2 * p, 2 * p + 1):
                    banks.await_read(pe, ("att_turned", l, h))
                    row = dst[64 * (h % 2) : 64 * (h % 2) + 64, :]
                    for s, (lo, k) in enumerate(TOK1):
                        b = (0, T, T + T - 128)[s]
                        mm(row[:, lo:T], MV[:k, s, 64 * h : 64 * h + 64], PT2[h % 2][:k, b : b + T - lo], s == 0, s == 2,
                           done if (h % 2, s) == (1, 2) else None)

            def mix_out(l):
                for m in range(KT):
                    project(("mix_out", l, m), lambda k: MIX[:, k, :], ready=None if m else till("mixed", KT * l))

            def ff1(l, half):
                for m in range(FH * half, FH * half + FH):
                    project(("ff1", l, m), lambda k: (FN_HI[:, k, :], FN_LO[:, k, :]), ready=None if m else till("norm_split", KT * l))

            def ff2(l, half):
                for m in range(KT):
                    project(("ff2", l, half, m), lambda k: (F1_HI[:, k, :], F1_LO[:, k, :]), chunks=2,
                            ready=None if m else till("hidden_split", FT * l + FH * half))

            ht = lambda k: HT[:, k, :]
            ht_tok = lambda k, lo, n: HT[:, k, lo : lo + n]
            TOK2 = [(0, 128), (128, 128)]

            def ab_in():
                for name in ("aq", "ak"):
                    for j in range(4):
                        project((name, j), ht, 256, ready=lambda k: banks.await_read(pe, ("ff2", DEPTH - 1, 1, k)) if (name, j) == ("aq", 0) else None)
                tokens(("av",), ht_tok, TOK2)

            def bqk_in(j):
                project(("bqk", j), ht, 256)

            def bo_in(j):
                project(("bo", j), ht, 256)

            def bv_in():
                tokens(("bv",), ht_tok, TOK2)

            def if_in():
                at = PARAMS["wif"][0]
                for g in range(2):
                    dst, done = take("if", g)
                    for k in range(KT):
                        mm(dst[:4, :256], PAR[:, at + 8 * k + 4 * g : at + 8 * k + 4 * g + 4], ht(k), k == 0, k == 7, done if k == 7 else None)

            def gate_rows():
                pe.wait_ge(sem("gate_rows"), 1)
                dst, done = take("gate_cols")
                for i in range(2):
                    for a in range(2):
                        turn(dst[:, 8 * i + 4 * a : 8 * i + 4 * a + 4], ROWS[:4, 1 + a, 128 * i : 128 * i + 128], 4,
                             done if (i, a) == (1, 1) else None)

            def a_scores(h):
                if h == 0:
                    banks.await_read(pe, ("aq", 3))
                    banks.await_read(pe, ("ak", 3))
                rows = slice(64 * (h % 2), 64 * (h % 2) + 64)
                for i in range(2):
                    dst, done = take("a", h, i)
                    mm(dst[:, : 128 * i + 128], AQ[rows, h // 2, 128 * i : 128 * i + 128], AK[rows, h // 2, : 128 * i + 128], done=done)

            def turn_probs(key, ready, count, p):
                pe.wait_ge(sem(ready), count)
                dst, done = take(*key)
                for i, s, b in ((0, 0, 0), (1, 0, 128), (1, 1, 256)):
                    turn(dst[:, b : b + 128], p[:, i, 128 * s : 128 * s + 128], 128, done if s else None)

            def a_turn(h):
                turn_probs(("a_turned", h), "a_probs", h + 1, P[h % 2])

            def a_values(p):
                dst, done = take("a_pv", p)
                for h in (2 * p, 2 * p + 1):
                    banks.await_read(pe, ("a_turned", h))
                    row = dst[64 * (h % 2) : 64 * (h % 2) + 64, :]
                    mm(row[:, 0:256], AV[:, 0, 64 * h : 64 * h + 64], PT[h % 2][:, 0:256], True, False)
                    mm(row[:, 128:256], AV[:, 1, 64 * h : 64 * h + 64], PT[h % 2][:, 256:384], False, True, done if h % 2 else None)

            def b_scores(h):
                if h == 0:
                    pe.wait_ge(sem("bqk_ready"), 1)
                for i in range(2):
                    dst, done = take("b_row", h, i)
                    mm(dst[:, :256], ident(4)[:, h : h + 1].to_broadcast([4, 128]), ROWS[:4, 0, :], done=done)
                    dst, done = take("b", h, i)
                    mm(dst[:, : 128 * i + 128], BC[:, h, 128 * i : 128 * i + 128], BC[:, 4 + h, : 128 * i + 128], done=done)

            def b_turn(h):
                turn_probs(("b_turned", h), "b_weights", h + 1, P[2 + h % 2])

            def b_values(h):
                banks.await_read(pe, ("b_turned", h))
                dst, done = take("b_pv", h)
                mm(dst[:, 0:256], BV[:, 0, 128 * h : 128 * h + 128], PT[2 + h % 2][:, 0:256], True, False)
                mm(dst[:, 128:256], BV[:, 1, 128 * h : 128 * h + 128], PT[2 + h % 2][:, 256:384], False, True, done)

            def b_norm():
                for h in range(4):
                    banks.await_read(pe, ("b_pv", h))
                for g in range(2):
                    dst, done = take("b_mean", g)
                    mm(dst[:, :], ones(128, 128), YAB[:, 4 + 2 * g : 6 + 2 * g, :], done=done)
                pe.wait_ge(sem("b_squares"), 1)
                for g in range(2):
                    dst, done = take("b_var", g)
                    mm(dst[:, :], ones(128, 128), SQ[:, 512 * g : 512 * g + 512], done=done)

            def y_out(l):
                def ready(k):
                    if l:
                        banks.await_read(pe, ("c_pv", k))
                    elif k < 4:
                        banks.await_read(pe, ("a_pv", k))
                    else:
                        pe.wait_ge(sem("y_ready"), k - 3)

                for m in range(KT):
                    project(("y_out", l, m), lambda k: YAB[:, k, :], 256, ready=None if m else ready)

            def layer_norm(r):
                ready = till("moe_done", KT * (r // 2)) if r % 2 else lambda k: banks.await_read(pe, ("y_out", r // 2, k))
                column_sums(("ln_mean", r), ht, KT, 256, ready)
                column_sums(("ln_var", r), lambda k: sq(k, 256), KT, 256, till("ln_squares", KT * r))

            def router(l):
                pe.wait_ge(sem("ln_done"), KT * (2 * l + 1))
                at = PARAMS[f"router{l}"][0]
                for i in range(2):
                    dst, done = take("router", l, i)
                    mm(dst[:, :20], ones(1, 128), par(f"rbias{l}", 1), True, False)
                    for k in range(KT):
                        mm(dst[:, :20], ht_tok(k, 128 * i, 128), PAR[:, at + 20 * k : at + 20 * k + 20], False, k == 7, done if k == 7 else None)

            def expert_gates(l):
                pe.wait_ge(sem("expert_gates"), 2 * l + 2)
                dst, done = take("gates_turned", l)
                for i in range(2):
                    turn(dst[:16, 128 * i : 128 * i + 128], SM[:, 200 + 16 * i : 216 + 16 * i], 128, done if i else None)
                banks.await_read(pe, ("gates_turned", l))
                for e in range(NEXP):
                    dst, done = take("gate_row", l, e)
                    mm(dst[:, :256], ident(16)[:, e : e + 1].to_broadcast([16, 128]), GATT[:16, :], done=done)

            x_parts = lambda k: (X_HI[:, k, :], X_LO[:, k, :])

            def gate_up(key, ready=None):
                for j in range(4):
                    project((*key, "gate", j), x_parts, 256, ready=ready)
                    project((*key, "up", j), x_parts, 256)

            def down(key, buffer, count):
                half_projects((*key, "down"), lambda k: (HE_HI[:, buffer, k, :], HE_LO[:, buffer, k, :]), 256, ready=lambda k: pe.wait_ge(sem("hidden"), count + k + 1))

            def moe_first(l):
                gate_up(("moe", l, 0), till("x_split", KT * l))

            def moe(l):
                first = (4 * NEXP + 8) * l + 8
                with pe.Fori(0, NEXP // 2 - 1) as i:
                    state["loop"], banks.loop = i, 4 * i
                    for j in range(2):
                        gate_up(("moe", l, 1 + j))
                        down(("moe", l, j), j, first + 4 * j + 8 * i)
                        splits.marks["moe", l, j, "end"] = (len(splits.chunks), state["n"])
                state["loop"] = banks.loop = None
                for _ in range(MOE_CHUNKS * (NEXP // 2 - 2)):
                    splits.chunks.append(state["n"])
                    state["n"] += 1
                banks.uses = [n + 4 * (NEXP // 2 - 2) for n in banks.uses]
                gate_up(("moe", l, NEXP - 1))
                for e in (NEXP - 2, NEXP - 1):
                    down(("moe", l, e), e % 2, first + 4 * e)

            def c_in():
                for j in range(4):
                    project(("c_src", j), ht, 256, ready=None if j else till("ln_done", KT))
                for j in range(8):
                    project(("c_q", j), ht, 256)
                for j in range(4):
                    project(("c_k", j), ht, 256)
                tokens(("c_v",), ht_tok, TOK2)
                at = PARAMS["wcg"][0]
                for i in range(2):
                    dst, done = take("c_gate", i)
                    mm(dst[:, :24], ones(1, 128), par("cgbias", 1), True, False)
                    for k in range(KT):
                        mm(dst[:, :24], ht_tok(k, 128 * i, 128), PAR[:, at + 24 * k : at + 24 * k + 24], False, k == 7, done if k == 7 else None)

            def compress(s):
                pe.wait_ge(sem("blocks"), s + 1)
                dst, done = take("c_hidden", s)
                for c in range(8):
                    w = chunk()
                    for j in range(4):
                        n = 4 * c + j
                        mm(dst[:30, :256], BLK[:, n, :], w[:, 256 * j : 256 * j + 256], n == 0, n == 31, done if n == 31 else None)

            def compress2():
                w = chunk()
                for s in range(2):
                    pe.wait_ge(sem("c_gelu"), s + 1)
                    dst, done = take("c_hidden_turned", s)
                    for j in range(2):
                        turn(dst[:, 32 * j : 32 * j + 30], CHID[:30, 2 * s, 128 * j : 128 * j + 128], 30, done if j else None)
                    banks.await_read(pe, ("c_hidden_turned", s))
                    hid = CHID[:, 2 * s + 1, :]
                    for g in range(1 + s):
                        dst, done = take("c_cmp", s, g)
                        for j in range(2):
                            wt = w[:, 256 * s + 128 * j : 256 * s + 128 * j + 128]
                            if s == 0:
                                mm(dst[:, :30], wt, hid[:, 32 * j : 32 * j + 30], j == 0, j == 1, done if j else None)
                            else:
                                mm(dst[:15, :128], hid[:, 32 * j + 15 * g : 32 * j + 15 * g + 15], wt, j == 0, j == 1, done if j else None)

            def c_scores(h):
                g = h // 4
                if h == 0:
                    for key in (("c_q", 7), ("c_k", 3), ("c_cmp", 0, 0), ("c_cmp", 1, 1)):
                        banks.await_read(pe, key)
                for i in range(2):
                    q = AQ[:, h, 128 * i : 128 * i + 128]
                    for b in range(2):
                        dst, done = take("c", h, i, b)
                        mm(dst[:, : 128 * i + 128], q, AK[:, 2 * b + g, : 128 * i + 128], done=done)
                dst, done = take("c_c", h)
                for i in range(2):
                    mm(dst[:, 16 * i : 16 * i + 15], AQ[:, h, 128 * i : 128 * i + 128], KC[:, 15 * g : 15 * g + 15], done=done if i else None)

            def c_turn(h):
                for b in range(2):
                    turn_probs(("c_turned", h, b), "c_probs", 3 * h + b + 1, P[2 * (h % 2) + b])
                pe.wait_ge(sem("c_probs"), 3 * h + 3)
                dst, done = take("c_turned", h, 2)
                for i in range(2):
                    turn(dst[:15, 128 * i : 128 * i + 128], PC[h % 2][:, i, :15], 128, done if i else None)

            def c_values(h):
                g = h // 4
                dst, done = take("c_pv", h)
                for b in range(2):
                    banks.await_read(pe, ("c_turned", h, b))
                    v = 256 * b + 128 * g
                    mm(dst[:, 0:256], AV[:, 0, v : v + 128], PT[2 * (h % 2) + b][:, 0:256], b == 0, False)
                    mm(dst[:, 128:256], AV[:, 1, v : v + 128], PT[2 * (h % 2) + b][:, 256:384], False, False)
                banks.await_read(pe, ("c_turned", h, 2))
                mm(dst[:, 0:256], VC[:15, g, :], PCT[h % 2][:15, :], False, True, done)

            steps = locals()
            for name, *args in SCHEDULE:
                if name in steps:
                    steps[name](*args)
                splits.marks["step", name, *args] = (len(splits.chunks), state["n"])
            splits.known = frozenset(splits.chunks)
            assert state["n"] == n_chunks, (state["n"], n_chunks)

        def bc(ap, shape):
            return ap.to_broadcast(shape)

        SCALE_MLA = QK ** -0.5

        @block.scalar
        def _(act):
            lane = Lane(act, sem("scalar_step"))
            loop = {"v": None, "i": None}

            def split(s, n):
                i = loop["i"]
                value = 16 * (n // RING + 1)
                act.wait_ge(arrived[n % RING], value if i is None else value + 16 * (MOE_CHUNKS // RING) * i)
                if s >= SPLIT:
                    act.wait_ge(split_used, s - SPLIT + 1 if i is None else s - SPLIT + 1 + MOE_CHUNKS * i)
                lane(nc.scalar.activation(W_HI[:, s % SPLIT, :], ring[:, n % RING, :], ACT.Copy), split_hi)

            follow = Follower(splits, split)

            def fn(dst, src, f, sem_=None, **kw):
                lane(nc.scalar.activation(dst, src, f, **kw), sem_)

            def fn_free(dst, src, f, key, **kw):
                nc.scalar.activation(dst, src, f, **kw).then_inc(banks.freed(key), 1)
                banks.await_read(act, key, loop["v"])
                follow(key)

            def wait_bank(*key):
                return banks.await_(act, key, loop["v"])

            def evacuate(key, dst, n=T, f=ACT.Copy, rows=128, **kw):
                fn_free(dst, wait_bank(*key)[:rows, :n], f, key, **kw)

            def root(ap):
                fn(ap, ap, ACT.Sqrt, sem("root"))

            def start():
                act.wait_ge(sem("lower_bound_args"), 1)
                fn(ST[:, 8:16], ST[:, 8:16], ACT.Exp, sem("lower_bound_exps"))

            def hankel():
                wait_bank("norm", 2 * DEPTH - 1)
                hankel_ = bass.AP(scratch.tensor, 0, [[1, 128], [384, HEADS], [1, 256]])
                act.dma_start(SQ[:, : 8 * 256].rearrange("p (h c) -> p h c", h=8), hankel_).then_inc(sem("hankel"), 16)

            def store_bias():
                banks.await_read(act, ("bucket_bias",))
                act.dma_start(scratch, MIX[:HEADS, 0:2, :].rearrange("p a b -> p (a b)")[:, :384]).then_inc(sem("bias_stored"), 16)
                act.wait_ge(sem("bias_stored"), 16)

            def norm(r):
                if r == 0:
                    act.wait_ge(sem("loaded"), 48)
                for k in range(KT):
                    if r % 2:
                        banks.await_read(act, ("mix_out", r // 2, k))
                    elif r:
                        banks.await_read(act, ("ff2", r // 2 - 1, 1, k))
                    fn(SQ[:, T * k : T * k + T], XT[:, k, :], ACT.Square, sem("norm_squares"))
                banks.await_read(act, ("norm", r))
                root(RS[:, :T])

            def conv_in(l):
                for j in range(4):
                    evacuate(("conv_g", l, j), MIX[:, j, :], f=ACT.Sigmoid)

            def hgrn_in(l):
                for j in range(4):
                    evacuate(("hf", l, j), HK[:, j, :T], f=ACT.Sigmoid, scale=-1.0)
                for j in range(4):
                    evacuate(("hq", l, j), HQ[:, j, :T])
                for j in range(4):
                    evacuate(("hg", l, j), HG[:, j, :], f=ACT.Silu)
                for i, (_, n) in enumerate(TOK1):
                    evacuate(("hi", l, i), HV[:n, i, :], 512, ACT.Silu, n)

            def mla_in(l):
                for j in range(2):
                    src = wait_bank("cq", l, j)
                    fn(SQ[:, T * (4 + j) : T * (5 + j)], src[:, :T], ACT.Square, sem("latent_squares") if j else None)
                    fn_free(CQ[:, j, :], src[:, :T], ACT.Copy, ("cq", l, j))
                src = wait_bank("ckv", l)
                fn(SQ[:, T * 6 : T * 7], src[:, :T], ACT.Square, sem("latent_squares"))
                fn_free(CKV[:, :], src[:, :T], ACT.Copy, ("ckv", l))
                fn_free(KR[NOPE:QK, :], wait_bank("rope", l)[NOPE:QK, :T], ACT.Copy, ("rope", l))

            def gate(l, b, m):
                if b == 2:
                    banks.await_read(act, ("branch", l, 0, m))
                elif l:
                    act.wait_ge(sem(("mixed", "gated")[b]), KT * (l - 1) + m + 1)
                evacuate(("gate", l, b, m), GATES[b % 2][:, m, :], f=ACT.Sigmoid)

            def conv_norm(l):
                act.wait_ge(sem("conv_centered"), l + 1)
                fn(SQ[:, : 4 * T], CO[:, :, :].rearrange("p k t -> p (k t)"), ACT.Square, sem("conv_squares"))
                banks.await_read(act, ("conv_var", l))
                root(RS[:, :T])
                act.wait_ge(sem("conv_scaled"), l + 1)
                for j in range(4):
                    fn(CO[:, j, :], CO[:, j, :], ACT.Silu, sem("conv_done"),
                       scale=par(f"clng{l}")[:, j : j + 1], bias=par(f"clnb{l}")[:, j : j + 1])

            def hgrn_prep(l):
                act.wait_ge(sem("clamped"), l + 1)
                fn(HB[:, :, :T], HB[:, :, :T], ACT.Ln, sem("logs"), scale=-1.0, bias=1.0)
                act.wait_ge(sem("strip_args"), l + 1)
                fn(HKK[:, :, :], HKK[:, :, :], ACT.Exp, sem("strip_exps"))

            def hgrn_args(l, i):
                act.wait_ge(sem("decay_args"), NB * l + i + 1)
                n = 1024 + 4 * SB * i
                fn(HD[i % 2][:, :n], HD[i % 2][:, :n], ACT.Exp, sem("decay_exps"))

            def hgrn_turn(l, i):
                n = -(-SB * (i + 1) // 128)
                src = wait_bank("turned", l, i)[:, : 128 * n].rearrange("p (s h t) -> p s h t", s=n, h=4)
                fn_free(HAT[:, :n, :, SB * i : SB * i + SB], src, ACT.Copy, ("turned", l, i))

            def hgrn_values(l):
                for h in range(4):
                    evacuate(("ho", l, h), HO[:, h, :T])
                fn(SQ[:, : 4 * T].rearrange("p (h t) -> p h t", h=4), HO[:, :, :T], ACT.Square, sem("hgrn_squares"))

            def hgrn_norm(l):
                banks.await_read(act, ("hgrn_var", l, 3))
                root(HR)

            def mla_norm(l):
                for key in ("cq_var", "ckv_var"):
                    banks.await_read(act, (key, l))
                    root(RS[:, :T])

            def mla_up(l):
                for h in range(HEADS):
                    evacuate(("q", l, h), QH[:QK, h, :], rows=QK)
                fn(KH[NOPE:QK, :, :], bc(KR[NOPE:QK, None, :], [ROPE, HEADS, T]), ACT.Copy)
                for h in range(HEADS):
                    evacuate(("k", l, h), KH[:NOPE, h, :], rows=NOPE)
                for i, (_, n) in enumerate(TOK1):
                    evacuate(("v", l, i), MV[:n, i, :], 512, rows=n)

            def head_norm(l, which):
                src = (QH, KH)[which][:QK, :, :].rearrange("p h t -> p (h t)")
                if which:
                    wait_bank("head_var", l, 0, HEADS - 1)
                fn(SQ[:QK, : HEADS * T], src, ACT.Square, sem("head_squares"))
                banks.await_read(act, ("head_var", l, which, HEADS - 1))
                root(RSQ[:QK, :, :])

            def att_scores(l, h):
                act.wait_ge(sem("att_max"), HEADS * l + h + 1)
                s = 16 * (h % 2)
                for i, (lo, n) in enumerate(TOK1):
                    p = P2[h % 2][:n, i, : lo + n]
                    fn(p, p, ACT.Exp, sem("att_exps"), scale=SCALE_MLA, bias=SM[:n, s + 4 + i : s + 5 + i], accum_out=SM[:n, s + 8 + i : s + 9 + i])

            def att_turn(l, h):
                src = wait_bank("att_turned", l, h)
                if h >= 2:
                    wait_bank("pv", l, h // 2 - 1)
                n = T + T - 128
                fn(PT2[h % 2][:, :n], src[:, :n], ACT.Copy)
                fn_free(PT2[h % 2][:16, n : n + 16], src[:16, n : n + 16], ACT.Copy, ("att_turned", l, h))

            def att_values(l, p):
                evacuate(("pv", l, p), OT[:, p, :])

            def ff1(l, half):
                for m in range(FH * half, FH * half + FH):
                    if FT * l + m >= 4:
                        act.wait_ge(sem("hidden_split"), FT * l + m - 3)
                    evacuate(("ff1", l, m), F1[:, m % 4, :], f=ACT.Relu)

            def ff2(l, half):
                for m in range(KT):
                    wait_bank("ff2", l, half, m)
                    follow(("ff2", l, half, m))

            def ab_in():
                for j in range(4):
                    evacuate(("aq", j), AQ[:, j, :], 256, scale=A_SCALE)
                for j in range(4):
                    evacuate(("ak", j), AK[:, j, :], 256)
                for i in range(2):
                    evacuate(("av", i), AV[:, i, :], 512)

            def bqk_in(j):
                evacuate(("bqk", j), BIN[:, j, 3:259], 256)

            def bv_in():
                for i in range(2):
                    evacuate(("bv", i), BV[:, i, :], 512)

            def bo_in(j):
                evacuate(("bo", j), SBO[:, j, :], 256, ACT.Sigmoid)

            def b_gates():
                act.wait_ge(sem("forget_abs"), 1)
                fn(ROWS[:4, 5, :], ROWS[:4, 5, :], ACT.Exp, scale=-1.0)
                fn(ROWS[:4, 5, :], ROWS[:4, 5, :], ACT.Ln, sem("forget_logs"), bias=1.0)

            def gate_rows():
                banks.await_read(act, ("gate_cols",))
                floors = COLS[:, :].rearrange("p (i c) -> p i c", i=2)[:, :, 4:8]
                fn(floors, floors, ACT.Exp, sem("floors"))

            def b_conv():
                act.wait_ge(sem("b_convolved"), 1)
                fn(BC[:, :, :], BC[:, :, :], ACT.Silu, sem("b_silu"))

            def a_scores(h):
                act.wait_ge(sem("a_max"), h + 1)
                s = 32 + 16 * (h % 2)
                for i in range(2):
                    p = P[h % 2][:, i, : 128 * i + 128]
                    fn(p, p, ACT.Exp, sem("a_exps"), bias=SM[:, s + 4 + i : s + 5 + i], accum_out=SM[:, s + 8 + i : s + 9 + i])

            def turned(key, dst, before):
                src = wait_bank(*key)
                if before is not None:
                    wait_bank(*before)
                fn_free(dst[:, :384], src[:, :384], ACT.Copy, key)

            def a_turn(h):
                turned(("a_turned", h), PT[h % 2], ("a_pv", h // 2 - 1) if h >= 2 else None)

            def a_values(p):
                evacuate(("a_pv", p), YAB[:, p, :], 256)

            def b_scores(h):
                if h == 0:
                    act.wait_ge(sem("floors"), 1)
                for i in range(2):
                    act.wait_ge(sem("b_masked"), 2 * h + i + 1)
                    p = P[2 + h % 2][:, i, : 128 * i + 128]
                    fn(p, p, ACT.Exp, sem("b_exps"), bias=COLS[:, 8 * i + h : 8 * i + h + 1])

            def b_turn(h):
                turned(("b_turned", h), PT[2 + h % 2], ("b_pv", h - 2) if h >= 2 else None)

            def b_values(h):
                evacuate(("b_pv", h), YAB[:, 4 + h, :], 256)

            def b_norm():
                act.wait_ge(sem("b_centered"), 1)
                fn(SQ[:, :1024], YAB[:, 4:8, :].rearrange("p h t -> p (h t)"), ACT.Square, sem("b_squares"))
                banks.await_read(act, ("b_var", 1))
                root(AQ[:, 0:4, :])

            def layer_norm(r):
                for k in range(KT):
                    act.wait_ge(sem("ln_centered"), KT * r + k + 1)
                    fn(SQ[:, 256 * k : 256 * k + 256], HT[:, k, :], ACT.Square, sem("ln_squares"))
                banks.await_read(act, ("ln_var", r))
                root(RS[:, :256])
                l, j = r // 2, r % 2
                for k in range(KT):
                    act.wait_ge(sem("ln_scaled"), KT * r + k + 1)
                    fn(HT[:, k, :], HT[:, k, :], ACT.Identity, sem("ln_done"),
                       scale=par(f"lng{j}_{l}")[:, k : k + 1], bias=par(f"lnb{j}_{l}")[:, k : k + 1])

            def router(l):
                for i in range(2):
                    act.wait_ge(sem("group_max"), l + 1)
                    s = RT[:, 56 + 4 * i : 60 + 4 * i]
                    fn(s, RT[:, 20 * i : 20 * i + 4], ACT.Exp, sem("group_exps"), bias=RT[:, 42 + i : 43 + i], accum_out=RT[:, 44 + i : 45 + i])
                act.wait_ge(sem("top_gap"), l + 1)
                fn(RT[:, 46:48], RT[:, 46:48], ACT.Exp, sem("top_exps"))

            def expert_gates(l):
                evacuate(("gates_turned", l), GATT[:16, :], 256, rows=16)
                for e in range(NEXP):
                    evacuate(("gate_row", l, e), GB[:, e, :], 256)

            def silu_gates(key, j, loop_):
                for t in range(4):
                    act.wait_ge(sem("hidden"), j + t + 1 if loop_ is None else j + t + 1 + loop_)
                    evacuate((*key, "gate", t), SGM[:, t, :], 256, ACT.Silu)
                    follow((*key, "up", t))

            def moe_first(l):
                silu_gates(("moe", l, 0), (4 * NEXP + 8) * l + 4, None)

            def moe(l):
                first = (4 * NEXP + 8) * l + 8
                with act.Fori(0, NEXP // 2 - 1) as i:
                    loop["v"], loop["i"] = 4 * i, i
                    lane.enter(i, {"split_hi": MOE_CHUNKS})
                    for j in range(2):
                        silu_gates(("moe", l, 1 + j), first + 4 * j, 8 * i)
                        follow(("moe", l, j, "end"))
                    lane.leave(NEXP // 2 - 1)
                loop["v"] = loop["i"] = None
                follow.next += MOE_CHUNKS * (NEXP // 2 - 2)
                silu_gates(("moe", l, NEXP - 1), first + 4 * (NEXP - 2), None)

            def c_in():
                for j in range(4):
                    evacuate(("c_src", j), BIN[:, j, :256], 256)
                for j in range(8):
                    evacuate(("c_q", j), AQ[:, j, :], 256, scale=C_SCALE)
                for j in range(4):
                    evacuate(("c_k", j), AK[:, j, :], 256)
                for i in range(2):
                    evacuate(("c_v", i), AV[:, i, :], 512)
                for i in range(2):
                    evacuate(("c_gate", i), CG[:, i, :], 24, ACT.Sigmoid)

            def compress(s):
                src = wait_bank("c_hidden", s)
                fn(CHID[:30, 2 * s, :], src[:30, :256], ACT.Gelu_apprx_tanh, sem("c_gelu"))

            def compress2():
                for s in range(2):
                    src = wait_bank("c_hidden_turned", s)[:, :64].rearrange("p (j n) -> p j n", j=2)[:, :, :30]
                    fn_free(CHID[:, 2 * s + 1, :64].rearrange("p (j n) -> p j n", j=2)[:, :, :30], src, ACT.Copy, ("c_hidden_turned", s))
                    for g in range(1 + s):
                        if s == 0:
                            evacuate(("c_cmp", s, g), KC[:, :], 30)
                        else:
                            evacuate(("c_cmp", s, g), VC[:15, g, :], 128, rows=15)

            def c_scores(h):
                act.wait_ge(sem("c_max"), h + 1)
                s = 64 + 20 * (h % 2)
                for b in range(3):
                    for i in range(2):
                        p = PC[h % 2][:, i, : 7 + 8 * i] if b == 0 else P[2 * (h % 2) + b - 1][:, i, : 128 * i + 128]
                        c = 2 * b + i
                        fn(p, p, ACT.Exp, sem("c_exps"), bias=SM[:, s + 6 + c : s + 7 + c], accum_out=SM[:, s + 12 + c : s + 13 + c])

            def c_turn(h):
                before = ("c_pv", h - 2) if h >= 2 else None
                for b in range(2):
                    turned(("c_turned", h, b), PT[2 * (h % 2) + b], before)
                evacuate(("c_turned", h, 2), PCT[h % 2][:15, :], 256, rows=15)

            def c_values(h):
                evacuate(("c_pv", h), YAB[:, h, :], 256)

            steps = locals()
            for name, *args in SCHEDULE:
                if name in steps:
                    steps[name](*args)
                follow(("step", name, *args))

        @block.vector
        def _(dve):
            lane = Lane(dve, sem("vector_step"))
            loop = {"v": None, "i": None}

            def split(s, n):
                i = loop["i"]
                dve.wait_ge(split_hi, s + 1 if i is None else s + 1 + MOE_CHUNKS * i)
                lane(nc.vector.tensor_tensor(W_LO[:, s % SPLIT, :], ring[:, n % RING, :], W_HI[:, s % SPLIT, :].bitcast(F32), ALU.subtract), split_lo)

            follow = Follower(splits, split)
            roots = [0]

            def tt(dst, a, b, op, done=None):
                lane(nc.vector.tensor_tensor(dst, a, b, op), done)

            def ts(dst, a, s1, s2, op0, op1=None, done=None):
                ins = nc.vector.tensor_scalar(dst, a, s1, s2, op0) if op1 is None else nc.vector.tensor_scalar(dst, a, s1, s2, op0, op1)
                lane(ins, done)

            def stt(dst, a, s, b, op0, op1, done=None):
                lane(nc.vector.scalar_tensor_tensor(dst, a, s, b, op0, op1), done)

            def ttr(dst, a, b, op0, op1, init, acc, done=None):
                lane(nc.vector.tensor_tensor_reduce(dst, a, b, 1.0, init, op0, op1, acc), done)

            def wait_bank(*key):
                return banks.await_(dve, key, loop["v"])

            def free(ins, *key):
                ins.then_inc(banks.freed(key), 1)
                banks.await_read(dve, key, loop["v"])
                follow(key)

            def mean_eps(key, dst, n, count, eps, rows=128):
                src = wait_bank(*key)
                free(nc.vector.tensor_scalar(dst, src[:rows, :n], 1.0 / count, eps, ALU.mult, ALU.add), *key)

            def reciprocal_root(ap):
                roots[0] += 1
                dve.wait_ge(sem("root"), roots[0])
                lane(nc.vector.reciprocal(ap, ap))

            def zeros():
                lane(nc.vector.memset(HC[:, :, : CONV_K - 1], 0.0))
                for t in (HB, HK, HQ):
                    lane(nc.vector.memset(t[:, :, T:TP], 0.0))

            def start():
                zeros()
                lane(nc.vector.memset(SM[:, :], 0.0))
                dve.wait_ge(sem("loaded"), 48)
                l0, l1 = par("lb0"), par("lb1")
                tt(ST[:, 16:20], l0, l1, ALU.max)
                tt(ST[:, 8:12], l0, ST[:, 16:20], ALU.subtract)
                tt(ST[:, 12:16], l1, ST[:, 16:20], ALU.subtract, sem("lower_bound_args"))
                dve.wait_ge(sem("lower_bound_exps"), 1)
                tt(ST[:, 16:20], ST[:, 8:12], ST[:, 12:16], ALU.add)
                lane(nc.vector.reciprocal(ST[:, 16:20], ST[:, 16:20]))
                tt(ST[:, 8:12], ST[:, 8:12], ST[:, 16:20], ALU.mult)
                tt(ST[:, 12:16], ST[:, 12:16], ST[:, 16:20], ALU.mult)
                tt(ST[:, 12:16], ST[:, 8:12], ST[:, 12:16], ALU.add)
                tt(ST[:, 20:24], ST[:, 8:12], ST[:, 8:12], ALU.subtract)
                tt(ST[:, 24:28], ST[:, 12:16], ST[:, 8:12], ALU.subtract)
                ts(ST[:, 0:8], ST[:, 20:28], -1.0, 1.0, ALU.mult, ALU.add)
                src = wait_bank("bucket_bias")
                flat = MIX[:HEADS, 0:2, :].rearrange("p a b -> p (a b)")[:, :384]
                free(nc.vector.tensor_copy(flat, src[:HEADS, :384]), "bucket_bias")

            def bias():
                for g in range(4):
                    src = wait_bank("bias", g)[:, :].rearrange("p (h c) -> p h c", h=2)
                    mask = bc(cst("causal", 128, 256)[:, None, :], [128, 2, 256])
                    count = bc(cst("logcount")[:, None, :], [128, 2, 256])
                    tt(BIAS_C[:, 2 * g : 2 * g + 2, :], src, mask, ALU.add)
                    free(nc.vector.tensor_tensor(BIAS_A[:, 2 * g : 2 * g + 2, :], src, count, ALU.add), "bias", g)

            def norm(r):
                mean_eps(("norm", r), RS[:, :T], T, D, EPS)
                reciprocal_root(RS[:, :T])
                g = par(f"norm{1 + r % 2}{r // 2}")
                for k in range(KT):
                    stt(HN[:, k, :], XT[:, k, :], g[:, k : k + 1], RS[:, :T], ALU.mult, ALU.mult, None if r % 2 else sem("normed"))
                    if r % 2:
                        lane(nc.vector.tensor_copy(FN_HI[:, k, :], HN[:, k, :]))
                        tt(FN_LO[:, k, :], HN[:, k, :], FN_HI[:, k, :].bitcast(F32), ALU.subtract, sem("norm_split"))
                if r == 2:
                    zeros()

            def conv_in(l):
                for j in range(4):
                    src = wait_bank("conv_a", l, j)
                    banks.await_read(dve, ("conv_g", l, j))
                    free(nc.vector.tensor_tensor(HC[:, j, CONV_K - 1 :], src[:, :T], MIX[:, j, :], ALU.mult), "conv_a", l, j)

            def conv_taps(l):
                w, b = par(f"convw{l}"), par(f"convb{l}")
                for j in range(4):
                    for i in range(CONV_K):
                        x, wi = HC[:, j, i : i + T], w[:, CONV_K * j + i : CONV_K * j + i + 1]
                        if i == 0:
                            ts(CO[:, j, :], x, wi, b[:, j : j + 1], ALU.mult, ALU.add)
                        else:
                            stt(CO[:, j, :], x, wi, CO[:, j, :], ALU.mult, ALU.add, sem("conv_out") if (i, j) == (CONV_K - 1, 3) else None)

            def conv_norm(l):
                mean_eps(("conv_mean", l), MU[:, :T], T, 512, 0.0)
                tt(CO[:, :, :], CO[:, :, :], bc(MU[:, None, :T], [128, 4, T]), ALU.subtract, sem("conv_centered"))
                mean_eps(("conv_var", l), RS[:, :T], T, 512, EPS)
                reciprocal_root(RS[:, :T])
                tt(CO[:, :, :], CO[:, :, :], bc(RS[:, None, :T], [128, 4, T]), ALU.mult, sem("conv_scaled"))

            def branch_out(l, b, c):
                gate_ = GATES[b % 2]
                for m in (2 * c, 2 * c + 1):
                    src = wait_bank("branch", l, b, m)
                    banks.await_read(dve, ("gate", l, b, m))
                    free(nc.vector.tensor_tensor((gate_ if b else MIX)[:, m, :], src[:, :T], gate_[:, m, :], ALU.mult), "branch", l, b, m)
                    if b:
                        tt(MIX[:, m, :], MIX[:, m, :], gate_[:, m, :], ALU.add, sem(("gated", "mixed")[b - 1]))

            def hgrn_prep(l):
                for j in range(4):
                    banks.await_read(dve, ("hf", l, j))
                    ts(HK[:, j, :T], HK[:, j, :T], ST[:, 4 * l + j : 4 * l + j + 1], None, ALU.mult)
                ts(HB[:, :, :T], HK[:, :, :T], CLAMP, None, ALU.min, done=sem("clamped"))
                for a in HA:
                    lane(nc.vector.memset(a, 0.0))
                if l:
                    lane(nc.vector.memset(HB[:, :, T:TP], 0.0))
                dve.wait_ge(sem("logs"), l + 1)
                one = bc(cst("ones", 0, 1), [128, TP])
                for j in range(4):
                    lane(nc.vector.tensor_tensor_scan(HB[:, j, :], one, HB[:, j, :], 0.0, ALU.mult, ALU.add), sem("summed") if j == 3 else None)
                s4 = HB[:, :, :].rearrange("p h (g f) -> p (h g) f", f=SS)
                k4 = HKK[:, :, :].rearrange("p h (g f) -> p (h g) f", f=SS)
                tt(k4, bc(s4[:, :, 0:1], [128, 4 * TP // SS, SS]), s4, ALU.subtract, sem("strip_args"))
                dve.wait_ge(sem("strip_exps"), l + 1)
                tt(HKK[:, :, :], HKK[:, :, :], HK[:, :, :], ALU.mult)
                banks.await_read(dve, ("hq", l, 3))

            def hgrn_args(l, i):
                dve.wait_ge(sem("decay_exps"), NB * l + i + 1)
                d = HD[i % 2]
                qq = d[:, :1024].rearrange("p (j h t) -> p j h t", j=8, h=4)
                q = bc(HQ[:, None, :, SB * i : SB * i + SB], [128, 8, 4, SB])
                tt(qq, qq, q, ALU.mult, None if i else sem("decayed"))
                if i:
                    n = SB * i
                    kk = d[:, 1024 : 1024 + 4 * n].rearrange("p (h s) -> p h s", h=4)
                    tt(kk, kk, HK[:, :, :n], ALU.mult, sem("decayed"))

            def hgrn_block(l, i):
                src = wait_bank("scores", l, i)
                if i >= 2:
                    wait_bank("turned", l, i - 2)
                n = SB * i
                if i:
                    lane(nc.vector.tensor_copy(HA[i % 2][:, :n], src[:, :n]))
                free(nc.vector.tensor_tensor(HA[i % 2][:, n : n + SB], src[:, n : n + SB], cst("tri"), ALU.mult), "scores", l, i)

            def hgrn_norm(l):
                for h in range(4):
                    mean_eps(("hgrn_var", l, h), HR[:, h, :], T, 128, EPS)
                reciprocal_root(HR)
                tt(HO[:, :, :T], HO[:, :, :T], HR, ALU.mult)
                for h in range(4):
                    stt(HO[:, h, :T], HO[:, h, :T], par(f"hn{l}")[:, h : h + 1], HG[:, h, :], ALU.mult, ALU.mult, sem("hgrn_done"))

            def mla_norm(l):
                mean_eps(("cq_var", l), RS[:, :T], T, 256, EPS)
                reciprocal_root(RS[:, :T])
                for k in range(2):
                    stt(CQ[:, k, :], CQ[:, k, :], par(f"qa{l}")[:, k : k + 1], RS[:, :T], ALU.mult, ALU.mult, sem("latents") if k else None)
                mean_eps(("ckv_var", l), RS[:, :T], T, 128, EPS)
                reciprocal_root(RS[:, :T])
                stt(CKV[:, :], CKV[:, :], par(f"kva{l}"), RS[:, :T], ALU.mult, ALU.mult, sem("latents"))

            def head_norm(l, which):
                x = (QH, KH)[which]
                for h in range(HEADS):
                    mean_eps(("head_var", l, which, h), RSQ[:QK, h, :], T, QK, EPS, QK)
                reciprocal_root(RSQ[:QK, :, :])
                flat = lambda a: a[:QK, :, :].rearrange("p h t -> p (h t)")
                stt(flat(x), flat(x), par(f"{'qk'[which]}n{l}", QK), flat(RSQ), ALU.mult, ALU.mult)
                r = slice(NOPE, QK)
                half = ROPE // 2
                shape = [ROPE, HEADS, T]
                c, s = CONSTS["cos"][0], CONSTS["sin"][0]
                lane(nc.vector.stream_shuffle(RSQ[r, :, :], x[r, :, :], [(i + half) % ROPE for i in range(ROPE)]))
                tt(RSQ[r, :, :], RSQ[r, :, :], bc(CST[r, None, s : s + T], shape), ALU.mult)
                tt(x[r, :, :], x[r, :, :], bc(CST[r, None, c : c + T], shape), ALU.mult)
                tt(x[r, :, :], x[r, :, :], RSQ[r, :, :], ALU.add, sem("heads_ready"))

            def att_scores(l, h):
                s = 16 * (h % 2)
                for i, (lo, n) in enumerate(TOK1):
                    src = wait_bank("att", l, h, i)
                    if i == 0 and h >= 2:
                        wait_bank("att_turned", l, h - 2)
                    ins = nc.vector.tensor_tensor_reduce(P2[h % 2][:n, i, : lo + n], src[:n, : lo + n], cst("causal", 256 - lo, lo + n)[:n, :],
                                                         1.0, NEG, ALU.add, ALU.max, SM[:n, s + i : s + i + 1])
                    free(ins, "att", l, h, i)
                ts(SM[:, s + 4 : s + 7], SM[:, s : s + 3], -SCALE_MLA, None, ALU.mult, done=sem("att_max"))

            def att_norm(l, h):
                s = 16 * (h % 2)
                dve.wait_ge(sem("att_exps"), 3 * (HEADS * l + h + 1))
                lane(nc.vector.reciprocal(SM[:128, s + 12 : s + 14], SM[:, s + 8 : s + 10]))
                lane(nc.vector.reciprocal(SM[:16, s + 14 : s + 15], SM[:16, s + 10 : s + 11]))
                for i, (lo, n) in enumerate(TOK1):
                    p = P2[h % 2][:n, i, : lo + n]
                    ts(p, p, SM[:n, s + 12 + i : s + 13 + i], None, ALU.mult, done=sem("att_probs") if i == 2 else None)

            def mix_out(l):
                for m in range(KT):
                    src = wait_bank("mix_out", l, m)
                    free(nc.vector.tensor_tensor(XT[:, m, :], src[:, :T], XT[:, m, :], ALU.add), "mix_out", l, m)

            def ff1(l, half):
                for m in range(FH * half, FH * half + FH):
                    follow(("ff1", l, m))
                    dve.wait_ge(sem("squared"), FT * l + m + 1)
                    j = m % FH
                    lane(nc.vector.tensor_copy(F1_HI[:, j, :], F1[:, m % 4, :]))
                    tt(F1_LO[:, j, :], F1[:, m % 4, :], F1_HI[:, j, :].bitcast(F32), ALU.subtract, sem("hidden_split"))

            def ff2(l, half):
                for m in range(KT):
                    src = wait_bank("ff2", l, half, m)
                    free(nc.vector.tensor_tensor(XT[:, m, :], src[:, :T], XT[:, m, :], ALU.add), "ff2", l, half, m)

            def b_gates():
                for row, g, name in ((4, 0, "ibias"), (3, 1, "fbias")):
                    src = wait_bank("if", g)
                    free(nc.vector.tensor_scalar(ROWS[:4, row, :], src[:4, :256], par(name, 4), None, ALU.add), "if", g)
                stt(ROWS[:4, 5, :], ROWS[:4, 3, :], -1.0, ROWS[:4, 3, :], ALU.mult, ALU.max, sem("forget_abs"))
                dve.wait_ge(sem("forget_logs"), 1)
                stt(ROWS[:4, 6, :], ROWS[:4, 3, :], 0.0, ROWS[:4, 5, :], ALU.min, ALU.subtract)
                lane(nc.vector.tensor_tensor_scan(ROWS[:4, 7, :], bc(cst("ones", 0, 1, 4), [4, 256]), ROWS[:4, 6, :], 0.0, ALU.mult, ALU.add))
                tt(ROWS[:4, 0, :], ROWS[:4, 4, :], ROWS[:4, 7, :], ALU.subtract)
                lane(nc.vector.tensor_tensor_scan(ROWS[:4, 1, :], ROWS[:4, 0, :], ROWS[:4, 0, :], 0.0, ALU.max, ALU.max))
                tt(ROWS[:4, 2, :], ROWS[:4, 7, :], ROWS[:4, 1, :], ALU.add)
                ts(ROWS[:4, 1:3, :], ROWS[:4, 1:3, :], -1.0, None, ALU.mult, done=sem("gate_rows"))

            def gate_rows():
                src = wait_bank("gate_cols")
                free(nc.vector.tensor_copy(COLS[:, :], src[:, :16]), "gate_cols")

            def b_conv():
                dve.wait_ge(sem("b_padding"), 1)
                w = par("abconv")
                for j in range(8):
                    banks.await_read(dve, ("bqk", j))
                    for i in range(4):
                        x, wi = BIN[:, j, i : i + 256], w[:, 4 * j + i : 4 * j + i + 1]
                        if i == 0:
                            ts(BC[:, j, :], x, wi, None, ALU.mult)
                        else:
                            stt(BC[:, j, :], x, wi, BC[:, j, :], ALU.mult, ALU.add, sem("b_convolved") if (i, j) == (3, 7) else None)
                dve.wait_ge(sem("b_silu"), 1)
                ts(BC[:, 0:4, :], BC[:, 0:4, :], C_SCALE, None, ALU.mult, done=sem("bqk_ready"))

            def masked_max(key, p, src, bias_, acc, first=None):
                if first is not None:
                    wait_bank(*first)
                lane(nc.vector.tensor_tensor_reduce(p, src, bias_, 1.0, NEG, ALU.add, ALU.max, acc))

            def a_scores(h):
                s = 32 + 16 * (h % 2)
                for i in range(2):
                    src = wait_bank("a", h, i)
                    if i == 0 and h >= 2:
                        wait_bank("a_turned", h - 2)
                    ins = nc.vector.tensor_tensor_reduce(P[h % 2][:, i, : 128 * i + 128], src[:, : 128 * i + 128], BIAS_A[:, h, 128 - 128 * i :],
                                                         1.0, NEG, ALU.add, ALU.max, SM[:, s + i : s + i + 1])
                    free(ins, "a", h, i)
                ts(SM[:, s + 4 : s + 6], SM[:, s : s + 2], -1.0, None, ALU.mult, done=sem("a_max"))

            def a_norm(h):
                s = 32 + 16 * (h % 2)
                dve.wait_ge(sem("a_exps"), 2 * (h + 1))
                lane(nc.vector.reciprocal(SM[:, s + 12 : s + 14], SM[:, s + 8 : s + 10]))
                for i in range(2):
                    p = P[h % 2][:, i, : 128 * i + 128]
                    ts(p, p, SM[:, s + 12 + i : s + 13 + i], None, ALU.mult, done=sem("a_probs") if i else None)

            def b_scores(h):
                for i in range(2):
                    src = wait_bank("b_row", h, i)
                    if i == 0 and h >= 2:
                        wait_bank("b_turned", h - 2)
                    n = 128 * i + 128
                    tt(P[2 + h % 2][:, i, :n], src[:, :n], cst("causal", 256 - 128 * i, n), ALU.add, sem("b_masked"))
                    free(nc.vector.memset(SM[:, 31:32], 0.0), "b_row", h, i)

            def b_norm_weights(h):
                s = 144
                for i in range(2):
                    p = P[2 + h % 2][:, i, : 128 * i + 128]
                    dve.wait_ge(sem("b_exps"), 2 * h + i + 1)
                    src = wait_bank("b", h, i)
                    free(nc.vector.tensor_tensor_reduce(p, src[:, : 128 * i + 128], p, 1.0, 0.0, ALU.mult, ALU.add, SM[:, s + i : s + i + 1]), "b", h, i)
                stt(SM[:, s : s + 2], SM[:, s : s + 2], -1.0, SM[:, s : s + 2], ALU.mult, ALU.max)
                floors = COLS[:, :].rearrange("p (i c) -> p i c", i=2)[:, :, 4 + h]
                tt(SM[:, s : s + 2], SM[:, s : s + 2], floors, ALU.max)
                lane(nc.vector.reciprocal(SM[:, s : s + 2], SM[:, s : s + 2]))
                for i in range(2):
                    p = P[2 + h % 2][:, i, : 128 * i + 128]
                    ts(p, p, SM[:, s + i : s + i + 1], None, ALU.mult, done=sem("b_weights") if i else None)

            def b_norm():
                y = YAB[:, 4:8, :]
                for g in range(2):
                    mean_eps(("b_mean", g), AQ[:, 2 * g : 2 * g + 2, :].rearrange("p h t -> p (h t)"), 512, 128, 0.0)
                tt(y, y, AQ[:, 0:4, :], ALU.subtract, sem("b_centered"))
                for g in range(2):
                    mean_eps(("b_var", g), AQ[:, 2 * g : 2 * g + 2, :].rearrange("p h t -> p (h t)"), 512, 128, LN_EPS)
                reciprocal_root(AQ[:, 0:4, :])
                tt(y, y, AQ[:, 0:4, :], ALU.mult)
                for h in range(4):
                    stt(YAB[:, 4 + h, :], YAB[:, 4 + h, :], par("abhead")[:, h : h + 1], SBO[:, h, :], ALU.mult, ALU.mult, sem("y_ready"))

            def y_out(l):
                for m in range(KT):
                    src = wait_bank("y_out", l, m)
                    free(nc.vector.scalar_tensor_tensor(HT[:, m, :], HT[:, m, :], ALPHA, src[:, :256], ALU.mult, ALU.add), "y_out", l, m)

            def layer_norm(r):
                mean_eps(("ln_mean", r), MU[:, :256], 256, D, 0.0)
                for k in range(KT):
                    tt(HT[:, k, :], HT[:, k, :], MU[:, :256], ALU.subtract, sem("ln_centered"))
                mean_eps(("ln_var", r), RS[:, :256], 256, D, LN_EPS)
                reciprocal_root(RS[:, :256])
                for k in range(KT):
                    tt(HT[:, k, :], HT[:, k, :], RS[:, :256], ALU.mult, sem("ln_scaled"))

            def first_of(dst, x, top, scratch_):
                s4 = [128, 2, 4]
                tt(scratch_, x, bc(top, s4), ALU.is_equal)
                tt(scratch_, scratch_, bc(cst("rank")[:, None, :], s4), ALU.mult)
                lane(nc.vector.tensor_reduce(RT[:, 48:50], scratch_, AX.X, ALU.max))
                tt(dst, scratch_, bc(RT[:, 48:50, None], s4), ALU.is_equal)

            def router(l):
                s4 = [128, 2, 4]
                pair = lambda a, n=4: RT[:, a : a + 2 * n].rearrange("p (i j) -> p i j", i=2)
                for i in range(2):
                    src = wait_bank("router", l, i)
                    free(nc.vector.tensor_copy(RT[:, 20 * i : 20 * i + 20], src[:, :20]), "router", l, i)
                logits = RT[:, 0:40].rearrange("p (i c) -> p i c", i=2)
                lane(nc.vector.tensor_reduce(RT[:, 40:42], logits[:, :, 0:4], AX.X, ALU.max))
                ts(RT[:, 42:44], RT[:, 40:42], -1.0, None, ALU.mult, done=sem("group_max"))
                group = pair(64)
                first_of(group, logits[:, :, 0:4], RT[:, 40:42, None], pair(72))
                for i in range(2):
                    e = RT[:, 80:96].rearrange("p (g j) -> p g j", g=4)
                    tt(e, RT[:, 20 * i + 4 : 20 * i + 20].rearrange("p (g j) -> p g j", g=4), bc(RT[:, 64 + 4 * i : 68 + 4 * i, None], [128, 4, 4]), ALU.mult)
                    lane(nc.vector.tensor_reduce(RT[:, 96 + 4 * i : 100 + 4 * i], e.rearrange("p g j -> p j g"), AX.X, ALU.add))
                chosen = pair(96)
                lane(nc.vector.tensor_reduce(RT[:, 50:52], chosen, AX.X, ALU.max))
                one, two = pair(104), pair(112)
                first_of(one, chosen, RT[:, 50:52, None], pair(72))
                stt(RT[:, 96:104], RT[:, 104:112], NEG, RT[:, 96:104], ALU.mult, ALU.add)
                lane(nc.vector.tensor_reduce(RT[:, 52:54], chosen, AX.X, ALU.max))
                first_of(two, chosen, RT[:, 52:54, None], pair(72))
                tt(RT[:, 46:48], RT[:, 52:54], RT[:, 50:52], ALU.subtract, sem("top_gap"))
                dve.wait_ge(sem("top_exps"), l + 1)
                dve.wait_ge(sem("group_exps"), 2 * (l + 1))
                ts(RT[:, 50:52], RT[:, 46:48], 1.0, None, ALU.add)
                tt(RT[:, 50:52], RT[:, 50:52], RT[:, 44:46], ALU.mult)
                lane(nc.vector.reciprocal(RT[:, 50:52], RT[:, 50:52]))
                tt(RT[:, 52:54], RT[:, 50:52], RT[:, 46:48], ALU.mult)
                tt(one, one, bc(RT[:, 50:52, None], s4), ALU.mult)
                tt(two, two, bc(RT[:, 52:54, None], s4), ALU.mult)
                tt(one, one, two, ALU.add)
                for i in range(2):
                    e = SM[:, 200 + 16 * i : 216 + 16 * i].rearrange("p (g j) -> p g j", g=4)
                    tt(e, bc(RT[:, 64 + 4 * i : 68 + 4 * i, None], [128, 4, 4]), bc(RT[:, None, 104 + 4 * i : 108 + 4 * i], [128, 4, 4]),
                       ALU.mult, sem("expert_gates"))

            def split_hidden(buffer, j, done):
                lane(nc.vector.tensor_copy(HE_HI[:, buffer, j, :], HE[:, j, :]))
                tt(HE_LO[:, buffer, j, :], HE[:, j, :], HE_HI[:, buffer, j, :].bitcast(F32), ALU.subtract, done)

            def hidden(key, buffer, gate_):
                for j in range(4):
                    follow((*key, "gate", j))
                    src = wait_bank(*key, "up", j)
                    free(nc.vector.tensor_tensor(HE[:, j, :], src[:, :256], gate_, ALU.mult), *key, "up", j)
                    banks.await_read(dve, (*key, "gate", j), loop["v"])
                    tt(HE[:, j, :], HE[:, j, :], SGM[:, j, :], ALU.mult)
                    split_hidden(buffer, j, sem("hidden"))

            def add_output(key):
                for m in range(KT):
                    src = wait_bank(*key, "down", m)
                    free(nc.vector.tensor_tensor(YT[:, m, :], src[:, :256], YT[:, m, :], ALU.add), *key, "down", m)

            def split_x(l):
                for k in range(KT):
                    dve.wait_ge(sem("ln_done"), KT * 2 * l + k + 1)
                    lane(nc.vector.tensor_copy(X_HI[:, k, :], HT[:, k, :]))
                    tt(X_LO[:, k, :], HT[:, k, :], X_HI[:, k, :].bitcast(F32), ALU.subtract, sem("x_split"))

            def moe_start(l):
                for j in range(8):
                    ts(YT[:, j, :], HT[:, j, :], ALPHA, None, ALU.mult, done=sem("hidden"))

            def moe_first(l):
                for j in range(4):
                    follow(("moe", l, 0, "gate", j))
                    src = wait_bank("moe", l, 0, "up", j)
                    banks.await_read(dve, ("moe", l, 0, "gate", j))
                    free(nc.vector.tensor_tensor(HE[:, j, :], src[:, :256], SGM[:, j, :], ALU.mult), "moe", l, 0, "up", j)

            def moe_hidden(l):
                banks.await_read(dve, ("gate_row", l, 0))
                for j in range(4):
                    tt(HE[:, j, :], HE[:, j, :], GB[:, 0, :], ALU.mult)
                    split_hidden(0, j, sem("hidden"))
                banks.await_read(dve, ("gate_row", l, NEXP - 1))

            def moe(l):
                gates = GB[:, :, :].rearrange("p e t -> p (e t)")
                with dve.Fori(0, NEXP // 2 - 1) as i:
                    loop["v"], loop["i"] = 4 * i, i
                    lane.enter(i, {"hidden": 8, "split_lo": MOE_CHUNKS, "vector_step": 16})
                    for j in range(2):
                        hidden(("moe", l, 1 + j), (1 + j) % 2, gates[:, bass.ds(512 * i + 256 * (1 + j), 256)])
                        add_output(("moe", l, j))
                    lane.leave(NEXP // 2 - 1)
                loop["v"] = loop["i"] = None
                follow.next += MOE_CHUNKS * (NEXP // 2 - 2)
                hidden(("moe", l, NEXP - 1), 1, GB[:, NEXP - 1, :])
                for e in (NEXP - 2, NEXP - 1):
                    add_output(("moe", l, e))
                for k in range(KT):
                    lane(nc.vector.tensor_copy(HT[:, k, :], YT[:, k, :]), sem("moe_done"))

            def blocks(s):
                for g in range(2):
                    banks.await_read(dve, ("c_src", 2 * s + g))
                if s:
                    wait_bank("c_hidden", 0)
                pos = par("pos")
                for g in range(2):
                    x = BIN[:, 2 * s + g, :256].rearrange("p (c r) -> p r c", r=16)
                    for a in range(2):
                        pv = pos[:, 32 * s + 16 * a : 32 * s + 16 * a + 16, None]
                        tt(BLK[:, 16 * a : 16 * a + 16, 15 * g : 15 * g + 15], x[:, :, a : a + 15], bc(pv, [128, 16, 15]), ALU.add,
                           sem("blocks") if (g, a) == (1, 1) else None)
                if s == 0:
                    for a in PC:
                        lane(nc.vector.memset(a, 0.0))

            def compress(s):
                dve.wait_ge(sem("c_gelu"), s + 1)
                free(nc.vector.memset(SM[:, 31:32], 0.0), "c_hidden", s)

            def c_scores(h):
                s = 64 + 20 * (h % 2)
                if h >= 2:
                    wait_bank("c_turned", h - 2, 2)
                for i in range(2):
                    n = 128 * i + 128
                    for b in range(2):
                        src = wait_bank("c", h, i, b)
                        c = s + 2 * (b + 1) + i
                        ins = nc.vector.tensor_tensor_reduce(P[2 * (h % 2) + b][:, i, :n], src[:, :n], BIAS_C[:, h, 256 - n :],
                                                             1.0, NEG, ALU.add, ALU.max, SM[:, c : c + 1])
                        free(ins, "c", h, i, b)
                src = wait_bank("c_c", h)
                for i in range(2):
                    n = 7 + 8 * i
                    bias_ = BIAS_C[:, h, 128 * (1 - i) + 31 :: 16]
                    ins = nc.vector.tensor_tensor_reduce(PC[h % 2][:, i, :n], src[:, 16 * i : 16 * i + n], bias_, 1.0, NEG, ALU.add, ALU.max, SM[:, s + i : s + i + 1])
                    if i:
                        free(ins, "c_c", h)
                    else:
                        lane(ins)
                ts(SM[:, s + 6 : s + 12], SM[:, s : s + 6], NEG / 10, -1.0, ALU.max, ALU.mult, sem("c_max"))

            def c_norm(h):
                s = 64 + 20 * (h % 2)
                dve.wait_ge(sem("c_exps"), 6 * (h + 1))
                banks.await_read(dve, ("c_gate", 1))
                ts(SM[:, s + 12 : s + 18], SM[:, s + 12 : s + 18], 1e-30, None, ALU.max)
                lane(nc.vector.reciprocal(SM[:, s : s + 6], SM[:, s + 12 : s + 18]))
                f = SM[:, s : s + 6].rearrange("p (b i) -> p b i", b=3)
                g = CG[:, :, :].rearrange("p i (b h) -> p b i h", b=3)[:, :, :, h]
                tt(f, f, g, ALU.mult)
                for b in (1, 2, 0):
                    for i in range(2):
                        p = PC[h % 2][:, i, : 7 + 8 * i] if b == 0 else P[2 * (h % 2) + b - 1][:, i, : 128 * i + 128]
                        ts(p, p, SM[:, s + 2 * b + i : s + 2 * b + i + 1], None, ALU.mult, done=sem("c_probs") if i else None)

            steps = locals()
            for name, *args in SCHEDULE:
                if name in steps:
                    steps[name](*args)
                follow(("step", name, *args))

        @block.gpsimd
        def _(pool):
            lane = Lane(pool, sem("gpsimd_step"))

            def hgrn_args(l, i):
                pool.wait_ge(sem("summed"), l + 1)
                if i >= 2:
                    banks.await_(pool, ("scores", l, i - 2))
                d, lo = HD[i % 2], SB * i
                qq = d[:, :1024].rearrange("p (j h t) -> p j h t", j=8, h=4)
                shape = [128, 8, 4, SB]
                b = HB[:, :, lo : lo + SB]
                ref = b.rearrange("p h (j f) -> p j h f", f=SS)[:, :, :, 0:1]
                lane(nc.gpsimd.tensor_tensor(qq, bc(b[:, None, :, :], shape), bc(ref, shape), ALU.subtract))
                lane(nc.gpsimd.tensor_scalar(d[:, :1024], d[:, :1024], 0.0, None, ALU.min), None if i else sem("decay_args"))
                if i:
                    kk = d[:, 1024 : 1024 + 4 * lo].rearrange("p (h s) -> p h s", h=4)
                    lane(nc.gpsimd.tensor_tensor(kk, bc(HB[:, :, lo : lo + 1], [128, 4, lo]), HB[:, :, :lo], ALU.subtract), sem("decay_args"))

            def ff1(l, half):
                for m in range(FH * half, FH * half + FH):
                    banks.await_read(pool, ("ff1", l, m))
                    lane(nc.gpsimd.tensor_tensor(F1[:, m % 4, :], F1[:, m % 4, :], F1[:, m % 4, :], ALU.mult), sem("squared"))

            def ab_in():
                banks.await_(pool, ("aq", 0))
                lane(nc.gpsimd.memset(BIN[:, :, 0:3], 0.0), sem("b_padding"))

            steps = locals()
            for name, *args in SCHEDULE:
                if name in steps:
                    steps[name](*args)

        @block.sync
        def _(sp):
            sp.dma_start(XT[:, :, :], x_in).then_inc(sem("loaded"), 16)
            sp.dma_start(PAR[:, :], params).then_inc(sem("loaded"), 16)
            sp.dma_start(CST[:, :], consts).then_inc(sem("loaded"), 16)

            def load(n, slot):
                sp.dma_start(ring[:, slot, :], stream[bass.ds(128 * n, 128), :]).then_inc(arrived[slot], 16)

            split_chunks = set(splits.chunks)
            rank, counts = [], [0, 0]
            for n in range(n_chunks):
                counts[n in split_chunks] += 1
                rank.append((n in split_chunks, counts[n in split_chunks]))

            def freed(n, i=None):
                split_, count = rank[n]
                sp.wait_ge(split_lo if split_ else w_used, count if i is None else count + RING * i)

            for s in range(RING):
                load(s, s)
            n = RING
            while n < n_chunks:
                rounds = 0
                while n % RING == 0 and n + RING * (rounds + 1) <= n_chunks and len({rank[m - RING][0] for m in range(n, n + RING * (rounds + 1))}) == 1:
                    rounds += 1
                if rounds > 1:
                    with sp.Fori(0, rounds) as i:
                        for s in range(RING):
                            freed(n - RING + s, i)
                            load(RING * i + n + s, s)
                    n += RING * rounds
                else:
                    freed(n - RING)
                    load(n, n % RING)
                    n += 1
            for k in range(KT):
                sp.wait_ge(sem("ln_done"), KT * 3 + k + 1)
                sp.dma_start(out[:, k, :], HT[:, k, :]).then_inc(sem("stored"), 16)
            sp.wait_ge(sem("stored"), 16 * KT)


def schedule():
    s = [("start",), ("norm", 0), ("store_bias",)]
    for l in range(DEPTH):
        s += [("norm", 2 * l)] if l else []
        s += [("conv_in", l), ("conv_taps", l), ("hgrn_in", l), ("mla_in", l), ("conv_norm", l), ("mla_norm", l), ("hgrn_prep", l)]
        s += [("gate", l, 0, m) for m in range(KT)] + [("branch_out", l, 0, c) for c in range(4)]
        s += [("hgrn_args", l, 0)]
        for i in range(NB):
            s += [("hgrn_args", l, i + 1)] if i + 1 < NB else []
            s += [("gate", l, 1, i)] if i < KT else []
            s += [("hgrn_block", l, i), ("hgrn_turn", l, i)]
        s += [("hgrn_values", l), ("mla_up", l), ("hgrn_norm", l)]
        s += [("gate", l, 2, m) for m in range(4)] + [("head_norm", l, 0)]
        s += [("gate", l, 2, m) for m in range(4, 6)] + [("head_norm", l, 1)]
        s += [("gate", l, 2, m) for m in range(6, 8)] + [("att_scores", l, 0)]
        for h in range(HEADS):
            s += [("att_scores", l, h + 1)] if h + 1 < HEADS else []
            s += [] if h % 2 else [("branch_out", l, 1, h // 2)]
            s += [("att_norm", l, h), ("att_turn", l, h)]
            s += [("att_values", l, h // 2)] if h % 2 else []
        s += [("branch_out", l, 2, c) for c in range(4)] + [("mix_out", l), ("norm", 2 * l + 1)]
        s += [("hankel",)] if l == DEPTH - 1 else []
        s += [("ff1", l, 0)]
        s += [("bias",)] if l == DEPTH - 1 else []
        s += [("ff2", l, 0), ("ff1", l, 1), ("ff2", l, 1)]
    s += [("ab_in",), ("a_scores", 0)]
    for h in range(HEADS):
        s += [("a_scores", h + 1)] if h + 1 < HEADS else []
        s += [("bqk_in", h), ("a_norm", h), ("a_turn", h)]
        s += [("a_values", h // 2)] if h % 2 else []
    s += [("if_in",), ("b_gates",)] + [("bo_in", j) for j in range(4)] + [("b_conv",), ("gate_rows",), ("bv_in",), ("b_scores", 0)]
    for h in range(H4):
        s += [("b_norm_weights", h)]
        s += [("b_scores", h + 1)] if h + 1 < H4 else []
        s += [("b_turn", h), ("b_values", h)]
    s += [("b_norm",)]
    for l in range(2):
        if l:
            s += [("c_in",), ("blocks", 0), ("compress", 0), ("blocks", 1), ("compress", 1), ("compress2",), ("c_scores", 0)]
            for h in range(HEADS):
                s += [("c_scores", h + 1)] if h + 1 < HEADS else []
                s += [("c_norm", h), ("c_turn", h), ("c_values", h)]
        s += [("y_out", l), ("layer_norm", 2 * l), ("split_x", l), ("router", l), ("moe_start", l), ("moe_first", l), ("expert_gates", l), ("moe_hidden", l), ("moe", l)]
        s += [("layer_norm", 2 * l + 1)]
    return s


def kernel(**inputs):
    from concourse import bacc, mybir as _mybir
    from concourse.bass_utils import run_bass_kernel_spmd

    i = {k: np.asarray(v) for k, v in inputs.items()}
    tokens = np.concatenate([i["meta"], i["x"][0]], axis=0)
    arrays = {
        "weights": np.ascontiguousarray(weight_stream(i).reshape(-1, CHUNK)),
        "params": parameters(i),
        "consts": constants(),
        "x": np.ascontiguousarray(tokens.T.reshape(KT, 128, T).transpose(1, 0, 2)),
    }
    nc = bacc.Bacc("TRN2", target_bir_lowering=False, num_devices=1)
    aps = {k: nc.dram_tensor(f"in_{k}", a.shape, _mybir.dt.from_np(a.dtype), kind="ExternalInput").ap() for k, a in arrays.items()}
    out = nc.dram_tensor("out", (128, KT, SEQ), F32, kind="ExternalOutput").ap()
    scratch = nc.dram_tensor("bias_by_distance", (HEADS, 384), F32, kind="Internal").ap()
    build_program(nc, aps["weights"], aps["params"], aps["consts"], aps["x"], out, scratch)
    r = run_bass_kernel_spmd(nc, [{f"in_{k}": a for k, a in arrays.items()}], core_ids=[0])
    y = np.asarray(r.results[0]["out"])
    return np.ascontiguousarray(y.transpose(2, 1, 0).reshape(1, SEQ, D))
```

```python
from contextlib import ExitStack

import numpy as np

import concourse.bass as bass
from concourse import mybir

F32 = mybir.dt.float32
F32R = mybir.dt.float32r
ALU = mybir.AluOpType
ACT = mybir.ActivationFunctionType
AX = mybir.AxisListType

D = 1024
KT = D // 128
DEPTH = 2
N_META = 16
SEQ = 256
T = SEQ + N_META
TOK1 = [(0, 128), (128, 128), (256, T - 256)]
TP = 288
EPS = 1e-6
CLAMP = 1.0 - 1e-6
CONV_K = 31
HEADS = 8
NOPE, ROPE, QK, VD = 64, 32, 96, 64
H4 = 4
SB, SS = 32, 4
NB = TP // SB
D_FF = 4 * D
FT = D_FF // 128
ALPHA = (2.0 * DEPTH) ** 0.25
LN_EPS = 1e-5
BUCKETS, MAX_DIST = 32, 2048
NCMP = (SEQ - 32) // 16 + 1
NEXP, EH = 16, D // 2
MOE_CHUNKS = 24
NEG = -1e30
A_SCALE, C_SCALE = 64 ** -0.5, 128 ** -0.5

CHUNK = 1024
RING = 4
SPLIT = 4
FH = FT // 2


def feature_chunks(w):
    k, m = w.shape
    return w.reshape(k // 128, 128, m // 128, 128).transpose(2, 1, 0, 3).reshape(m // 128, 128, k)


def grouped(w, n):
    t = feature_chunks(w)
    return t.reshape(t.shape[0] // n, n, 128, -1).transpose(0, 2, 1, 3).reshape(-1, 128, n * t.shape[2])


def token_chunks(w):
    return w.reshape(4, 2, 128, 512).transpose(0, 2, 1, 3).reshape(4, 128, 1024)


def padded(a):
    out = np.zeros((a.shape[0], 128, CHUNK), np.float32)
    out[:, :, : a.shape[2]] = a
    return out


def weight_stream(i):
    out = []
    for l in range(DEPTH):
        w = i["w_in"][l]
        at = np.cumsum([0, 1024, 256, 128, 32, 512, 512, 512, 512, 3072])
        conv, cq, ckv, rope, hq, hf, hi, hg, gate = (w[:, at[j] : at[j + 1]] for j in range(9))
        c = feature_chunks(conv)
        out += [c.reshape(2, 4, 128, 1024).transpose(1, 0, 2, 3).reshape(8, 128, 1024)]
        out += [feature_chunks(hf), feature_chunks(hq), feature_chunks(hg), token_chunks(hi)]
        out += [feature_chunks(cq), feature_chunks(ckv)]
        r = np.zeros((D, 128), np.float32)
        r[:, NOPE:QK] = rope
        out += [feature_chunks(r)]
        gates = [feature_chunks(gate[:, g * D : (g + 1) * D]) for g in range(3)]
        out += [gates[0], grouped(i["w_conv_out"][l], 2), gates[2]]
        uq = i["w_uq"][l].reshape(2, 128, HEADS, QK).transpose(2, 1, 0, 3)
        out += [padded(uq.reshape(2, 4, 128, 2 * QK).transpose(0, 2, 1, 3).reshape(2, 128, 8 * QK))]
        ukv = i["w_ukv"][l].reshape(128, HEADS, 2, 64).transpose(0, 2, 1, 3)
        out += [ukv.reshape(1, 128, 1024)]
        out += [gates[1], grouped(i["w_hgrn_out"][l], 2), grouped(i["w_attn_out"][l], 2)]
        out += [feature_chunks(i["w_out"][l])]
        f1, f2 = feature_chunks(i["w_ff1"][l]), feature_chunks(i["w_ff2"][l]).reshape(KT, 128, 4, 1024)
        for half in range(2):
            out += [f1[FH * half : FH * half + FH], f2[:, :, 2 * half : 2 * half + 2].transpose(0, 2, 1, 3).reshape(-1, 128, 1024)]
    w = i["ab_w_in_2"][0]
    part = lambda j: w[:, 512 * j : 512 * j + 512]
    out += [feature_chunks(part(0)), feature_chunks(part(1)), token_chunks(part(2))]
    out += [feature_chunks(part(3)), feature_chunks(part(4)), feature_chunks(part(6)), token_chunks(part(5))]
    out += [feature_chunks(i["ab_w_out_2"][0])]
    moe = lambda l: experts(i["moe_w_gate_2"][l], i["moe_w_up_2"][l], i["moe_w_down_2"][l])
    out += [moe(0)]
    w = i["c_w_in_2"][0]
    kv = w[:, D : D + 1536].reshape(D, 3, 2, 256)
    out += [feature_chunks(kv[:, 0].reshape(D, 512)), feature_chunks(w[:, :D])]
    out += [feature_chunks(kv[:, 1, 0]), feature_chunks(kv[:, 2, 0])]
    out += [token_chunks(kv[:, 1:, 1].reshape(D, 512))]
    for s in range(2):
        out += [i["c_cmp_w1_2"][0, s].reshape(8, 4, 128, 256).transpose(0, 2, 1, 3).reshape(8, 128, 1024)]
    w2 = i["c_cmp_w2_2"][0].reshape(2, 2, 128, 128).transpose(2, 0, 1, 3).reshape(1, 128, 512)
    out += [padded(w2), feature_chunks(i["c_w_out_2"][0]), moe(1)]
    return np.concatenate(out, axis=0)


def experts(gate, up, down):
    out = []
    for e in range(NEXP):
        g, u = feature_chunks(gate[e]), feature_chunks(up[e])
        out += [np.stack([g, u], 1).reshape(8, 128, 1024)]
        if e:
            out += [grouped(down[e - 1], 2)]
    return np.concatenate([*out, grouped(down[-1], 2)], axis=0)


def layout(widths):
    at, out = 0, {}
    for name, n in widths:
        out[name] = (at, n)
        at += n
    return out, at


PARAMS, NPAR = layout(
    [(f"{n}{l}", c) for l in range(DEPTH) for n, c in (
        ("norm1", 8), ("convw", 4 * CONV_K), ("convb", 4), ("clng", 4), ("clnb", 4), ("qa", 2), ("kva", 1),
        ("qn", 1), ("kn", 1), ("lb", 4), ("hn", 4), ("norm2", 8),
        ("lng0_", 8), ("lnb0_", 8), ("lng1_", 8), ("lnb1_", 8), ("router", KT * 20), ("rbias", 20))]
    + [("ibias", 1), ("fbias", 1), ("abconv", 8 * 4), ("abhead", 4), ("wif", KT * 8),
       ("pos", 64), ("wcg", KT * 24), ("cgbias", 24), ("rel", HEADS)])

CONSTS, NCONST = layout([
    ("ident", 128), ("flip", 128), ("ones", 128), ("causal", 528), ("logcount", 256), ("tri", SB),
    ("cos", T), ("sin", T), ("bucket", 384), ("rank", 4), ("pick", 31), ("eps", 2)])


def parameters(i):
    out = np.zeros((128, NPAR), np.float32)

    def put(name, a):
        at, n = PARAMS[name]
        a = np.asarray(a, np.float32)
        a = a.reshape(a.shape[0], -1)
        out[: a.shape[0], at : at + n] = a

    col = lambda v: np.asarray(v).reshape(-1, 128).T
    for l in range(DEPTH):
        put(f"norm1{l}", col(i["norm1_g"][l]))
        put(f"convw{l}", i["conv_w"][l].reshape(CONV_K, 4, 128).transpose(2, 1, 0))
        put(f"convb{l}", col(i["conv_b"][l]))
        put(f"clng{l}", col(i["conv_ln_g"][l]))
        put(f"clnb{l}", col(i["conv_ln_b"][l]))
        put(f"qa{l}", col(i["q_a_norm_g"][l]))
        put(f"kva{l}", col(i["kv_a_norm_g"][l]))
        put(f"qn{l}", i["q_norm_g"][l][:, None])
        put(f"kn{l}", i["k_norm_g"][l][:, None])
        put(f"lb{l}", col(i["hgrn_lb_logits"][l]))
        put(f"hn{l}", col(i["hgrn_norm_g"][l]))
        put(f"norm2{l}", col(i["norm2_g"][l]))
        for j in range(2):
            put(f"lng{j}_{l}", col(i["ln_g_2"][l, j]))
            put(f"lnb{j}_{l}", col(i["ln_b_2"][l, j]))
        r = np.concatenate([i["moe_wr_g_2"][l], i["moe_wr_e_2"][l].transpose(1, 0, 2).reshape(D, 16)], axis=1)
        put(f"router{l}", r.reshape(KT, 128, 20).transpose(1, 0, 2))
        put(f"rbias{l}", np.concatenate([i["moe_br_g_2"][l], i["moe_br_e_2"][l].reshape(-1)])[None])
    put("ibias", i["ab_gate_b_2"][0, :4][:, None])
    put("fbias", i["ab_gate_b_2"][0, 4:][:, None])
    put("abconv", i["ab_conv_2"][0].reshape(4, 8, 128).transpose(2, 1, 0))
    put("abhead", col(i["ab_head_norm_2"][0]))
    put("wif", i["ab_w_in_2"][0][:, 3584:3592].reshape(KT, 128, 8).transpose(1, 0, 2))
    put("pos", i["c_cmp_pos_2"][0].transpose(2, 0, 1))
    put("wcg", i["c_w_in_2"][0][:, 2560:2584].reshape(KT, 128, 24).transpose(1, 0, 2))
    put("cgbias", i["c_gate_b_2"][0][None])
    put("rel", i["rel_bias_2"])
    return out


def constants():
    out = np.zeros((128, NCONST), np.float32)

    def put(name, a, row=0):
        at, n = CONSTS[name]
        out[row : row + a.shape[0], at : at + n] = a.reshape(a.shape[0], -1)

    p = np.arange(128)
    put("ident", np.eye(128))
    put("flip", np.eye(128)[::-1])
    put("ones", np.ones((128, 128)))
    put("causal", np.where(np.arange(528)[None] - 256 <= p[:, None], 0.0, NEG))
    d = p[:, None] + 128 - np.arange(256)[None]
    n = ((d <= 128).astype(int) + (d % 4 == 0) + (d % 16 == 0)) * (d >= 0)
    put("logcount", np.where(n > 0, np.log(np.maximum(n, 1)), NEG))
    put("tri", (np.arange(SB)[None] <= (p % SB)[:, None]).astype(float))
    half = ROPE // 2
    inv = 10000.0 ** (-np.arange(half, dtype=np.float32) / np.float32(half))
    ang = (np.arange(T, dtype=np.float32)[None] * inv.astype(np.float32)[:, None]).astype(np.float32)
    put("cos", np.concatenate([np.cos(ang)] * 2), NOPE)
    put("sin", np.concatenate([-np.sin(ang), np.sin(ang)]), NOPE)
    n = np.maximum(255 - np.arange(384), 0)
    exact = BUCKETS // 2
    large = exact + (np.log(np.maximum(n, 1) / exact) / np.log(MAX_DIST / exact) * (BUCKETS - exact)).astype(int)
    put("bucket", (np.where(n < exact, n, np.minimum(large, BUCKETS - 1))[None] == np.arange(BUCKETS)[:, None]).astype(float))
    put("pick", np.tile(np.eye(31)[15], (128, 1)))
    put("eps", np.tile([EPS, LN_EPS], (128, 1)))
    put("rank", np.tile([4.0, 3.0, 2.0, 1.0], (128, 1)))
    return out


class Lane:

    def __init__(self, eng, step):
        self.eng, self.step, self.count, self.loop = eng, step, {}, None

    def __call__(self, ins, sem=None):
        sem = sem or self.step
        n = self.count[sem.name] = self.count.get(sem.name, 0) + 1
        ins.then_inc(sem, 1)
        self.eng.wait_ge(sem, self.at(sem, n))

    def at(self, sem, n):
        return n if self.loop is None else n + self.loop[0] * self.loop[1][sem.name]

    def enter(self, i, per):
        self.loop, self.before = (i, per), dict(self.count)

    def leave(self, times):
        for name, n in self.loop[1].items():
            assert self.count.get(name, 0) - self.before.get(name, 0) == n, (name, self.count[name], self.before.get(name, 0))
            self.count[name] += n * (times - 1)
        self.loop = None


class Splits:

    def __init__(self):
        self.chunks, self.marks, self.known = [], {}, ()

    def limit(self, mark):
        begun, n = self.marks[mark]
        count = min(begun - 1 + SPLIT, len(self.chunks))
        while count and self.chunks[count - 1] > n - 2 + RING and self.chunks[count - 1] - RING not in self.known:
            count -= 1
        return count


class Follower:

    def __init__(self, splits, split):
        self.splits, self.split, self.next, self.paused = splits, split, 0, False

    def __call__(self, mark):
        while not self.paused and self.next < self.splits.limit(mark):
            self.split(self.next, self.splits.chunks[self.next])
            self.next += 1


class Banks:

    def __init__(self, psum, full, free):
        self.psum, self.full, self.free = psum, full, free
        self.next, self.uses, self.of = 0, [0] * 8, {}
        self.loop = None

    def value(self, n, loop):
        return n if loop is None else n + loop

    def take(self, pe, key):
        b, n = self.next, self.uses[self.next]
        self.next, self.uses[b] = (b + 1) % 8, n + 1
        assert key not in self.of, key
        self.of[key] = (b, n)
        if n:
            pe.wait_ge(self.free[b], n if self.loop is None else n + self.loop)
        return self.psum[:, b, :]

    def filled(self, key):
        return self.full[self.of[key][0]]

    def await_(self, eng, key, loop=None):
        b, n = self.of[key]
        eng.wait_ge(self.full[b], n + 1 if loop is None else n + 1 + loop)
        return self.psum[:, b, :]

    def freed(self, key):
        return self.free[self.of[key][0]]

    def await_read(self, eng, key, loop=None):
        b, n = self.of[key]
        eng.wait_ge(self.free[b], n + 1 if loop is None else n + 1 + loop)


def build_program(nc, stream, params, consts, x_in, out, scratch):
    n_chunks = stream.shape[0] // 128
    with ExitStack() as ctx:
        def sb(name, *shape, dtype=F32, stack=ctx):
            return stack.enter_context(nc.sbuf_tensor(name, [128, *shape], dtype))

        sems = {}

        def sem(name):
            if name not in sems:
                sems[name] = ctx.enter_context(nc.semaphore(name))
            return sems[name]

        ring = sb("ring", RING, CHUNK)
        W_HI = sb("W_HI", SPLIT, CHUNK, dtype=F32R)
        W_LO = sb("W_LO", SPLIT, CHUNK, dtype=F32R)
        XT = sb("XT", KT, T)
        SQ = sb("SQ", 8 * TP)
        PAR = sb("PAR", NPAR)
        CST = sb("CST", NCONST)
        MIX = sb("MIX", KT, T)
        GATE1 = sb("GATE1", KT, T)
        RS = sb("RS", TP)
        MU = sb("MU", TP)
        psum = ctx.enter_context(nc.psum_tensor("psum", [128, 8, 512], F32))

        SM = sb("SM", 264)
        RT = sb("RT", 120)
        ST = sb("ST", 64)
        size = 212000 // 4 - ((RING + 2 * SPLIT) * CHUNK + 5 * KT * T + 8 * TP + NPAR + NCONST + 16 * 256 + 2 * TP + 264 + 120 + 64)
        with ExitStack() as phase:
            HN = sb("HN", KT, T, stack=phase)
            GATES = [sb("GATE0", KT, T, stack=phase), GATE1]
            BIAS_C = sb("BIAS_C", HEADS, 256, stack=phase)
            BIAS_A = sb("BIAS_A", HEADS, 256, stack=phase)
            region = sb("region", size, stack=phase)
        with ExitStack() as parts:
            X_HI, X_LO = (sb(f"X_{p}", KT, 256, dtype=F32R, stack=parts) for p in ("HI", "LO"))
            sb("unused", 2 * KT * T - 2 * KT * 256 + 16 * 256, stack=parts)
            with ExitStack() as phase:
                F1_HI, F1_LO = (sb(f"F1_{p}", FH, T, dtype=F32R, stack=phase) for p in ("HI", "LO"))
                F1 = sb("F1", 4, T, stack=phase)
                FN_HI, FN_LO = (sb(f"FN_{p}", KT, T, dtype=F32R, stack=phase) for p in ("HI", "LO"))
                assert (2 * (KT + FH) + 4) * T <= size
            with ExitStack() as phase:
                HE_HI, HE_LO = (sb(f"HE_{p}", 2, 4, 256, dtype=F32R, stack=phase) for p in ("HI", "LO"))
                HE = sb("HE", 4, 256, stack=phase)
                GB = sb("GB", NEXP, 256, stack=phase)
                GATT = sb("GATT", 256, stack=phase)
                SGM = sb("SGM", 4, 256, stack=phase)
                assert (16 + 4 + NEXP + 1 + 4) * 256 <= size
        used = [0]

        def at_region(*shape):
            n = int(np.prod(shape))
            v = region[:, used[0] : used[0] + n]
            used[0] += n
            assert used[0] <= region.shape[1], (used[0], region.shape)
            if len(shape) == 2:
                return v.rearrange("p (a b) -> p a b", a=shape[0])
            if len(shape) == 3:
                return v.rearrange("p (a b c) -> p a b c", a=shape[0], b=shape[1])
            return v

        HC = at_region(4, T + CONV_K - 1)
        CO = at_region(4, T)
        HB = at_region(4, TP)
        HK = at_region(4, TP)
        HQ = at_region(4, TP)
        HG = at_region(4, T)
        HV = at_region(3, 512)
        HR = RS[:, :T]
        CQ = at_region(2, T)
        CKV = at_region(T)
        MV = HV
        KR = at_region(T)
        work = used[0]
        HKK = at_region(4, TP)
        HD = [at_region(1024 + 4 * 256) for _ in range(2)] + [SQ[:, : 1024 + 4 * 256]]
        HA = [at_region(TP + 96) for _ in range(2)]
        HAT = at_region(3, 4, TP)
        used[0] = work
        QH = at_region(HEADS, T)
        KH = at_region(HEADS, T)
        RSQ = at_region(HEADS, T)
        P2 = [at_region(3, T) for _ in range(2)] + [SQ[:, : 3 * T].rearrange("p (i t) -> p i t", i=3)]
        PT2 = [at_region(432) for _ in range(2)]
        OT = CO
        HO = HB
        used[0] = 0
        YT = MIX[:, :, :256]
        AQ = at_region(KT, 256)
        AK = at_region(KT, 256)
        AV = at_region(2, 512)
        BV = at_region(2, 512)
        BIN = at_region(8, 259)
        BC = at_region(8, 256)
        SBO = at_region(4, 256)
        YAB = at_region(KT, 256)
        ROWS = SQ[:, :2048].rearrange("p (r t) -> p r t", r=8)
        COLS = at_region(16)
        P = [GATES[1][:, :, :].rearrange("p k t -> p (k t)")[:, 512 * j : 512 * j + 512].rearrange("p (i t) -> p i t", i=2) for j in range(4)]
        P += [MIX[:, :, :].rearrange("p k t -> p (k t)")[:, 512 * j : 512 * j + 512].rearrange("p (i t) -> p i t", i=2) for j in range(2)]
        PT = [at_region(384) for _ in range(4)]
        PC = [SM[:, 130 + 32 * j : 162 + 32 * j].rearrange("p (i t) -> p i t", i=2) for j in range(3)]
        PCT = [at_region(256) for _ in range(2)]
        KC = at_region(30)
        VC = at_region(2, 128)
        CG = at_region(2, 24)
        BLK = at_region(960).rearrange("p (i n) -> p i n", i=32)
        CHID = BC

        def par(name, rows=128):
            at, n = PARAMS[name]
            return PAR[:rows, at : at + n]

        def cst(name, lo=0, n=None, rows=128):
            at, w = CONSTS[name]
            return CST[:rows, at + lo : at + lo + (w if n is None else n)]

        def ones(k, m):
            return cst("ones", 0, m, k)

        ident = lambda k: cst("ident", 0, k, k)
        HT = XT[:, :, N_META:T]

        banks = Banks(psum, [sem(f"bank_full{b}") for b in range(8)], [sem(f"bank_free{b}") for b in range(8)])
        arrived = [sem(f"weights_arrived{s}") for s in range(RING)]
        w_used, split_hi, split_lo, split_used = (sem(n) for n in ("weights_used", "split_hi", "split_lo", "split_used"))
        splits = Splits()
        block = ctx.enter_context(nc.Block())
        SCHEDULE = schedule()

        @block.tensor
        def _(pe):
            state = {"n": 0, "held": None, "release": [], "loop": None}
            keys = {}

            def filled(done):
                splits.marks[keys.pop(done.name)] = (len(splits.chunks), state["n"])

            def mm(dst, w, x, start=True, stop=True, done=None):
                if isinstance(w, tuple):
                    mm(dst, w[0], x[0], start, False)
                    mm(dst, w[0], x[1], False, False)
                    mm(dst, w[1], x[0], False, stop, done)
                    return
                ins = nc.tensor.matmul(dst, w, x, start=start, stop=stop, skip_group_check=True)
                if done is not None:
                    ins.then_inc(done, 1)
                    filled(done)
                elif state["release"]:
                    ins.then_inc(state["release"].pop(0), 1)

            def turn(dst, src, k, done=None):
                ins = nc.tensor.transpose(dst, src, ident(k))
                if done is not None:
                    ins.then_inc(done, 1)
                    filled(done)

            def columns(w, lo, n):
                return tuple(p[:, lo : lo + n] for p in w) if isinstance(w, tuple) else w[:, lo : lo + n]

            def chunk(split=False):
                n = state["n"]
                state["n"] += 1
                state["release"] += [state["held"]] if state["held"] is not None else []
                state["held"] = split_used if split else w_used
                if split:
                    i = len(splits.chunks)
                    splits.chunks.append(n)
                    pe.wait_ge(split_lo, i + 1 if state["loop"] is None else i + 1 + MOE_CHUNKS * state["loop"])
                    return W_HI[:, i % SPLIT, :], W_LO[:, i % SPLIT, :]
                pe.wait_ge(arrived[n % RING], 16 * (n // RING + 1))
                return ring[:, n % RING, :]

            def take(*key):
                dst = banks.take(pe, key)
                keys[banks.filled(key).name] = key
                return dst, banks.filled(key)

            def project(key, x, n=T, chunks=1, ready=None):
                dst, done = take(*key)
                for c in range(chunks):
                    w = chunk(isinstance(x(0), tuple))
                    for k in range(KT):
                        last = c == chunks - 1 and k == KT - 1
                        if ready is not None:
                            ready(8 * c + k)
                        mm(dst[:, :n], columns(w, 128 * k, 128), x(8 * c + k), c + k == 0, last, done if last else None)

            def tokens(key, x, tiles):
                dsts = [take(*key, i) for i in range(len(tiles))]
                for c in range(4):
                    w = chunk(isinstance(x(0, 0, 128), tuple))
                    splits.marks[(*key, "chunks")] = (len(splits.chunks), state["n"])
                    for i, (lo, n) in enumerate(tiles):
                        for k in range(2):
                            last = c == 3 and k == 1
                            mm(dsts[i][0][:n, :], x(2 * c + k, lo, n), columns(w, 512 * k, 512),
                               c + k == 0, last, dsts[i][1] if last else None)

            def half_projects(key, x, n, parts=range(4), ready=None):
                for c in parts:
                    w = chunk(isinstance(x(0), tuple))
                    for j in range(2):
                        dst, done = take(*key, 2 * c + j)
                        for k in range(4):
                            if ready is not None and (c, j) == (parts[0], 0):
                                ready(k)
                            mm(dst[:, :n], columns(w, 512 * j + 128 * k, 128), x(k), k == 0, k == 3, done if k == 3 else None)

            def column_sums(key, x, kt, n, ready=None):
                dst, done = take(*key)
                for k in range(kt):
                    if ready is not None:
                        ready(k)
                    mm(dst[:, :n], ones(128, 128), x(k), k == 0, k == kt - 1, done if k == kt - 1 else None)

            sq = lambda k, n=T: SQ[:, n * k : n * k + n]
            hn = lambda k: HN[:, k, :]

            def start():
                dst, done = take("bucket_bias")
                mm(dst[:HEADS, :384], PAR[:BUCKETS, PARAMS["rel"][0] : PARAMS["rel"][0] + HEADS], cst("bucket", rows=BUCKETS), done=done)

            def till(name, before):
                return lambda k: pe.wait_ge(sem(name), before + k + 1)

            def bias():
                pe.wait_ge(sem("hankel"), 16)
                for g in range(4):
                    dst, done = take("bias", g)
                    mm(dst[:, :], cst("flip"), SQ[:, 512 * g : 512 * g + 512], done=done)

            def norm(r):
                if r == 0:
                    pe.wait_ge(sem("loaded"), 32)
                column_sums(("norm", r), sq, KT, T, till("norm_squares", KT * r))

            def conv_in(l):
                for j in range(4):
                    project(("conv_a", l, j), hn, ready=None if j else till("normed", KT * 2 * l))
                    project(("conv_g", l, j), hn)

            def hgrn_in(l):
                for name in ("hf", "hq", "hg"):
                    for j in range(4):
                        project((name, l, j), hn)
                tokens(("hi", l), lambda k, lo, n: HN[:, k, lo : lo + n], TOK1)

            def mla_in(l):
                for j in range(2):
                    project(("cq", l, j), hn)
                project(("ckv", l), hn)
                project(("rope", l), hn)

            def conv_norm(l):
                column_sums(("conv_mean", l), lambda k: CO[:, k, :], 4, T, lambda k: pe.wait_ge(sem(f"conv_out{k}"), l + 1))

            def conv_var(l):
                pe.wait_ge(sem("conv_squares"), l + 1)
                column_sums(("conv_var", l), sq, 4, T)

            def gate(l, b, m):
                project(("gate", l, b, m), hn)

            def branch_out(l, b, c):
                src, name = ((CO, "conv_done"), (HO, "hgrn_done"), (OT, None))[b]
                ready = till(name, 4 * l) if name else lambda k: banks.await_read(pe, ("pv", l, k))
                half_projects(("branch", l, b), lambda k: src[:, k, :T], T, (c,), None if c else ready)

            def hgrn_block(l, i):
                pe.wait_ge(sem("decayed"), NB * l + i + 1)
                d = HD[i % 3]
                qq = d[:, 0:1024].rearrange("p (j h t) -> p j h t", j=8, h=4)
                dst, done = take("scores", l, i)
                for h in range(4):
                    row = dst[SB * h : SB * h + SB, :]
                    if i:
                        mm(row[:, : SB * i], qq[:, 0, h, :], d[:, 1024 + SB * i * h : 1024 + SB * i * (h + 1)])
                    for j in range(8):
                        lo = SB * i + SS * j
                        mm(row[:, lo : lo + SS], qq[:, j, h, :], HKK[:, h, lo : lo + SS], done=done if (h, j) == (3, 7) else None)

            def hgrn_turn(l, i):
                banks.await_read(pe, ("scores", l, i))
                dst, done = take("turned", l, i)
                n = -(-SB * (i + 1) // 128)
                for s in range(n):
                    turn(dst[:, 128 * s : 128 * s + 128], HA[i % 2][:, 128 * s : 128 * s + 128], 128, done if s == n - 1 else None)

            def hgrn_values(l):
                banks.await_read(pe, ("turned", l, NB - 1))
                banks.await_read(pe, ("hi", l, 2))
                for h in range(4):
                    dst, done = take("ho", l, h)
                    for s, (lo, k) in enumerate(TOK1):
                        mm(dst[:, lo:TP], HV[:k, s, 128 * h : 128 * h + 128], HAT[:k, s, h, lo:TP], s == 0, s == 2, done if s == 2 else None)

            def row_sums(key, x, rows, heads):
                dst, done = take(*key)
                for h in range(heads):
                    mm(dst[:heads, :T], cst("pick", 15 - h, heads, rows), x(h), h == 0, h == heads - 1, done if h == heads - 1 else None)

            def spread(key, row, rows, heads):
                dst, done = take(*key)
                mm(dst[:rows, :T], ident(heads)[:, row : row + 1].to_broadcast([heads, rows]), HR[:heads, :], done=done)

            def hgrn_norm(l):
                pe.wait_ge(sem("hgrn_squares"), l + 1)
                row_sums(("hgrn_var", l), sq, 128, 4)

            def hgrn_spread(l):
                pe.wait_ge(sem("row_roots"), 3 * l + 1)
                for h in range(4):
                    spread(("hgrn_root", l, h), h, 128, 4)

            def mla_norm(l):
                pe.wait_ge(sem("latent_squares"), 2 * l + 1)
                column_sums(("cq_var", l), lambda k: sq(4 + k), 2, T)
                pe.wait_ge(sem("latent_squares"), 2 * l + 2)
                column_sums(("ckv_var", l), lambda k: sq(6), 1, T)

            def mla_up(l):
                pe.wait_ge(sem("latents"), 2 * l + 1)
                for g in range(2):
                    w = chunk()
                    for h in range(4):
                        dst, done = take("q", l, 4 * g + h)
                        for k in range(2):
                            mm(dst[:QK, :T], w[:, 192 * h + 96 * k : 192 * h + 96 * k + 96], CQ[:, k, :], k == 0, k == 1, done if k else None)
                pe.wait_ge(sem("latents"), 2 * l + 2)
                w = chunk()
                for h in range(HEADS):
                    dst, done = take("k", l, h)
                    mm(dst[:NOPE, :T], w[:, 64 * h : 64 * h + 64], CKV[:, :], done=done)
                for i, (lo, n) in enumerate(TOK1):
                    dst, done = take("v", l, i)
                    mm(dst[:n, :], CKV[:, lo : lo + n], w[:, 512:1024], done=done)

            def head_norm(l, which):
                pe.wait_ge(sem("head_squares"), 2 * l + which + 1)
                row_sums(("head_var", l, which), lambda h: SQ[:QK, T * h : T * h + T], QK, HEADS)

            def head_spread(l, which):
                pe.wait_ge(sem("row_roots"), 3 * l + 2 + which)
                for h in range(HEADS):
                    spread(("head_root", l, which, h), h, QK, HEADS)

            def att_scores(l, h):
                if h == 0:
                    pe.wait_ge(sem("heads_ready"), 2 * l + 2)
                for i, (lo, n) in enumerate(TOK1):
                    dst, done = take("att", l, h, i)
                    mm(dst[:n, : lo + n], QH[:QK, h, lo : lo + n], KH[:QK, h, : lo + n], done=done)

            def att_turn(l, h):
                pe.wait_ge(sem("att_probs"), HEADS * l + h + 1)
                dst, done = take("att_turned", l, h)
                base = (0, T, T + T - 128)
                for i, (lo, n) in enumerate(TOK1):
                    for s in range(i + 1):
                        k = TOK1[s][1]
                        turn(dst[:k, base[s] + lo - 128 * s : base[s] + lo - 128 * s + n], P2[h % 3][:n, i, 128 * s : 128 * s + k], n,
                             done if (i, s) == (2, 2) else None)

            def att_values(l, p):
                dst, done = take("pv", l, p)
                for h in (2 * p, 2 * p + 1):
                    banks.await_read(pe, ("att_turned", l, h))
                    row = dst[64 * (h % 2) : 64 * (h % 2) + 64, :]
                    for s, (lo, k) in enumerate(TOK1):
                        b = (0, T, T + T - 128)[s]
                        mm(row[:, lo:T], MV[:k, s, 64 * h : 64 * h + 64], PT2[h % 2][:k, b : b + T - lo], s == 0, s == 2,
                           done if (h % 2, s) == (1, 2) else None)

            def mix_out(l):
                for m in range(KT):
                    project(("mix_out", l, m), (lambda k: (FN_HI[:, k, :], FN_LO[:, k, :])) if m else (lambda k: MIX[:, k, :]),
                            ready=(till("mixed", KT * l), till("mix_split", KT * l))[m] if m < 2 else None)

            def ff1(l, half):
                for m in range(FH * half, FH * half + FH):
                    project(("ff1", l, m), (lambda k: (FN_HI[:, k, :], FN_LO[:, k, :])) if m > 1 else hn,
                            ready=(till("normed", KT * (2 * l + 1)), None, till("norm_split", KT * l))[m] if m < 3 else None)

            def ff2(l, half):
                for m in range(KT):
                    project(("ff2", l, half, m), lambda k: (F1_HI[:, k, :], F1_LO[:, k, :]), chunks=2,
                            ready=None if m else till("hidden_split", FT * l + FH * half))

            ht = lambda k: HT[:, k, :]
            x_parts = lambda k: (X_HI[:, k, :], X_LO[:, k, :])
            x_tok = lambda k, lo, n: (X_HI[:, k, lo : lo + n], X_LO[:, k, lo : lo + n])
            ht_tok = lambda k, lo, n: HT[:, k, lo : lo + n]
            TOK2 = [(0, 128), (128, 128)]

            def ab_in():
                for i, name in enumerate(("aq", "ak")):
                    for j in range(4):
                        project((name, j), x_parts if i + j else ht, 256,
                                ready=(lambda k: banks.await_read(pe, ("ff2", DEPTH - 1, 1, k)), till("x_split", 0))[j] if i == 0 and j < 2 else None)
                tokens(("av",), ht_tok, TOK2)

            def bqk_in(j):
                project(("bqk", j), ht, 256)

            def bo_in(j):
                project(("bo", j), ht, 256)

            def bv_in():
                tokens(("bv",), ht_tok, TOK2)

            def if_in():
                at = PARAMS["wif"][0]
                for g in range(2):
                    dst, done = take("if", g)
                    for k in range(KT):
                        mm(dst[:4, :256], PAR[:, at + 8 * k + 4 * g : at + 8 * k + 4 * g + 4], ht(k), k == 0, k == 7, done if k == 7 else None)

            def gate_rows():
                pe.wait_ge(sem("gate_rows"), 1)
                dst, done = take("gate_cols")
                for i in range(2):
                    for a in range(2):
                        turn(dst[:, 8 * i + 4 * a : 8 * i + 4 * a + 4], ROWS[:4, 1 + a, 128 * i : 128 * i + 128], 4,
                             done if (i, a) == (1, 1) else None)

            def a_scores(h):
                if h == 0:
                    banks.await_read(pe, ("aq", 3))
                    banks.await_read(pe, ("ak", 3))
                rows = slice(64 * (h % 2), 64 * (h % 2) + 64)
                for i in range(2):
                    dst, done = take("a", h, i)
                    mm(dst[:, : 128 * i + 128], AQ[rows, h // 2, 128 * i : 128 * i + 128], AK[rows, h // 2, : 128 * i + 128], done=done)

            def turn_probs(key, ready, count, p):
                pe.wait_ge(sem(ready), count)
                dst, done = take(*key)
                for i, s, b in ((0, 0, 0), (1, 0, 128), (1, 1, 256)):
                    turn(dst[:, b : b + 128], p[:, i, 128 * s : 128 * s + 128], 128, done if s else None)

            def a_turn(h):
                turn_probs(("a_turned", h), "a_probs", h + 1, P[h % 2])

            def a_values(p):
                dst, done = take("a_pv", p)
                for h in (2 * p, 2 * p + 1):
                    banks.await_read(pe, ("a_turned", h))
                    row = dst[64 * (h % 2) : 64 * (h % 2) + 64, :]
                    mm(row[:, 0:256], AV[:, 0, 64 * h : 64 * h + 64], PT[h % 2][:, 0:256], True, False)
                    mm(row[:, 128:256], AV[:, 1, 64 * h : 64 * h + 64], PT[h % 2][:, 256:384], False, True, done if h % 2 else None)

            def b_scores(h):
                if h == 0:
                    pe.wait_ge(sem("bqk_ready"), 1)
                for i in range(2):
                    dst, done = take("b_row", h, i)
                    mm(dst[:, :256], ident(4)[:, h : h + 1].to_broadcast([4, 128]), ROWS[:4, 0, :], done=done)
                    dst, done = take("b", h, i)
                    mm(dst[:, : 128 * i + 128], BC[:, h, 128 * i : 128 * i + 128], BC[:, 4 + h, : 128 * i + 128], done=done)

            def b_turn(h):
                turn_probs(("b_turned", h), "b_weights", h + 1, P[2 + h % 2])

            def b_values(h):
                banks.await_read(pe, ("b_turned", h))
                dst, done = take("b_pv", h)
                mm(dst[:, 0:256], BV[:, 0, 128 * h : 128 * h + 128], PT[2 + h % 2][:, 0:256], True, False)
                mm(dst[:, 128:256], BV[:, 1, 128 * h : 128 * h + 128], PT[2 + h % 2][:, 256:384], False, True, done)

            def b_norm():
                for h in range(4):
                    banks.await_read(pe, ("b_pv", h))
                for g in range(2):
                    dst, done = take("b_mean", g)
                    mm(dst[:, :], ones(128, 128), YAB[:, 4 + 2 * g : 6 + 2 * g, :], done=done)
                pe.wait_ge(sem("b_squares"), 1)
                for g in range(2):
                    dst, done = take("b_var", g)
                    mm(dst[:, :], ones(128, 128), SQ[:, 512 * g : 512 * g + 512], done=done)

            def y_out(l):
                def ready(k):
                    if l:
                        banks.await_read(pe, ("c_pv", k))
                    elif k < 4:
                        banks.await_read(pe, ("a_pv", k))
                    else:
                        pe.wait_ge(sem("y_ready"), k - 3)

                for m in range(KT):
                    project(("y_out", l, m), x_parts if m else lambda k: YAB[:, k, :], 256,
                            ready=(ready, till("x_split", KT * (3 * l + 1)))[m] if m < 2 else None)

            def layer_norm(r):
                ready = till("moe_done", KT * (r // 2)) if r % 2 else lambda k: banks.await_read(pe, ("y_out", r // 2, k))
                column_sums(("ln_mean", r), ht, KT, 256, ready)
                column_sums(("ln_var", r), lambda k: sq(k, 256), KT, 256, till("ln_squares", KT * r))

            def router(l):
                pe.wait_ge(sem("ln_done"), KT * (2 * l + 1))
                at = PARAMS[f"router{l}"][0]
                for i in range(2):
                    dst, done = take("router", l, i)
                    mm(dst[:, :20], ones(1, 128), par(f"rbias{l}", 1), True, False)
                    for k in range(KT):
                        mm(dst[:, :20], ht_tok(k, 128 * i, 128), PAR[:, at + 20 * k : at + 20 * k + 20], False, k == 7, done if k == 7 else None)

            def expert_gates(l):
                pe.wait_ge(sem("expert_gates"), 2 * l + 2)
                dst, done = take("gates_turned", l)
                for i in range(2):
                    turn(dst[:16, 128 * i : 128 * i + 128], SM[:, 232 + 16 * i : 248 + 16 * i], 128, done if i else None)
                banks.await_read(pe, ("gates_turned", l))
                for e in range(NEXP):
                    dst, done = take("gate_row", l, e)
                    mm(dst[:, :256], ident(16)[:, e : e + 1].to_broadcast([16, 128]), GATT[:16, :], done=done)

            def gate_up(key):
                for j in range(4):
                    project((*key, "gate", j), x_parts, 256)
                    project((*key, "up", j), x_parts, 256)

            def down(key, buffer, count):
                half_projects((*key, "down"), lambda k: (HE_HI[:, buffer, k, :], HE_LO[:, buffer, k, :]), 256, ready=lambda k: pe.wait_ge(sem("hidden"), count + k + 1))

            def moe_lead(l):
                project(("moe", l, 0, "gate", 0), ht, 256, ready=till("ln_done", KT * 2 * l))

            def moe_first(l):
                for j in range(4):
                    if j:
                        project(("moe", l, 0, "gate", j), x_parts, 256)
                    project(("moe", l, 0, "up", j), x_parts, 256, ready=None if j else till("x_split", KT * (3 * l + 2)))

            def moe(l):
                first = (4 * NEXP + 8) * l + 8
                with pe.Fori(0, NEXP // 2 - 1) as i:
                    state["loop"], banks.loop = i, 4 * i
                    for j in range(2):
                        gate_up(("moe", l, 1 + j))
                        down(("moe", l, j), j, first + 4 * j + 8 * i)
                        splits.marks["moe", l, j, "end"] = (len(splits.chunks), state["n"])
                state["loop"] = banks.loop = None
                for _ in range(MOE_CHUNKS * (NEXP // 2 - 2)):
                    splits.chunks.append(state["n"])
                    state["n"] += 1
                banks.uses = [n + 4 * (NEXP // 2 - 2) for n in banks.uses]
                gate_up(("moe", l, NEXP - 1))
                for e in (NEXP - 2, NEXP - 1):
                    down(("moe", l, e), e % 2, first + 4 * e)

            def c_in():
                for j in range(4):
                    project(("c_src", j), x_parts if j else ht, 256, ready=(till("ln_done", KT), till("x_split", 3 * KT))[j] if j < 2 else None)
                for j in range(8):
                    project(("c_q", j), x_parts, 256)
                for j in range(4):
                    project(("c_k", j), x_parts, 256)
                tokens(("c_v",), x_tok, TOK2)
                at = PARAMS["wcg"][0]
                for i in range(2):
                    dst, done = take("c_gate", i)
                    mm(dst[:, :24], ones(1, 128), par("cgbias", 1), True, False)
                    for k in range(KT):
                        mm(dst[:, :24], ht_tok(k, 128 * i, 128), PAR[:, at + 24 * k : at + 24 * k + 24], False, k == 7, done if k == 7 else None)

            def compress(s):
                pe.wait_ge(sem("blocks"), s + 1)
                dst, done = take("c_hidden", s)
                for c in range(8):
                    w = chunk()
                    for j in range(4):
                        n = 4 * c + j
                        mm(dst[:30, :256], BLK[:, n, :], w[:, 256 * j : 256 * j + 256], n == 0, n == 31, done if n == 31 else None)

            def compress2():
                w = chunk()
                for s in range(2):
                    pe.wait_ge(sem("c_gelu"), s + 1)
                    dst, done = take("c_hidden_turned", s)
                    for j in range(2):
                        turn(dst[:, 32 * j : 32 * j + 30], CHID[:30, 2 * s, 128 * j : 128 * j + 128], 30, done if j else None)
                    banks.await_read(pe, ("c_hidden_turned", s))
                    hid = CHID[:, 2 * s + 1, :]
                    for g in range(1 + s):
                        dst, done = take("c_cmp", s, g)
                        for j in range(2):
                            wt = w[:, 256 * s + 128 * j : 256 * s + 128 * j + 128]
                            if s == 0:
                                mm(dst[:, :30], wt, hid[:, 32 * j : 32 * j + 30], j == 0, j == 1, done if j else None)
                            else:
                                mm(dst[:15, :128], hid[:, 32 * j + 15 * g : 32 * j + 15 * g + 15], wt, j == 0, j == 1, done if j else None)

            def c_scores(h):
                g = h // 4
                if h == 0:
                    for key in (("c_q", 7), ("c_k", 3), ("c_cmp", 0, 0), ("c_cmp", 1, 1)):
                        banks.await_read(pe, key)
                for i in range(2):
                    q = AQ[:, h, 128 * i : 128 * i + 128]
                    for b in range(2):
                        dst, done = take("c", h, i, b)
                        mm(dst[:, : 128 * i + 128], q, AK[:, 2 * b + g, : 128 * i + 128], done=done)
                dst, done = take("c_c", h)
                for i in range(2):
                    mm(dst[:, 16 * i : 16 * i + 15], AQ[:, h, 128 * i : 128 * i + 128], KC[:, 15 * g : 15 * g + 15], done=done if i else None)

            def c_turn(h):
                for b in range(2):
                    turn_probs(("c_turned", h, b), "c_probs", 3 * h + b + 1, P[2 * (h % 3) + b])
                pe.wait_ge(sem("c_probs"), 3 * h + 3)
                dst, done = take("c_turned", h, 2)
                for i in range(2):
                    turn(dst[:15, 128 * i : 128 * i + 128], PC[h % 3][:, i, :15], 128, done if i else None)

            def c_values(h):
                g = h // 4
                dst, done = take("c_pv", h)
                for b in range(2):
                    banks.await_read(pe, ("c_turned", h, b))
                    v = 256 * b + 128 * g
                    mm(dst[:, 0:256], AV[:, 0, v : v + 128], PT[2 * (h % 2) + b][:, 0:256], b == 0, False)
                    mm(dst[:, 128:256], AV[:, 1, v : v + 128], PT[2 * (h % 2) + b][:, 256:384], False, False)
                banks.await_read(pe, ("c_turned", h, 2))
                mm(dst[:, 0:256], VC[:15, g, :], PCT[h % 2][:15, :], False, True, done)

            steps = locals()
            for name, *args in SCHEDULE:
                if name in steps:
                    steps[name](*args)
                splits.marks["step", name, *args] = (len(splits.chunks), state["n"])
            splits.known = frozenset(splits.chunks)
            assert state["n"] == n_chunks, (state["n"], n_chunks)

        def bc(ap, shape):
            return ap.to_broadcast(shape)

        SCALE_MLA = QK ** -0.5

        def tap(l, j, i):
            return HC[:, j, i : i + T], par(f"convw{l}")[:, CONV_K * j + i : CONV_K * j + i + 1], par(f"convb{l}")[:, j : j + 1]

        @block.scalar
        def _(act):
            lane = Lane(act, sem("scalar_step"))
            loop = {"v": None, "i": None}

            def split(s, n):
                i = loop["i"]
                value = 16 * (n // RING + 1)
                act.wait_ge(arrived[n % RING], value if i is None else value + 16 * (MOE_CHUNKS // RING) * i)
                if s >= SPLIT:
                    act.wait_ge(split_used, s - SPLIT + 1 if i is None else s - SPLIT + 1 + MOE_CHUNKS * i)
                lane(nc.scalar.activation(W_HI[:, s % SPLIT, :], ring[:, n % RING, :], ACT.Copy), split_hi)

            follow = Follower(splits, split)

            def fn(dst, src, f, sem_=None, **kw):
                lane(nc.scalar.activation(dst, src, f, **kw), sem_)

            def fn_free(dst, src, f, key, **kw):
                nc.scalar.activation(dst, src, f, **kw).then_inc(banks.freed(key), 1)
                banks.await_read(act, key, loop["v"])
                follow(key)

            def wait_bank(*key):
                return banks.await_(act, key, loop["v"])

            def evacuate(key, dst, n=T, f=ACT.Copy, rows=128, **kw):
                fn_free(dst, wait_bank(*key)[:rows, :n], f, key, **kw)

            def root(key, dst, n, count, rows=128, eps=0):
                evacuate(key, dst, n, ACT.Sqrt, rows, scale=1.0 / count, bias=cst("eps", eps, 1, rows))

            def start():
                act.wait_ge(sem("lower_bound_args"), 1)
                fn(ST[:, 8:16], ST[:, 8:16], ACT.Exp, sem("lower_bound_exps"))

            def hankel():
                wait_bank("norm", 2 * DEPTH - 1)
                hankel_ = bass.AP(scratch.tensor, 0, [[1, 128], [384, HEADS], [1, 256]])
                act.dma_start(SQ[:, : 8 * 256].rearrange("p (h c) -> p h c", h=8), hankel_).then_inc(sem("hankel"), 16)

            def store_bias():
                banks.await_read(act, ("bucket_bias",))
                act.dma_start(scratch, MIX[:HEADS, 0:2, :].rearrange("p a b -> p (a b)")[:, :384]).then_inc(sem("bias_stored"), 16)
                act.wait_ge(sem("bias_stored"), 16)

            def norm(r):
                if r == 0:
                    act.wait_ge(sem("x_loaded"), 16)
                for k in range(KT):
                    if r % 2:
                        banks.await_read(act, ("mix_out", r // 2, k))
                    elif r:
                        banks.await_read(act, ("ff2", r // 2 - 1, 1, k))
                    fn(SQ[:, T * k : T * k + T], XT[:, k, :], ACT.Square, sem("norm_squares"))
                root(("norm", r), RS[:, :T], T, D)

            def conv_in(l):
                for j in range(4):
                    evacuate(("conv_g", l, j), MIX[:, j, :], f=ACT.Sigmoid)

            def hgrn_in(l):
                for j in range(4):
                    evacuate(("hf", l, j), HK[:, j, :T], f=ACT.Sigmoid, scale=-1.0)
                for j in range(4):
                    evacuate(("hq", l, j), HQ[:, j, :T])
                for j in range(4):
                    evacuate(("hg", l, j), HG[:, j, :], f=ACT.Silu)
                for i, (_, n) in enumerate(TOK1):
                    evacuate(("hi", l, i), HV[:n, i, :], 512, ACT.Silu, n)

            def mla_in(l):
                for j in range(2):
                    src = wait_bank("cq", l, j)
                    fn(SQ[:, T * (4 + j) : T * (5 + j)], src[:, :T], ACT.Square, sem("latent_squares") if j else None)
                    fn_free(CQ[:, j, :], src[:, :T], ACT.Copy, ("cq", l, j))
                src = wait_bank("ckv", l)
                fn(SQ[:, T * 6 : T * 7], src[:, :T], ACT.Square, sem("latent_squares"))
                fn_free(CKV[:, :], src[:, :T], ACT.Copy, ("ckv", l))
                fn_free(KR[NOPE:QK, :], wait_bank("rope", l)[NOPE:QK, :T], ACT.Copy, ("rope", l))

            def gate(l, b, m):
                if b == 2:
                    banks.await_read(act, ("branch", l, 0, m))
                elif l:
                    act.wait_ge(sem(("mixed", "gated")[b]), KT * (l - 1) + m + 1)
                evacuate(("gate", l, b, m), GATES[b % 2][:, m, :], f=ACT.Copy if b == 1 else ACT.Sigmoid)

            def hgrn_gates(l):
                fn(GATES[1][:, :, :], GATES[1][:, :, :], ACT.Sigmoid, sem("hgrn_gates"))

            def conv_norm(l):
                act.wait_ge(sem("conv_centered"), l + 1)
                fn(SQ[:, : 4 * T], CO[:, :, :].rearrange("p k t -> p (k t)"), ACT.Square, sem("conv_squares"))
                root(("conv_var", l), RS[:, :T], T, 512)
                act.wait_ge(sem("conv_scaled"), l + 1)
                for j in range(4):
                    fn(CO[:, j, :], CO[:, j, :], ACT.Silu, sem("conv_done"),
                       scale=par(f"clng{l}")[:, j : j + 1], bias=par(f"clnb{l}")[:, j : j + 1])

            def hgrn_prep(l):
                act.wait_ge(sem("clamped"), l + 1)
                fn(HB[:, :, :T], HB[:, :, :T], ACT.Ln, sem("logs"), scale=-1.0, bias=1.0)
                act.wait_ge(sem("strip_args"), l + 1)
                fn(HKK[:, :, :], HKK[:, :, :], ACT.Exp, sem("strip_exps"))

            def hgrn_args(l, i):
                act.wait_ge(sem("clamped_args"), NB * l + i + 1)
                n = 1024 + 4 * SB * i
                fn(HD[i % 3][:, :n], HD[i % 3][:, :n], ACT.Exp, sem("decay_exps"))

            def hgrn_turn(l, i):
                n = -(-SB * (i + 1) // 128)
                src = wait_bank("turned", l, i)[:, : 128 * n].rearrange("p (s h t) -> p s h t", s=n, h=4)
                fn_free(HAT[:, :n, :, SB * i : SB * i + SB], src, ACT.Copy, ("turned", l, i))

            def hgrn_values(l):
                for h in range(4):
                    evacuate(("ho", l, h), HO[:, h, :T])
                fn(SQ[:, : 4 * T].rearrange("p (h t) -> p h t", h=4), HO[:, :, :T], ACT.Square, sem("hgrn_squares"))

            def hgrn_norm(l):
                root(("hgrn_var", l), HR[:4, :], T, 128, 4)

            def mla_norm(l):
                root(("cq_var", l), RS[:, :T], T, 256)
                root(("ckv_var", l), MU[:, :T], T, 128)

            def mla_up(l):
                for h in range(HEADS):
                    evacuate(("q", l, h), QH[:QK, h, :], rows=QK)
                fn(KH[NOPE:QK, :, :], bc(KR[NOPE:QK, None, :], [ROPE, HEADS, T]), ACT.Copy)
                for h in range(HEADS):
                    evacuate(("k", l, h), KH[:NOPE, h, :], rows=NOPE)
                for i, (_, n) in enumerate(TOK1):
                    evacuate(("v", l, i), MV[:n, i, :], 512, rows=n)

            def head_norm(l, which):
                src = (QH, KH)[which][:QK, :, :].rearrange("p h t -> p (h t)")
                if which:
                    wait_bank("head_var", l, 0)
                fn(SQ[:QK, : HEADS * T], src, ACT.Square, sem("head_squares"))
                wait_bank(*(("head_root", l, 0, HEADS - 1) if which else ("hgrn_root", l, 3)))
                root(("head_var", l, which), HR[:HEADS, :], T, QK, HEADS)

            def att_scores(l, h):
                act.wait_ge(sem("att_max"), HEADS * l + h + 1)
                s = 16 * (h % 3)
                for i, (lo, n) in enumerate(TOK1):
                    p = P2[h % 3][:n, i, : lo + n]
                    fn(p, p, ACT.Exp, sem("att_exps"), scale=SCALE_MLA, bias=SM[:n, s + 4 + i : s + 5 + i], accum_out=SM[:n, s + 8 + i : s + 9 + i])

            def att_turn(l, h):
                src = wait_bank("att_turned", l, h)
                if h >= 2:
                    wait_bank("pv", l, h // 2 - 1)
                n = T + T - 128
                fn(PT2[h % 2][:, :n], src[:, :n], ACT.Copy)
                fn_free(PT2[h % 2][:16, n : n + 16], src[:16, n : n + 16], ACT.Copy, ("att_turned", l, h))

            def att_values(l, p):
                evacuate(("pv", l, p), OT[:, p, :])

            def ff1(l, half):
                for m in range(FH * half, FH * half + FH):
                    if FT * l + m >= 4:
                        act.wait_ge(sem("hidden_split"), FT * l + m - 3)
                    evacuate(("ff1", l, m), F1[:, m % 4, :], f=ACT.Relu)

            def ff2(l, half):
                for m in range(KT):
                    wait_bank("ff2", l, half, m)
                    follow(("ff2", l, half, m))

            def ab_in():
                for j in range(4):
                    evacuate(("aq", j), AQ[:, j, :], 256, scale=A_SCALE)
                for j in range(4):
                    evacuate(("ak", j), AK[:, j, :], 256)
                for i in range(2):
                    evacuate(("av", i), AV[:, i, :], 512)

            def bqk_in(j):
                evacuate(("bqk", j), BIN[:, j, 3:259], 256)

            def bv_in():
                for i in range(2):
                    evacuate(("bv", i), BV[:, i, :], 512)

            def bo_in(j):
                evacuate(("bo", j), SBO[:, j, :], 256, ACT.Sigmoid)

            def b_gates():
                act.wait_ge(sem("forget_abs"), 1)
                fn(ROWS[:4, 5, :], ROWS[:4, 5, :], ACT.Exp, scale=-1.0)
                fn(ROWS[:4, 5, :], ROWS[:4, 5, :], ACT.Ln, sem("forget_logs"), bias=1.0)

            def gate_rows():
                banks.await_read(act, ("gate_cols",))
                floors = COLS[:, :].rearrange("p (i c) -> p i c", i=2)[:, :, 4:8]
                fn(floors, floors, ACT.Exp, sem("floors"))

            def b_conv():
                act.wait_ge(sem("b_convolved"), 1)
                fn(BC[:, :, :], BC[:, :, :], ACT.Silu, sem("b_silu"))

            def a_scores(h):
                act.wait_ge(sem("a_max"), h + 1)
                s = 32 + 16 * (h % 2)
                for i in range(2):
                    p = P[h % 2][:, i, : 128 * i + 128]
                    fn(p, p, ACT.Exp, sem("a_exps"), bias=SM[:, s + 4 + i : s + 5 + i], accum_out=SM[:, s + 8 + i : s + 9 + i])

            def turned(key, dst, before):
                src = wait_bank(*key)
                if before is not None:
                    wait_bank(*before)
                fn_free(dst[:, :384], src[:, :384], ACT.Copy, key)

            def a_turn(h):
                turned(("a_turned", h), PT[h % 2], ("a_pv", h // 2 - 1) if h >= 2 else None)

            def a_values(p):
                evacuate(("a_pv", p), YAB[:, p, :], 256)

            def b_scores(h):
                if h == 0:
                    act.wait_ge(sem("floors"), 1)
                for i in range(2):
                    act.wait_ge(sem("b_masked"), 2 * h + i + 1)
                    p = P[2 + h % 2][:, i, : 128 * i + 128]
                    fn(p, p, ACT.Exp, sem("b_exps"), bias=COLS[:, 8 * i + h : 8 * i + h + 1])

            def b_turn(h):
                turned(("b_turned", h), PT[2 + h % 2], ("b_pv", h - 2) if h >= 2 else None)

            def b_values(h):
                evacuate(("b_pv", h), YAB[:, 4 + h, :], 256)

            def b_norm():
                act.wait_ge(sem("b_centered"), 1)
                fn(SQ[:, :1024], YAB[:, 4:8, :].rearrange("p h t -> p (h t)"), ACT.Square, sem("b_squares"))
                for g in range(2):
                    root(("b_var", g), AQ[:, 2 * g : 2 * g + 2, :].rearrange("p h t -> p (h t)"), 512, 128, eps=1)

            def layer_norm(r):
                for k in range(KT):
                    act.wait_ge(sem("ln_centered"), KT * r + k + 1)
                    fn(SQ[:, 256 * k : 256 * k + 256], HT[:, k, :], ACT.Square, sem("ln_squares"))
                root(("ln_var", r), RS[:, :256], 256, D, eps=1)
                l, j = r // 2, r % 2
                for k in range(KT):
                    act.wait_ge(sem("ln_scaled"), KT * r + k + 1)
                    fn(HT[:, k, :], HT[:, k, :], ACT.Identity, sem("ln_done"),
                       scale=par(f"lng{j}_{l}")[:, k : k + 1], bias=par(f"lnb{j}_{l}")[:, k : k + 1])

            def router(l):
                for i in range(2):
                    act.wait_ge(sem("group_max"), l + 1)
                    s = RT[:, 56 + 4 * i : 60 + 4 * i]
                    fn(s, RT[:, 20 * i : 20 * i + 4], ACT.Exp, sem("group_exps"), bias=RT[:, 42 + i : 43 + i], accum_out=RT[:, 44 + i : 45 + i])
                act.wait_ge(sem("top_gap"), l + 1)
                fn(RT[:, 46:48], RT[:, 46:48], ACT.Exp, sem("top_exps"))

            def expert_gates(l):
                evacuate(("gates_turned", l), GATT[:16, :], 256, rows=16)
                for e in range(NEXP):
                    evacuate(("gate_row", l, e), GB[:, e, :], 256)

            def silu_gates(key, j, loop_):
                for t in range(4):
                    act.wait_ge(sem("hidden"), j + t + 1 if loop_ is None else j + t + 1 + loop_)
                    evacuate((*key, "gate", t), SGM[:, t, :], 256, ACT.Silu)
                    follow((*key, "up", t))

            def moe_first(l):
                silu_gates(("moe", l, 0), (4 * NEXP + 8) * l + 4, None)

            def moe(l):
                first = (4 * NEXP + 8) * l + 8
                with act.Fori(0, NEXP // 2 - 1) as i:
                    loop["v"], loop["i"] = 4 * i, i
                    lane.enter(i, {"split_hi": MOE_CHUNKS})
                    for j in range(2):
                        silu_gates(("moe", l, 1 + j), first + 4 * j, 8 * i)
                        follow(("moe", l, j, "end"))
                    lane.leave(NEXP // 2 - 1)
                loop["v"] = loop["i"] = None
                follow.next += MOE_CHUNKS * (NEXP // 2 - 2)
                silu_gates(("moe", l, NEXP - 1), first + 4 * (NEXP - 2), None)

            def c_in():
                for j in range(4):
                    evacuate(("c_src", j), BIN[:, j, :256], 256)
                for j in range(8):
                    evacuate(("c_q", j), AQ[:, j, :], 256, scale=C_SCALE)
                for j in range(4):
                    evacuate(("c_k", j), AK[:, j, :], 256)
                follow(("c_v", "chunks"))
                for i in range(2):
                    evacuate(("c_v", i), AV[:, i, :], 512)
                for i in range(2):
                    evacuate(("c_gate", i), CG[:, i, :], 24, ACT.Sigmoid)

            def compress(s):
                src = wait_bank("c_hidden", s)
                fn(CHID[:30, 2 * s, :], src[:30, :256], ACT.Gelu_apprx_tanh, sem("c_gelu"))

            def compress2():
                for s in range(2):
                    src = wait_bank("c_hidden_turned", s)[:, :64].rearrange("p (j n) -> p j n", j=2)[:, :, :30]
                    fn_free(CHID[:, 2 * s + 1, :64].rearrange("p (j n) -> p j n", j=2)[:, :, :30], src, ACT.Copy, ("c_hidden_turned", s))
                    for g in range(1 + s):
                        if s == 0:
                            evacuate(("c_cmp", s, g), KC[:, :], 30)
                        else:
                            evacuate(("c_cmp", s, g), VC[:15, g, :], 128, rows=15)

            def c_scores(h):
                act.wait_ge(sem("c_max"), h + 1)
                s = 64 + 20 * (h % 3)
                for b in range(3):
                    for i in range(2):
                        p = PC[h % 3][:, i, : 7 + 8 * i] if b == 0 else P[2 * (h % 3) + b - 1][:, i, : 128 * i + 128]
                        c = 2 * b + i
                        fn(p, p, ACT.Exp, sem("c_exps"), bias=SM[:, s + 6 + c : s + 7 + c], accum_out=SM[:, s + 12 + c : s + 13 + c])

            def c_turn(h):
                before = ("c_pv", h - 2) if h >= 2 else None
                for b in range(2):
                    turned(("c_turned", h, b), PT[2 * (h % 2) + b], before)
                evacuate(("c_turned", h, 2), PCT[h % 2][:15, :], 256, rows=15)

            def c_values(h):
                evacuate(("c_pv", h), YAB[:, h, :], 256)

            steps = locals()
            for name, *args in SCHEDULE:
                follow.paused = name in ("blocks", "compress", "compress2")
                if name == "c_scores" and args == [0]:
                    follow(("step", "compress2"))
                if name in steps:
                    steps[name](*args)
                follow(("step", name, *args))

        @block.vector
        def _(dve):
            lane = Lane(dve, sem("vector_step"))
            loop = {"v": None, "i": None}

            def split(s, n):
                i = loop["i"]
                dve.wait_ge(split_hi, s + 1 if i is None else s + 1 + MOE_CHUNKS * i)
                lane(nc.vector.tensor_tensor(W_LO[:, s % SPLIT, :], ring[:, n % RING, :], W_HI[:, s % SPLIT, :].bitcast(F32), ALU.subtract), split_lo)

            follow = Follower(splits, split)

            def tt(dst, a, b, op, done=None):
                lane(nc.vector.tensor_tensor(dst, a, b, op), done)

            def ts(dst, a, s1, s2, op0, op1=None, done=None):
                ins = nc.vector.tensor_scalar(dst, a, s1, s2, op0) if op1 is None else nc.vector.tensor_scalar(dst, a, s1, s2, op0, op1)
                lane(ins, done)

            def stt(dst, a, s, b, op0, op1, done=None):
                lane(nc.vector.scalar_tensor_tensor(dst, a, s, b, op0, op1), done)

            def ttr(dst, a, b, op0, op1, init, acc, done=None):
                lane(nc.vector.tensor_tensor_reduce(dst, a, b, 1.0, init, op0, op1, acc), done)

            def wait_bank(*key):
                return banks.await_(dve, key, loop["v"])

            def free(ins, *key):
                ins.then_inc(banks.freed(key), 1)
                banks.await_read(dve, key, loop["v"])
                follow(key)

            def split_tile(hi, lo, x, done):
                lane(nc.vector.tensor_copy(hi, x))
                tt(lo, x, hi.bitcast(F32), ALU.subtract, done)

            def mean(key, dst, n, count):
                src = wait_bank(*key)
                free(nc.vector.tensor_scalar(dst, src[:, :n], 1.0 / count, None, ALU.mult), *key)

            def reciprocal_root(key, ap):
                banks.await_read(dve, key)
                lane(nc.vector.reciprocal(ap, ap))

            def zeros():
                lane(nc.vector.memset(HC[:, :, : CONV_K - 1], 0.0))
                for t in (HB, HK, HQ):
                    lane(nc.vector.memset(t[:, :, T:TP], 0.0))

            def start():
                zeros()
                lane(nc.vector.memset(SM[:, :], 0.0))
                l0, l1 = par("lb0"), par("lb1")
                tt(ST[:, 16:20], l0, l1, ALU.max)
                tt(ST[:, 8:12], l0, ST[:, 16:20], ALU.subtract)
                tt(ST[:, 12:16], l1, ST[:, 16:20], ALU.subtract, sem("lower_bound_args"))
                dve.wait_ge(sem("lower_bound_exps"), 1)
                tt(ST[:, 16:20], ST[:, 8:12], ST[:, 12:16], ALU.add)
                lane(nc.vector.reciprocal(ST[:, 16:20], ST[:, 16:20]))
                tt(ST[:, 8:12], ST[:, 8:12], ST[:, 16:20], ALU.mult)
                tt(ST[:, 12:16], ST[:, 12:16], ST[:, 16:20], ALU.mult)
                tt(ST[:, 12:16], ST[:, 8:12], ST[:, 12:16], ALU.add)
                tt(ST[:, 20:24], ST[:, 8:12], ST[:, 8:12], ALU.subtract)
                tt(ST[:, 24:28], ST[:, 12:16], ST[:, 8:12], ALU.subtract)
                ts(ST[:, 0:8], ST[:, 20:28], -1.0, 1.0, ALU.mult, ALU.add)
                src = wait_bank("bucket_bias")
                flat = MIX[:HEADS, 0:2, :].rearrange("p a b -> p (a b)")[:, :384]
                free(nc.vector.tensor_copy(flat, src[:HEADS, :384]), "bucket_bias")

            def bias():
                for g in range(4):
                    src = wait_bank("bias", g)[:, :].rearrange("p (h c) -> p h c", h=2)
                    mask = bc(cst("causal", 128, 256)[:, None, :], [128, 2, 256])
                    count = bc(cst("logcount")[:, None, :], [128, 2, 256])
                    tt(BIAS_C[:, 2 * g : 2 * g + 2, :], src, mask, ALU.add)
                    free(nc.vector.tensor_tensor(BIAS_A[:, 2 * g : 2 * g + 2, :], src, count, ALU.add), "bias", g)

            def norm(r):
                if r == 0:
                    dve.wait_ge(sem("x_loaded"), 16)
                    dve.wait_ge(sem("loaded"), 32)
                reciprocal_root(("norm", r), RS[:, :T])
                g = par(f"norm{1 + r % 2}{r // 2}")
                for k in range(KT):
                    stt(HN[:, k, :], XT[:, k, :], g[:, k : k + 1], RS[:, :T], ALU.mult, ALU.mult, sem("normed"))
                if r % 2:
                    for k in range(KT):
                        split_tile(FN_HI[:, k, :], FN_LO[:, k, :], HN[:, k, :], sem("norm_split"))
                if r == 2:
                    zeros()

            def conv_in(l):
                for j in range(4):
                    src = wait_bank("conv_a", l, j)
                    banks.await_read(dve, ("conv_g", l, j))
                    free(nc.vector.tensor_tensor(HC[:, j, CONV_K - 1 :], src[:, :T], MIX[:, j, :], ALU.mult), "conv_a", l, j)

            def conv_taps(l):
                for j in range(3):
                    for i in range(CONV_K):
                        x, w, b = tap(l, j, i)
                        if i == 0:
                            ts(CO[:, j, :], x, w, b, ALU.mult, ALU.add)
                        else:
                            stt(CO[:, j, :], x, w, CO[:, j, :], ALU.mult, ALU.add, sem(f"conv_out{j}") if i == CONV_K - 1 else None)

            def conv_norm(l):
                mean(("conv_mean", l), MU[:, :T], T, 512)
                tt(CO[:, :, :], CO[:, :, :], bc(MU[:, None, :T], [128, 4, T]), ALU.subtract, sem("conv_centered"))
                reciprocal_root(("conv_var", l), RS[:, :T])
                tt(CO[:, :, :], CO[:, :, :], bc(RS[:, None, :T], [128, 4, T]), ALU.mult, sem("conv_scaled"))

            def branch_out(l, b, c):
                gate_ = GATES[b % 2]
                for m in (2 * c, 2 * c + 1):
                    src = wait_bank("branch", l, b, m)
                    if b == 1:
                        dve.wait_ge(sem("hgrn_gates"), l + 1)
                    banks.await_read(dve, ("gate", l, b, m))
                    free(nc.vector.tensor_tensor((gate_ if b else MIX)[:, m, :], src[:, :T], gate_[:, m, :], ALU.mult), "branch", l, b, m)
                    if b == 1:
                        tt(MIX[:, m, :], MIX[:, m, :], gate_[:, m, :], ALU.add, sem("gated"))
                    if b == 2:
                        tt(MIX[:, m, :], MIX[:, m, :], gate_[:, m, :], ALU.add, sem("mixed"))
                        split_tile(FN_HI[:, m, :], FN_LO[:, m, :], MIX[:, m, :], sem("mix_split"))

            def hgrn_prep(l):
                for j in range(4):
                    banks.await_read(dve, ("hf", l, j))
                    ts(HK[:, j, :T], HK[:, j, :T], ST[:, 4 * l + j : 4 * l + j + 1], None, ALU.mult)
                ts(HB[:, :, :T], HK[:, :, :T], CLAMP, None, ALU.min, done=sem("clamped"))
                for a in HA:
                    lane(nc.vector.memset(a, 0.0))
                if l:
                    lane(nc.vector.memset(HB[:, :, T:TP], 0.0))
                dve.wait_ge(sem("logs"), l + 1)
                one = bc(cst("ones", 0, 1), [128, TP])
                for j in range(4):
                    lane(nc.vector.tensor_tensor_scan(HB[:, j, :], one, HB[:, j, :], 0.0, ALU.mult, ALU.add), sem("summed") if j == 3 else None)
                s4 = HB[:, :, :].rearrange("p h (g f) -> p (h g) f", f=SS)
                k4 = HKK[:, :, :].rearrange("p h (g f) -> p (h g) f", f=SS)
                tt(k4, bc(s4[:, :, 0:1], [128, 4 * TP // SS, SS]), s4, ALU.subtract, sem("strip_args"))
                dve.wait_ge(sem("strip_exps"), l + 1)
                tt(HKK[:, :, :], HKK[:, :, :], HK[:, :, :], ALU.mult)
                banks.await_read(dve, ("hq", l, 3))

            def hgrn_clamp(l, i):
                dve.wait_ge(sem("decay_args"), NB * l + i + 1)
                ts(HD[i % 3][:, :1024], HD[i % 3][:, :1024], 0.0, None, ALU.min, done=sem("clamped_args"))

            def hgrn_args(l, i):
                dve.wait_ge(sem("decay_exps"), NB * l + i + 1)
                d = HD[i % 3]
                qq = d[:, :1024].rearrange("p (j h t) -> p j h t", j=8, h=4)
                q = bc(HQ[:, None, :, SB * i : SB * i + SB], [128, 8, 4, SB])
                tt(qq, qq, q, ALU.mult, None if i else sem("decayed"))
                if i:
                    n = SB * i
                    kk = d[:, 1024 : 1024 + 4 * n].rearrange("p (h s) -> p h s", h=4)
                    tt(kk, kk, HK[:, :, :n], ALU.mult, sem("decayed"))

            def hgrn_block(l, i):
                src = wait_bank("scores", l, i)
                if i >= 2:
                    wait_bank("turned", l, i - 2)
                n = SB * i
                if i:
                    lane(nc.vector.tensor_copy(HA[i % 2][:, :n], src[:, :n]))
                free(nc.vector.tensor_tensor(HA[i % 2][:, n : n + SB], src[:, n : n + SB], cst("tri"), ALU.mult), "scores", l, i)

            def hgrn_norm(l):
                banks.await_read(dve, ("hgrn_var", l))
                lane(nc.vector.reciprocal(HR[:4, :], HR[:4, :]), sem("row_roots"))

            def hgrn_spread(l):
                for h in range(4):
                    src = wait_bank("hgrn_root", l, h)
                    free(nc.vector.tensor_tensor(HO[:, h, :T], src[:, :T], HO[:, h, :T], ALU.mult), "hgrn_root", l, h)
                    stt(HO[:, h, :T], HO[:, h, :T], par(f"hn{l}")[:, h : h + 1], HG[:, h, :], ALU.mult, ALU.mult, sem("hgrn_done"))

            def mla_norm(l):
                reciprocal_root(("cq_var", l), RS[:, :T])
                for k in range(2):
                    stt(CQ[:, k, :], CQ[:, k, :], par(f"qa{l}")[:, k : k + 1], RS[:, :T], ALU.mult, ALU.mult, sem("latents") if k else None)
                reciprocal_root(("ckv_var", l), MU[:, :T])
                stt(CKV[:, :], CKV[:, :], par(f"kva{l}"), MU[:, :T], ALU.mult, ALU.mult, sem("latents"))

            def head_norm(l, which):
                banks.await_read(dve, ("head_var", l, which))
                lane(nc.vector.reciprocal(HR[:HEADS, :], HR[:HEADS, :]), sem("row_roots"))

            def head_spread(l, which):
                x = (QH, KH)[which]
                for h in range(HEADS):
                    src = wait_bank("head_root", l, which, h)
                    ins = nc.vector.scalar_tensor_tensor(x[:QK, h, :], x[:QK, h, :], par(f"{'qk'[which]}n{l}", QK), src[:QK, :T], ALU.mult, ALU.mult)
                    free(ins, "head_root", l, which, h)
                r = slice(NOPE, QK)
                half = ROPE // 2
                shape = [ROPE, HEADS, T]
                c, s = CONSTS["cos"][0], CONSTS["sin"][0]
                lane(nc.vector.stream_shuffle(RSQ[r, :, :], x[r, :, :], [(i + half) % ROPE for i in range(ROPE)]))
                tt(RSQ[r, :, :], RSQ[r, :, :], bc(CST[r, None, s : s + T], shape), ALU.mult)
                tt(x[r, :, :], x[r, :, :], bc(CST[r, None, c : c + T], shape), ALU.mult)
                tt(x[r, :, :], x[r, :, :], RSQ[r, :, :], ALU.add, sem("heads_ready"))

            def att_scores(l, h):
                s = 16 * (h % 3)
                for i, (lo, n) in enumerate(TOK1):
                    src = wait_bank("att", l, h, i)
                    if i == 0 and h >= 3:
                        wait_bank("att_turned", l, h - 3)
                    ins = nc.vector.tensor_tensor_reduce(P2[h % 3][:n, i, : lo + n], src[:n, : lo + n], cst("causal", 256 - lo, lo + n)[:n, :],
                                                         1.0, NEG, ALU.add, ALU.max, SM[:n, s + i : s + i + 1])
                    free(ins, "att", l, h, i)
                ts(SM[:, s + 4 : s + 7], SM[:, s : s + 3], -SCALE_MLA, None, ALU.mult, done=sem("att_max"))

            def att_norm(l, h):
                s = 16 * (h % 3)
                dve.wait_ge(sem("att_exps"), 3 * (HEADS * l + h + 1))
                lane(nc.vector.reciprocal(SM[:128, s + 12 : s + 14], SM[:, s + 8 : s + 10]))
                lane(nc.vector.reciprocal(SM[:16, s + 14 : s + 15], SM[:16, s + 10 : s + 11]))
                for i, (lo, n) in enumerate(TOK1):
                    p = P2[h % 3][:n, i, : lo + n]
                    ts(p, p, SM[:n, s + 12 + i : s + 13 + i], None, ALU.mult, done=sem("att_probs") if i == 2 else None)

            def mix_out(l):
                for m in range(KT):
                    src = wait_bank("mix_out", l, m)
                    free(nc.vector.tensor_tensor(XT[:, m, :], src[:, :T], XT[:, m, :], ALU.add), "mix_out", l, m)

            def ff1(l, half):
                for m in range(FH * half, FH * half + FH):
                    follow(("ff1", l, m))
                    dve.wait_ge(sem("squared"), FT * l + m + 1)
                    j = m % FH
                    split_tile(F1_HI[:, j, :], F1_LO[:, j, :], F1[:, m % 4, :], sem("hidden_split"))

            def ff2(l, half):
                for m in range(KT):
                    src = wait_bank("ff2", l, half, m)
                    free(nc.vector.tensor_tensor(XT[:, m, :], src[:, :T], XT[:, m, :], ALU.add), "ff2", l, half, m)

            def b_gates():
                for row, g, name in ((4, 0, "ibias"), (3, 1, "fbias")):
                    src = wait_bank("if", g)
                    free(nc.vector.tensor_scalar(ROWS[:4, row, :], src[:4, :256], par(name, 4), None, ALU.add), "if", g)
                stt(ROWS[:4, 5, :], ROWS[:4, 3, :], -1.0, ROWS[:4, 3, :], ALU.mult, ALU.max, sem("forget_abs"))
                dve.wait_ge(sem("forget_logs"), 1)
                stt(ROWS[:4, 6, :], ROWS[:4, 3, :], 0.0, ROWS[:4, 5, :], ALU.min, ALU.subtract)
                lane(nc.vector.tensor_tensor_scan(ROWS[:4, 7, :], bc(cst("ones", 0, 1, 4), [4, 256]), ROWS[:4, 6, :], 0.0, ALU.mult, ALU.add))
                tt(ROWS[:4, 0, :], ROWS[:4, 4, :], ROWS[:4, 7, :], ALU.subtract)
                lane(nc.vector.tensor_tensor_scan(ROWS[:4, 1, :], ROWS[:4, 0, :], ROWS[:4, 0, :], 0.0, ALU.max, ALU.max))
                tt(ROWS[:4, 2, :], ROWS[:4, 7, :], ROWS[:4, 1, :], ALU.add)
                ts(ROWS[:4, 1:3, :], ROWS[:4, 1:3, :], -1.0, None, ALU.mult, done=sem("gate_rows"))

            def gate_rows():
                src = wait_bank("gate_cols")
                free(nc.vector.tensor_copy(COLS[:, :], src[:, :16]), "gate_cols")

            def b_conv():
                dve.wait_ge(sem("b_padding"), 1)
                w = par("abconv")
                for j in range(8):
                    banks.await_read(dve, ("bqk", j))
                    for i in range(4):
                        x, wi = BIN[:, j, i : i + 256], w[:, 4 * j + i : 4 * j + i + 1]
                        if i == 0:
                            ts(BC[:, j, :], x, wi, None, ALU.mult)
                        else:
                            stt(BC[:, j, :], x, wi, BC[:, j, :], ALU.mult, ALU.add, sem("b_convolved") if (i, j) == (3, 7) else None)
                dve.wait_ge(sem("b_silu"), 1)
                ts(BC[:, 0:4, :], BC[:, 0:4, :], C_SCALE, None, ALU.mult, done=sem("bqk_ready"))

            def masked_max(key, p, src, bias_, acc, first=None):
                if first is not None:
                    wait_bank(*first)
                lane(nc.vector.tensor_tensor_reduce(p, src, bias_, 1.0, NEG, ALU.add, ALU.max, acc))

            def a_scores(h):
                s = 32 + 16 * (h % 2)
                for i in range(2):
                    src = wait_bank("a", h, i)
                    if i == 0 and h >= 2:
                        wait_bank("a_turned", h - 2)
                    ins = nc.vector.tensor_tensor_reduce(P[h % 2][:, i, : 128 * i + 128], src[:, : 128 * i + 128], BIAS_A[:, h, 128 - 128 * i :],
                                                         1.0, NEG, ALU.add, ALU.max, SM[:, s + i : s + i + 1])
                    free(ins, "a", h, i)
                ts(SM[:, s + 4 : s + 6], SM[:, s : s + 2], -1.0, None, ALU.mult, done=sem("a_max"))

            def a_norm(h):
                s = 32 + 16 * (h % 2)
                dve.wait_ge(sem("a_exps"), 2 * (h + 1))
                lane(nc.vector.reciprocal(SM[:, s + 12 : s + 14], SM[:, s + 8 : s + 10]))
                for i in range(2):
                    p = P[h % 2][:, i, : 128 * i + 128]
                    ts(p, p, SM[:, s + 12 + i : s + 13 + i], None, ALU.mult, done=sem("a_probs") if i else None)

            def b_scores(h):
                for i in range(2):
                    src = wait_bank("b_row", h, i)
                    if i == 0 and h >= 2:
                        wait_bank("b_turned", h - 2)
                    n = 128 * i + 128
                    tt(P[2 + h % 2][:, i, :n], src[:, :n], cst("causal", 256 - 128 * i, n), ALU.add, sem("b_masked"))
                    free(nc.vector.memset(SM[:, 31:32], 0.0), "b_row", h, i)

            def b_norm_weights(h):
                s = 144
                for i in range(2):
                    p = P[2 + h % 2][:, i, : 128 * i + 128]
                    dve.wait_ge(sem("b_exps"), 2 * h + i + 1)
                    src = wait_bank("b", h, i)
                    free(nc.vector.tensor_tensor_reduce(p, src[:, : 128 * i + 128], p, 1.0, 0.0, ALU.mult, ALU.add, SM[:, s + i : s + i + 1]), "b", h, i)
                stt(SM[:, s : s + 2], SM[:, s : s + 2], -1.0, SM[:, s : s + 2], ALU.mult, ALU.max)
                floors = COLS[:, :].rearrange("p (i c) -> p i c", i=2)[:, :, 4 + h]
                tt(SM[:, s : s + 2], SM[:, s : s + 2], floors, ALU.max)
                lane(nc.vector.reciprocal(SM[:, s : s + 2], SM[:, s : s + 2]))
                for i in range(2):
                    p = P[2 + h % 2][:, i, : 128 * i + 128]
                    ts(p, p, SM[:, s + i : s + i + 1], None, ALU.mult, done=sem("b_weights") if i else None)

            def b_norm():
                y = YAB[:, 4:8, :]
                for g in range(2):
                    mean(("b_mean", g), AQ[:, 2 * g : 2 * g + 2, :].rearrange("p h t -> p (h t)"), 512, 128)
                tt(y, y, AQ[:, 0:4, :], ALU.subtract, sem("b_centered"))
                banks.await_read(dve, ("b_var", 0))
                reciprocal_root(("b_var", 1), AQ[:, 0:4, :])
                tt(y, y, AQ[:, 0:4, :], ALU.mult)
                for h in range(4):
                    stt(YAB[:, 4 + h, :], YAB[:, 4 + h, :], par("abhead")[:, h : h + 1], SBO[:, h, :], ALU.mult, ALU.mult, sem("y_ready"))
                for h in range(4):
                    split_y(4 + h)

            def split_a():
                wait_bank("ak", 3)
                for p in range(4):
                    banks.await_read(dve, ("a_pv", p))
                    split_y(p)

            def c_split(h):
                banks.await_read(dve, ("c_pv", h))
                split_y(h)

            def y_out(l):
                for m in range(KT):
                    src = wait_bank("y_out", l, m)
                    free(nc.vector.scalar_tensor_tensor(HT[:, m, :], HT[:, m, :], ALPHA, src[:, :256], ALU.mult, ALU.add), "y_out", l, m)

            def layer_norm(r):
                mean(("ln_mean", r), MU[:, :256], 256, D)
                for k in range(KT):
                    tt(HT[:, k, :], HT[:, k, :], MU[:, :256], ALU.subtract, sem("ln_centered"))
                reciprocal_root(("ln_var", r), RS[:, :256])
                for k in range(KT):
                    tt(HT[:, k, :], HT[:, k, :], RS[:, :256], ALU.mult, sem("ln_scaled"))

            def first_of(dst, x, top, scratch_):
                s4 = [128, 2, 4]
                tt(scratch_, x, bc(top, s4), ALU.is_equal)
                tt(scratch_, scratch_, bc(cst("rank")[:, None, :], s4), ALU.mult)
                lane(nc.vector.tensor_reduce(RT[:, 48:50], scratch_, AX.X, ALU.max))
                tt(dst, scratch_, bc(RT[:, 48:50, None], s4), ALU.is_equal)

            def router(l):
                s4 = [128, 2, 4]
                pair = lambda a, n=4: RT[:, a : a + 2 * n].rearrange("p (i j) -> p i j", i=2)
                for i in range(2):
                    src = wait_bank("router", l, i)
                    free(nc.vector.tensor_copy(RT[:, 20 * i : 20 * i + 20], src[:, :20]), "router", l, i)
                logits = RT[:, 0:40].rearrange("p (i c) -> p i c", i=2)
                lane(nc.vector.tensor_reduce(RT[:, 40:42], logits[:, :, 0:4], AX.X, ALU.max))
                ts(RT[:, 42:44], RT[:, 40:42], -1.0, None, ALU.mult, done=sem("group_max"))
                group = pair(64)
                first_of(group, logits[:, :, 0:4], RT[:, 40:42, None], pair(72))
                for i in range(2):
                    e = RT[:, 80:96].rearrange("p (g j) -> p g j", g=4)
                    tt(e, RT[:, 20 * i + 4 : 20 * i + 20].rearrange("p (g j) -> p g j", g=4), bc(RT[:, 64 + 4 * i : 68 + 4 * i, None], [128, 4, 4]), ALU.mult)
                    lane(nc.vector.tensor_reduce(RT[:, 96 + 4 * i : 100 + 4 * i], e.rearrange("p g j -> p j g"), AX.X, ALU.add))
                chosen = pair(96)
                lane(nc.vector.tensor_reduce(RT[:, 50:52], chosen, AX.X, ALU.max))
                one, two = pair(104), pair(112)
                first_of(one, chosen, RT[:, 50:52, None], pair(72))
                stt(RT[:, 96:104], RT[:, 104:112], NEG, RT[:, 96:104], ALU.mult, ALU.add)
                lane(nc.vector.tensor_reduce(RT[:, 52:54], chosen, AX.X, ALU.max))
                first_of(two, chosen, RT[:, 52:54, None], pair(72))
                tt(RT[:, 46:48], RT[:, 52:54], RT[:, 50:52], ALU.subtract, sem("top_gap"))
                dve.wait_ge(sem("top_exps"), l + 1)
                dve.wait_ge(sem("group_exps"), 2 * (l + 1))
                ts(RT[:, 50:52], RT[:, 46:48], 1.0, None, ALU.add)
                tt(RT[:, 50:52], RT[:, 50:52], RT[:, 44:46], ALU.mult)
                lane(nc.vector.reciprocal(RT[:, 50:52], RT[:, 50:52]))
                tt(RT[:, 52:54], RT[:, 50:52], RT[:, 46:48], ALU.mult)
                tt(one, one, bc(RT[:, 50:52, None], s4), ALU.mult)
                tt(two, two, bc(RT[:, 52:54, None], s4), ALU.mult)
                tt(one, one, two, ALU.add)
                for i in range(2):
                    e = SM[:, 232 + 16 * i : 248 + 16 * i].rearrange("p (g j) -> p g j", g=4)
                    tt(e, bc(RT[:, 64 + 4 * i : 68 + 4 * i, None], [128, 4, 4]), bc(RT[:, None, 104 + 4 * i : 108 + 4 * i], [128, 4, 4]),
                       ALU.mult, sem("expert_gates"))

            def hidden(key, buffer, gate_):
                for j in range(4):
                    follow((*key, "gate", j))
                    src = wait_bank(*key, "up", j)
                    free(nc.vector.tensor_tensor(HE[:, j, :], src[:, :256], gate_, ALU.mult), *key, "up", j)
                    banks.await_read(dve, (*key, "gate", j), loop["v"])
                    tt(HE[:, j, :], HE[:, j, :], SGM[:, j, :], ALU.mult)
                    split_tile(HE_HI[:, buffer, j, :], HE_LO[:, buffer, j, :], HE[:, j, :], sem("hidden"))

            def add_output(key):
                for m in range(KT):
                    src = wait_bank(*key, "down", m)
                    free(nc.vector.tensor_tensor(YT[:, m, :], src[:, :256], YT[:, m, :], ALU.add), *key, "down", m)

            def split_x(r):
                for k in range(KT):
                    if r >= 0:
                        dve.wait_ge(sem("ln_done"), KT * r + k + 1)
                    split_tile(X_HI[:, k, :], X_LO[:, k, :], HT[:, k, :], sem("x_split"))

            def split_y(k):
                split_tile(X_HI[:, k, :], X_LO[:, k, :], YAB[:, k, :], sem("x_split"))

            def moe_start(l):
                for j in range(8):
                    ts(YT[:, j, :], HT[:, j, :], ALPHA, None, ALU.mult, done=sem("hidden"))

            def moe_first(l):
                for j in range(4):
                    follow(("moe", l, 0, "gate", j))
                    src = wait_bank("moe", l, 0, "up", j)
                    banks.await_read(dve, ("moe", l, 0, "gate", j))
                    free(nc.vector.tensor_tensor(HE[:, j, :], src[:, :256], SGM[:, j, :], ALU.mult), "moe", l, 0, "up", j)

            def moe_hidden(l):
                banks.await_read(dve, ("gate_row", l, 0))
                for j in range(4):
                    tt(HE[:, j, :], HE[:, j, :], GB[:, 0, :], ALU.mult)
                    split_tile(HE_HI[:, 0, j, :], HE_LO[:, 0, j, :], HE[:, j, :], sem("hidden"))
                banks.await_read(dve, ("gate_row", l, NEXP - 1))

            def moe(l):
                gates = GB[:, :, :].rearrange("p e t -> p (e t)")
                with dve.Fori(0, NEXP // 2 - 1) as i:
                    loop["v"], loop["i"] = 4 * i, i
                    lane.enter(i, {"hidden": 8, "split_lo": MOE_CHUNKS, "vector_step": 16})
                    for j in range(2):
                        hidden(("moe", l, 1 + j), (1 + j) % 2, gates[:, bass.ds(512 * i + 256 * (1 + j), 256)])
                        add_output(("moe", l, j))
                    lane.leave(NEXP // 2 - 1)
                loop["v"] = loop["i"] = None
                follow.next += MOE_CHUNKS * (NEXP // 2 - 2)
                hidden(("moe", l, NEXP - 1), 1, GB[:, NEXP - 1, :])
                for e in (NEXP - 2, NEXP - 1):
                    add_output(("moe", l, e))
                for k in range(KT):
                    lane(nc.vector.tensor_copy(HT[:, k, :], YT[:, k, :]), sem("moe_done"))

            def blocks(s):
                for g in range(2):
                    banks.await_read(dve, ("c_src", 2 * s + g))
                if s:
                    wait_bank("c_hidden", 0)
                pos = par("pos")
                for g in range(2):
                    x = BIN[:, 2 * s + g, :256].rearrange("p (c r) -> p r c", r=16)
                    for a in range(2):
                        pv = pos[:, 32 * s + 16 * a : 32 * s + 16 * a + 16, None]
                        tt(BLK[:, 16 * a : 16 * a + 16, 15 * g : 15 * g + 15], x[:, :, a : a + 15], bc(pv, [128, 16, 15]), ALU.add,
                           sem("blocks") if (g, a) == (1, 1) else None)
                if s == 0:
                    for a in PC:
                        lane(nc.vector.memset(a, 0.0))

            def compress(s):
                dve.wait_ge(sem("c_gelu"), s + 1)
                free(nc.vector.memset(SM[:, 31:32], 0.0), "c_hidden", s)

            def c_scores(h):
                s = 64 + 20 * (h % 3)
                if h >= 3:
                    wait_bank("c_turned", h - 3, 2)
                for i in range(2):
                    n = 128 * i + 128
                    for b in range(2):
                        src = wait_bank("c", h, i, b)
                        c = s + 2 * (b + 1) + i
                        ins = nc.vector.tensor_tensor_reduce(P[2 * (h % 3) + b][:, i, :n], src[:, :n], BIAS_C[:, h, 256 - n :],
                                                             1.0, NEG, ALU.add, ALU.max, SM[:, c : c + 1])
                        free(ins, "c", h, i, b)
                src = wait_bank("c_c", h)
                for i in range(2):
                    n = 7 + 8 * i
                    bias_ = BIAS_C[:, h, 128 * (1 - i) + 31 :: 16]
                    ins = nc.vector.tensor_tensor_reduce(PC[h % 3][:, i, :n], src[:, 16 * i : 16 * i + n], bias_, 1.0, NEG, ALU.add, ALU.max, SM[:, s + i : s + i + 1])
                    if i:
                        free(ins, "c_c", h)
                    else:
                        lane(ins)
                ts(SM[:, s + 6 : s + 12], SM[:, s : s + 6], NEG / 10, -1.0, ALU.max, ALU.mult, sem("c_max"))

            def c_norm(h):
                s = 64 + 20 * (h % 3)
                dve.wait_ge(sem("c_exps"), 6 * (h + 1))
                banks.await_read(dve, ("c_gate", 1))
                ts(SM[:, s + 12 : s + 18], SM[:, s + 12 : s + 18], 1e-30, None, ALU.max)
                lane(nc.vector.reciprocal(SM[:, s : s + 6], SM[:, s + 12 : s + 18]))
                f = SM[:, s : s + 6].rearrange("p (b i) -> p b i", b=3)
                g = CG[:, :, :].rearrange("p i (b h) -> p b i h", b=3)[:, :, :, h]
                tt(f, f, g, ALU.mult)
                for b in (1, 2, 0):
                    for i in range(2):
                        p = PC[h % 3][:, i, : 7 + 8 * i] if b == 0 else P[2 * (h % 3) + b - 1][:, i, : 128 * i + 128]
                        ts(p, p, SM[:, s + 2 * b + i : s + 2 * b + i + 1], None, ALU.mult, done=sem("c_probs") if i else None)

            steps = locals()
            for name, *args in SCHEDULE:
                follow.paused = name in ("blocks", "compress", "compress2")
                if name == "c_scores" and args == [0]:
                    follow(("step", "compress2"))
                if name in steps:
                    steps[name](*args)
                follow(("step", name, *args))

        @block.gpsimd
        def _(pool):
            lane = Lane(pool, sem("gpsimd_step"))

            def conv_taps(l):
                banks.await_read(pool, ("conv_a", l, 3))
                product = HKK[:, 0, :T]
                for i in range(CONV_K):
                    x, w, b = tap(l, 3, i)
                    if i == 0:
                        lane(nc.gpsimd.tensor_scalar(CO[:, 3, :], x, w, b, ALU.mult, ALU.add))
                    else:
                        lane(nc.gpsimd.tensor_scalar(product, x, w, None, ALU.mult))
                        lane(nc.gpsimd.tensor_tensor(CO[:, 3, :], product, CO[:, 3, :], ALU.add), sem("conv_out3") if i == CONV_K - 1 else None)

            def hgrn_args(l, i):
                pool.wait_ge(sem("summed"), l + 1)
                if i >= 3:
                    banks.await_(pool, ("scores", l, i - 3))
                d, lo = HD[i % 3], SB * i
                qq = d[:, :1024].rearrange("p (j h t) -> p j h t", j=8, h=4)
                shape = [128, 8, 4, SB]
                b = HB[:, :, lo : lo + SB]
                ref = b.rearrange("p h (j f) -> p j h f", f=SS)[:, :, :, 0:1]
                lane(nc.gpsimd.tensor_tensor(qq, bc(b[:, None, :, :], shape), bc(ref, shape), ALU.subtract), None if i else sem("decay_args"))
                if i:
                    kk = d[:, 1024 : 1024 + 4 * lo].rearrange("p (h s) -> p h s", h=4)
                    lane(nc.gpsimd.tensor_tensor(kk, bc(HB[:, :, lo : lo + 1], [128, 4, lo]), HB[:, :, :lo], ALU.subtract), sem("decay_args"))

            def ff1(l, half):
                for m in range(FH * half, FH * half + FH):
                    banks.await_read(pool, ("ff1", l, m))
                    lane(nc.gpsimd.tensor_tensor(F1[:, m % 4, :], F1[:, m % 4, :], F1[:, m % 4, :], ALU.mult), sem("squared"))

            def ab_in():
                banks.await_(pool, ("aq", 0))
                lane(nc.gpsimd.memset(BIN[:, :, 0:3], 0.0), sem("b_padding"))

            steps = locals()
            for name, *args in SCHEDULE:
                if name in steps:
                    steps[name](*args)

        @block.sync
        def _(sp):
            sp.dma_start(XT[:, :, :], x_in).then_inc(sem("x_loaded"), 16)
            sp.dma_start(CST[:, :], consts).then_inc(sem("loaded"), 16)
            sp.dma_start(PAR[:, :], params).then_inc(sem("loaded"), 16)

            def load(n, slot):
                sp.dma_start(ring[:, slot, :], stream[bass.ds(128 * n, 128), :]).then_inc(arrived[slot], 16)

            split_chunks = set(splits.chunks)
            rank, counts = [], [0, 0]
            for n in range(n_chunks):
                counts[n in split_chunks] += 1
                rank.append((n in split_chunks, counts[n in split_chunks]))

            def freed(n, i=None):
                split_, count = rank[n]
                sp.wait_ge(split_lo if split_ else w_used, count if i is None else count + RING * i)

            for s in range(RING):
                load(s, s)
            n = RING
            while n < n_chunks:
                rounds = 0
                while n % RING == 0 and n + RING * (rounds + 1) <= n_chunks and len({rank[m - RING][0] for m in range(n, n + RING * (rounds + 1))}) == 1:
                    rounds += 1
                if rounds > 1:
                    with sp.Fori(0, rounds) as i:
                        for s in range(RING):
                            freed(n - RING + s, i)
                            load(RING * i + n + s, s)
                    n += RING * rounds
                else:
                    freed(n - RING)
                    load(n, n % RING)
                    n += 1
            for k in range(KT):
                sp.wait_ge(sem("ln_done"), KT * 3 + k + 1)
                sp.dma_start(out[:, k, :], HT[:, k, :]).then_inc(sem("stored"), 16)
            sp.wait_ge(sem("stored"), 16 * KT)


def schedule():
    s = [("norm", 0), ("start",), ("store_bias",)]
    for l in range(DEPTH):
        s += [("norm", 2 * l)] if l else []
        s += [("conv_in", l), ("conv_taps", l), ("hgrn_in", l), ("mla_in", l), ("conv_norm", l)]
        s += [("gate", l, 0, 0), ("conv_var", l), ("mla_norm", l), ("hgrn_prep", l)]
        s += [("gate", l, 0, m) for m in range(1, KT)] + [("hgrn_clamp", l, 0), ("hgrn_clamp", l, 1), ("hgrn_args", l, 0)]
        s += [("branch_out", l, 0, c) for c in range(4)]
        for i in range(NB):
            s += [("hgrn_args", l, i + 1)] if i + 1 < NB else []
            s += [("hgrn_block", l, i)] + ([("gate", l, 1, i)] if i < KT else []) + [("hgrn_turn", l, i)]
            s += [("hgrn_clamp", l, i + 2)] if i + 2 < NB else []
        s += [("hgrn_values", l), ("mla_up", l), ("hgrn_norm", l), ("gate", l, 2, 0), ("hgrn_gates", l), ("hgrn_spread", l), ("head_norm", l, 0)]
        s += [("gate", l, 2, 1), ("head_spread", l, 0), ("head_norm", l, 1), ("gate", l, 2, 2), ("head_spread", l, 1)]
        s += [("gate", l, 2, m) for m in range(3, 6)] + [("att_scores", l, 0), ("att_scores", l, 1), ("gate", l, 2, 6), ("gate", l, 2, 7)]
        for h in range(HEADS):
            s += [("att_norm", l, h)]
            s += [("att_scores", l, h + 2)] if h + 2 < HEADS else []
            s += [("att_turn", l, h)]
            s += [("branch_out", l, 1, h // 2)] if h % 2 else []
            s += [("att_values", l, h // 2)] if h % 2 else []
        s += [("branch_out", l, 2, c) for c in range(4)] + [("mix_out", l), ("norm", 2 * l + 1)]
        s += [("hankel",)] if l == DEPTH - 1 else []
        s += [("ff1", l, 0)]
        s += [("bias",)] if l == DEPTH - 1 else []
        s += [("ff2", l, 0), ("ff1", l, 1), ("ff2", l, 1)]
    s += [("split_x", -1), ("ab_in",), ("a_scores", 0)]
    for h in range(HEADS):
        s += [("a_scores", h + 1)] if h + 1 < HEADS else []
        s += [("bqk_in", h), ("a_norm", h), ("a_turn", h)]
        s += [("a_values", h // 2)] if h % 2 else []
    s += [("if_in",), ("b_gates",)] + [("bo_in", j) for j in range(4)] + [("b_conv",), ("gate_rows",), ("bv_in",), ("b_scores", 0)]
    for h in range(H4):
        s += [("b_norm_weights", h)]
        s += [("b_scores", h + 1)] if h + 1 < H4 else []
        s += [("b_turn", h), ("b_values", h)]
        s += [("split_a",)] if h == H4 - 2 else []
    s += [("b_norm",)]
    for l in range(2):
        if l:
            s += [("split_x", 1), ("c_in",), ("blocks", 0), ("compress", 0), ("blocks", 1), ("compress", 1), ("compress2",), ("c_scores", 0), ("c_scores", 1)]
            for h in range(HEADS):
                s += [("c_norm", h), ("c_turn", h)]
                s += [("c_scores", h + 2)] if h + 2 < HEADS else []
                s += [("c_values", h)] + ([("c_split", h - 2)] if h >= 2 else [])
            s += [("c_split", HEADS - 2), ("c_split", HEADS - 1)]
        s += [("y_out", l), ("layer_norm", 2 * l), ("split_x", 2 * l), ("moe_lead", l), ("router", l), ("moe_start", l), ("moe_first", l), ("expert_gates", l), ("moe_hidden", l), ("moe", l)]
        s += [("layer_norm", 2 * l + 1)]
    return s


def kernel(**inputs):
    from concourse import bacc, mybir as _mybir
    from concourse.bass_utils import run_bass_kernel_spmd

    i = {k: np.asarray(v) for k, v in inputs.items()}
    tokens = np.concatenate([i["meta"], i["x"][0]], axis=0)
    arrays = {
        "weights": np.ascontiguousarray(weight_stream(i).reshape(-1, CHUNK)),
        "params": parameters(i),
        "consts": constants(),
        "x": np.ascontiguousarray(tokens.T.reshape(KT, 128, T).transpose(1, 0, 2)),
    }
    nc = bacc.Bacc("TRN2", target_bir_lowering=False, num_devices=1)
    aps = {k: nc.dram_tensor(f"in_{k}", a.shape, _mybir.dt.from_np(a.dtype), kind="ExternalInput").ap() for k, a in arrays.items()}
    out = nc.dram_tensor("out", (128, KT, SEQ), F32, kind="ExternalOutput").ap()
    scratch = nc.dram_tensor("bias_by_distance", (HEADS, 384), F32, kind="Internal").ap()
    build_program(nc, aps["weights"], aps["params"], aps["consts"], aps["x"], out, scratch)
    r = run_bass_kernel_spmd(nc, [{f"in_{k}": a for k, a in arrays.items()}], core_ids=[0])
    y = np.asarray(r.results[0]["out"])
    return np.ascontiguousarray(y.transpose(2, 1, 0).reshape(1, SEQ, D))
```
